# Optimizing a Trainium2 kernel written in Bass

```python
import jax, jax.numpy as jnp
from jax import lax
import numpy as np

D_MODEL = 1024
BATCH = 1
SEQ = 512
DEPTH = 1

EPS = 1e-6
D_FF = 4 * D_MODEL
M_HEADS = 4
M_DV = D_MODEL // 8
M_DQK = M_DV // 2
M_CONV = 5
M_CHUNK = 128
A_HEADS = 4
A_NOPE = D_MODEL // 8
A_ROPE = D_MODEL // 16
A_DV = D_MODEL // 8
A_DH = A_NOPE + A_ROPE
Q_LORA = D_MODEL // 4
KV_LORA = D_MODEL // 8
ROPE_THETA = 10000.0
Q_BLOCK = 128
M_QK_W = M_HEADS * M_DQK
M_V_W = M_HEADS * M_DV
N_GATES = 4 * M_HEADS
D_MIX = M_HEADS * M_DV + A_HEADS * A_DV
IN_WIDTHS = (M_QK_W, M_QK_W, M_V_W, M_V_W, N_GATES, Q_LORA, KV_LORA, A_ROPE)
D_IN = M_QK_W * 2 + M_V_W * 2 + N_GATES + Q_LORA + KV_LORA + A_ROPE


def rms_norm(x, g):
    xf = x.astype(jnp.float32)
    y = xf * lax.rsqrt(jnp.mean(xf * xf, axis=-1, keepdims=True) + EPS)
    return (y * g.astype(jnp.float32)).astype(x.dtype)

def rope(x, cos, sin):
    extra = x.ndim - 3
    c = cos.reshape(cos.shape[:2] + (1,) * extra + cos.shape[2:]).astype(jnp.float32)
    s = sin.reshape(sin.shape[:2] + (1,) * extra + sin.shape[2:]).astype(jnp.float32)
    xf = x.astype(jnp.float32)
    x1, x2 = xf[..., : A_ROPE // 2], xf[..., A_ROPE // 2:]
    return jnp.concatenate([x1 * c - x2 * s, x2 * c + x1 * s], axis=-1).astype(x.dtype)

def conv_centred(u, w, b):
    out = lax.conv_general_dilated(
        u, w[:, None, :].astype(u.dtype), window_strides=(1,),
        padding=[(M_CONV // 2, M_CONV // 2)],
        dimension_numbers=("NWC", "WIO", "NWC"), feature_group_count=u.shape[-1])
    return out + b.astype(u.dtype)

def mlstm_chunkwise(q, k, v, log_i, log_f):
    B, H, S, _ = q.shape
    L = M_CHUNK
    NC = S // L
    qc = q.reshape(B, H, NC, L, M_DQK)
    kc = k.reshape(B, H, NC, L, M_DQK)
    vc = v.reshape(B, H, NC, L, M_DV)
    li = log_i.reshape(B, H, NC, L)
    b = jnp.cumsum(log_f.reshape(B, H, NC, L), axis=-1)
    a = b[..., -1]
    w_log = a[..., None] - b + li
    g = jnp.max(w_log, axis=-1)
    w = jnp.exp(w_log - g[..., None])
    S_c = jnp.einsum('bhclv,bhcld->bhcvd', w[..., None] * vc, kc)
    n_c = jnp.einsum('bhcl,bhcld->bhcd', w, kc)

    def step(carry, inp):
        C, n, m = carry
        a_k, g_k, S_k, n_k = inp
        m_new = jnp.maximum(a_k + m, g_k)
        dec = jnp.exp(a_k + m - m_new)
        add = jnp.exp(g_k - m_new)
        C_new = dec[..., None, None] * C + add[..., None, None] * S_k
        n_new = dec[..., None] * n + add[..., None] * n_k
        return (C_new, n_new, m_new), (C, n, m)

    init = (jnp.zeros((B, H, M_DV, M_DQK), jnp.float32),
            jnp.zeros((B, H, M_DQK), jnp.float32),
            jnp.zeros((B, H), jnp.float32))
    xs = (jnp.moveaxis(a, 2, 0), jnp.moveaxis(g, 2, 0),
          jnp.moveaxis(S_c, 2, 0), jnp.moveaxis(n_c, 2, 0))
    _, (C_prev, n_prev, m_prev) = lax.scan(step, init, xs)
    C_prev = jnp.moveaxis(C_prev, 0, 2)
    n_prev = jnp.moveaxis(n_prev, 0, 2)
    m_prev = jnp.moveaxis(m_prev, 0, 2)

    D = b[..., :, None] - b[..., None, :] + li[..., None, :]
    causal_in_chunk = jnp.tril(jnp.ones((L, L), dtype=bool))
    D = jnp.where(causal_in_chunk, D, -jnp.inf)
    m_t = jnp.maximum(b + m_prev[..., None], jnp.max(D, axis=-1))
    P = jnp.exp(D - m_t[..., None]) * jnp.einsum('bhctd,bhcsd->bhcts', qc, kc)
    inter = jnp.exp(b + m_prev[..., None] - m_t)
    num = (jnp.einsum('bhcts,bhcsv->bhctv', P, vc)
           + inter[..., None] * jnp.einsum('bhctd,bhcvd->bhctv', qc, C_prev))
    den = jnp.sum(P, axis=-1) + inter * jnp.einsum('bhctd,bhcd->bhct', qc, n_prev)
    den = jnp.maximum(jnp.abs(den), jnp.exp(-m_t))
    return (num / den[..., None]).reshape(B, H, S, M_DV)

def mlstm_group(q, k, v, o, gates, b_gates, g_out):
    B, S, _ = q.shape
    f32 = jnp.float32

    def heads(t, d):
        return t.reshape(B, S, M_HEADS, d).transpose(0, 2, 1, 3).astype(f32)

    qh = heads(q, M_DQK) * (M_DQK ** -0.5)
    kh = heads(k, M_DQK)
    vh = heads(v, M_DV)
    gp = (gates.astype(f32) + b_gates.astype(f32)).reshape(B, S, 4, M_HEADS).transpose(2, 0, 3, 1)
    i_fw, f_fw, i_bw, f_bw = gp[0], gp[1], gp[2], gp[3]
    h_fw = mlstm_chunkwise(qh, kh, vh, i_fw, jax.nn.log_sigmoid(f_fw))

    def flip(t):
        return jnp.flip(t, axis=2)

    h_bw = flip(mlstm_chunkwise(flip(qh), flip(kh), flip(vh), flip(i_bw),
                                flip(jax.nn.log_sigmoid(f_bw))))
    h = (h_fw + h_bw).transpose(0, 2, 1, 3)
    h = rms_norm(h, g_out.reshape(M_HEADS, M_DV)).reshape(B, S, M_V_W)
    return (jax.nn.sigmoid(o.astype(f32)) * h).astype(q.dtype)

def mla_group(c_q, c_kv, k_pe, cos, sin, g_cq, g_ckv, w_uq, w_ukv, g_q, g_k):
    B, S, _ = c_q.shape
    q = (rms_norm(c_q, g_cq) @ w_uq).reshape(B, S, A_HEADS, A_DH)
    kv = (rms_norm(c_kv, g_ckv) @ w_ukv).reshape(B, S, A_HEADS, A_NOPE + A_DV)
    k_nope, v = kv[..., :A_NOPE], kv[..., A_NOPE:]
    k = jnp.concatenate(
        [k_nope, jnp.broadcast_to(k_pe[:, :, None, :], (B, S, A_HEADS, A_ROPE))], axis=-1)
    q = rms_norm(q, g_q)
    k = rms_norm(k, g_k)
    q = jnp.concatenate([q[..., :A_NOPE], rope(q[..., A_NOPE:], cos, sin)], axis=-1)
    k = jnp.concatenate([k[..., :A_NOPE], rope(k[..., A_NOPE:], cos, sin)], axis=-1)
    nb = S // Q_BLOCK
    qb = q.reshape(B, nb, Q_BLOCK, A_HEADS, A_DH).transpose(1, 0, 3, 2, 4)
    kh = k.transpose(0, 2, 1, 3)
    vh = v.transpose(0, 2, 1, 3)
    scale = A_DH ** -0.5

    def attend(q_blk):
        s = jnp.einsum('bhqd,bhkd->bhqk', q_blk, kh,
                       preferred_element_type=jnp.float32) * scale
        p = jax.nn.softmax(s, axis=-1)
        return jnp.einsum('bhqk,bhkv->bhqv', p.astype(vh.dtype), vh)

    out = lax.map(attend, qb)
    return out.transpose(1, 0, 3, 2, 4).reshape(B, S, A_HEADS * A_DV)

def first_inputs(seed: int = 0) -> dict:
    key = jax.random.key(seed)
    ks = jax.random.split(key, 24)
    f32 = jnp.float32

    def nrm(k, shape, scale):
        return jax.random.normal(k, shape, f32) * scale

    def gain(k, shape):
        return 1.0 + 0.02 * jax.random.normal(k, shape, f32)

    x = jax.random.normal(ks[0], (BATCH, SEQ, D_MODEL), f32)
    offset = jax.random.randint(ks[1], (BATCH, 1), 0, 1024, dtype=jnp.int32)
    positions = (jnp.arange(SEQ, dtype=jnp.int32)[None, :] + offset).astype(jnp.int32)
    gb = jax.random.normal(ks[2], (DEPTH, 4, M_HEADS), f32)
    forget_bias = 3.0 + jnp.linspace(0.0, 3.0, M_HEADS, dtype=f32)
    b_gates = jnp.stack([0.1 * gb[:, 0], forget_bias + 0.3 * gb[:, 1],
                         0.1 * gb[:, 2], forget_bias + 0.3 * gb[:, 3]], axis=1).reshape(DEPTH, N_GATES)
    return {
        "x": x,
        "positions": positions,
        "g_mix_norm": gain(ks[3], (DEPTH, D_MODEL)),
        "w_in": nrm(ks[4], (DEPTH, D_MODEL, D_IN), D_MODEL ** -0.5),
        "conv_w": nrm(ks[5], (DEPTH, M_CONV, 2 * M_QK_W), M_CONV ** -0.5),
        "conv_b": nrm(ks[6], (DEPTH, 2 * M_QK_W), 0.01),
        "b_gates": b_gates,
        "g_mlstm_out": gain(ks[7], (DEPTH, M_V_W)),
        "g_cq": gain(ks[8], (DEPTH, Q_LORA)),
        "g_ckv": gain(ks[9], (DEPTH, KV_LORA)),
        "w_uq": nrm(ks[10], (DEPTH, Q_LORA, A_HEADS * A_DH), Q_LORA ** -0.5),
        "w_ukv": nrm(ks[11], (DEPTH, KV_LORA, A_HEADS * (A_NOPE + A_DV)), KV_LORA ** -0.5),
        "g_q": gain(ks[12], (DEPTH, A_DH)),
        "g_k": gain(ks[13], (DEPTH, A_DH)),
        "w_out": nrm(ks[14], (DEPTH, D_MIX, D_MODEL), D_MIX ** -0.5),
        "g_ffn_norm": gain(ks[15], (DEPTH, D_MODEL)),
        "w_ff1": nrm(ks[16], (DEPTH, D_MODEL, D_FF), D_MODEL ** -0.5),
        "w_ff2": nrm(ks[17], (DEPTH, D_FF, D_MODEL), D_FF ** -0.5),
    }

def first_block(x, positions, g_mix_norm, w_in, conv_w, conv_b, b_gates, g_mlstm_out,
              g_cq, g_ckv, w_uq, w_ukv, g_q, g_k, w_out, g_ffn_norm, w_ff1, w_ff2):
    inv_freq = ROPE_THETA ** (-jnp.arange(0, A_ROPE, 2, dtype=jnp.float32) / A_ROPE)
    ang = positions.astype(jnp.float32)[..., None] * inv_freq
    cos, sin = jnp.cos(ang), jnp.sin(ang)
    splits = [int(s) for s in np.cumsum(IN_WIDTHS)[:-1]]
    for l in range(DEPTH):
        h = rms_norm(x, g_mix_norm[l])
        z = h @ w_in[l]
        q_m, k_m, v_m, o_m, gates, c_q, c_kv, k_pe = jnp.split(z, splits, axis=-1)
        qk = jax.nn.silu(conv_centred(jnp.concatenate([q_m, k_m], axis=-1), conv_w[l], conv_b[l]))
        q_m, k_m = qk[..., :M_QK_W], qk[..., M_QK_W:]
        y_a = mlstm_group(q_m, k_m, v_m, o_m, gates, b_gates[l], g_mlstm_out[l])
        y_b = mla_group(c_q, c_kv, k_pe, cos, sin, g_cq[l], g_ckv[l], w_uq[l], w_ukv[l],
                        g_q[l], g_k[l])
        x = x + jnp.concatenate([y_a, y_b], axis=-1) @ w_out[l]
        h = rms_norm(x, g_ffn_norm[l])
        x = x + jnp.square(jax.nn.relu(h @ w_ff1[l])) @ w_ff2[l]
    return x


MIX_WIDTH = D_MODEL
RET_HEADS = 4
RET_DK = MIX_WIDTH // (2 * RET_HEADS)
RET_DV = MIX_WIDTH // (2 * RET_HEADS)
RET_WIDTH = RET_HEADS * RET_DV
RET_CHUNK = 128
DIFF_HEADS = 4
DIFF_DQK = MIX_WIDTH // (4 * DIFF_HEADS)
DIFF_DV = 2 * DIFF_DQK
DIFF_WIDTH = DIFF_HEADS * DIFF_DV
IN_SPLITS = [RET_HEADS * RET_DK, RET_HEADS * RET_DK, RET_WIDTH, RET_WIDTH,
             DIFF_HEADS * 2 * DIFF_DQK, DIFF_HEADS * 2 * DIFF_DQK, DIFF_WIDTH]
IN_COLS = sum(IN_SPLITS)
IN_OFFSETS = [int(o) for o in np.cumsum(IN_SPLITS)[:-1]]

PEER_HEADS = 8
PEER_TOPK = 16
N_KEYS = 128
N_EXPERTS = N_KEYS * N_KEYS
PEER_DQ = 256
PEER_TOKEN_BLOCK = 128

RMS_EPS = 1e-6
NEG_INF = -1e30


def rmsnorm(x, g=None):
    xf = x.astype(jnp.float32)
    y = xf * lax.rsqrt(jnp.mean(xf * xf, axis=-1, keepdims=True) + RMS_EPS)
    if g is not None:
        y = y * g.astype(jnp.float32)
    return y.astype(x.dtype)

def lambda_init(layer_idx):
    return 0.8 - 0.6 * float(np.exp(-0.3 * layer_idx))

def retention(q, k, v):
    B, T, H, dk = q.shape
    dv = v.shape[-1]
    C = RET_CHUNK
    N = T // C
    log_gamma = jnp.log1p(-jnp.exp2(-5.0 - jnp.arange(H, dtype=jnp.float32)))

    def chunks(a):
        return a.astype(jnp.float32).reshape(B, N, C, H, a.shape[-1]).transpose(1, 0, 3, 2, 4)

    qc, kc, vc = chunks(q), chunks(k) * (dk ** -0.5), chunks(v)
    idx = jnp.arange(C, dtype=jnp.float32)
    rel = idx[:, None] - idx[None, :]
    intra = jnp.where(rel >= 0, jnp.exp(log_gamma[:, None, None] * jnp.maximum(rel, 0.0)), 0.0)
    cross = jnp.exp(log_gamma[:, None] * (idx + 1.0))
    kdec = jnp.exp(log_gamma[:, None] * (C - 1.0 - idx))
    cdec = jnp.exp(log_gamma * C)

    def step(S, inp):
        qi, ki, vi = inp
        o = jnp.einsum('bhij,bhjv->bhiv', jnp.einsum('bhid,bhjd->bhij', qi, ki) * intra[None], vi)
        o = o + jnp.einsum('bhid,bhdv->bhiv', qi, S) * cross[None, :, :, None]
        S = S * cdec[None, :, None, None] + jnp.einsum('bhjd,bhjv->bhdv', ki * kdec[None, :, :, None], vi)
        return S, o

    S0 = jnp.zeros((B, H, dk, dv), jnp.float32)
    _, o = lax.scan(step, S0, (qc, kc, vc))
    return o.transpose(1, 0, 3, 2, 4).reshape(B, T, H, dv)

def alibi_slopes(n_heads):
    return jnp.exp2(-8.0 * (jnp.arange(n_heads, dtype=jnp.float32) + 1.0) / n_heads)

def diff_attention(q, k, v, lam):
    B, T, H, _, d = q.shape
    dv = v.shape[-1]
    C = Q_BLOCK
    N = T // C
    qb = (q.astype(jnp.float32) * (d ** -0.5)).reshape(B, N, C, H, 2, d).transpose(1, 0, 3, 4, 2, 5)
    kt = k.astype(jnp.float32).transpose(0, 2, 3, 1, 4)
    vt = v.astype(jnp.float32).transpose(0, 2, 1, 3)
    slopes = alibi_slopes(H)
    kpos = jnp.arange(T)

    def block(args):
        qi, start = args
        qpos = start + jnp.arange(C)
        dist = (qpos[:, None] - kpos[None, :]).astype(jnp.float32)
        bias = jnp.where(dist >= 0, -slopes[:, None, None] * dist, NEG_INF)
        s = jnp.einsum('bhpid,bhpjd->bhpij', qi, kt) + bias[None, :, None]
        p = jax.nn.softmax(s, axis=-1)
        a = p[:, :, 0] - lam * p[:, :, 1]
        return jnp.einsum('bhij,bhjv->bhiv', a, vt)

    o = lax.map(block, (qb, jnp.arange(N) * C))
    return o.transpose(1, 0, 3, 2, 4).reshape(B, T, H, dv)

def peer(xn, wq, subkeys, u, v):
    B, T, D = xn.shape
    xt = xn.reshape(-1, PEER_TOKEN_BLOCK, D)
    K = PEER_TOPK

    def block(xb):
        t = xb.shape[0]
        q = (xb @ wq).reshape(t, PEER_HEADS, 2, PEER_DQ // 2)
        s = jnp.einsum('thpd,hpkd->thpk', q, subkeys).astype(jnp.float32)
        s_top, i_top = lax.top_k(s, K)
        cand = (s_top[:, :, 0, :, None] + s_top[:, :, 1, None, :]).reshape(t, PEER_HEADS, K * K)
        c_top, c_idx = lax.top_k(cand, K)
        i1 = jnp.take_along_axis(i_top[:, :, 0], c_idx // K, axis=-1)
        i2 = jnp.take_along_axis(i_top[:, :, 1], c_idx % K, axis=-1)
        e = i1 * N_KEYS + i2
        g = jax.nn.softmax(c_top, axis=-1)
        ue = jnp.take(u, e, axis=0)
        ve = jnp.take(v, e, axis=0)
        act = jax.nn.gelu(jnp.einsum('thkd,td->thk', ue, xb).astype(jnp.float32), approximate=False)
        return jnp.einsum('thk,thkd->td', (g * act).astype(xb.dtype), ve)

    return lax.map(block, xt).reshape(B, T, D)

def second_inputs(seed: int = 0) -> dict:
    key = jax.random.key(seed)
    ks = jax.random.split(key, 13)
    f = jnp.float32
    x = jax.random.normal(ks[0], (BATCH, SEQ, D_MODEL), f)
    norm_mix_g = 1.0 + 0.02 * jax.random.normal(ks[1], (DEPTH, D_MODEL), f)
    w_in = jax.random.normal(ks[2], (DEPTH, D_MODEL, IN_COLS), f) * D_MODEL ** -0.5
    diff_lambda = 0.1 * jax.random.normal(ks[3], (DEPTH, 4, DIFF_DQK), f)
    diff_subln_g = 1.0 + 0.02 * jax.random.normal(ks[4], (DEPTH, DIFF_DV), f)
    w_out = jax.random.normal(ks[5], (DEPTH, MIX_WIDTH, D_MODEL), f) * MIX_WIDTH ** -0.5
    norm_ffn_g = 1.0 + 0.02 * jax.random.normal(ks[6], (DEPTH, D_MODEL), f)
    peer_wq = jax.random.normal(ks[7], (DEPTH, D_MODEL, PEER_HEADS * PEER_DQ), f) * D_MODEL ** -0.5
    peer_subkeys = jax.random.normal(ks[8], (DEPTH, PEER_HEADS, 2, N_KEYS, PEER_DQ // 2), f) * (PEER_DQ // 2) ** -0.5
    peer_u = jax.random.normal(ks[9], (DEPTH, N_EXPERTS, D_MODEL), f) * D_MODEL ** -0.5
    peer_v = jax.random.normal(ks[10], (DEPTH, N_EXPERTS, D_MODEL), f) * PEER_TOPK ** -0.5
    final_norm_g = 1.0 + 0.02 * jax.random.normal(ks[11], (D_MODEL,), f)
    return {"x": x, "norm_mix_g": norm_mix_g, "w_in": w_in, "diff_lambda": diff_lambda,
            "diff_subln_g": diff_subln_g, "w_out": w_out, "norm_ffn_g": norm_ffn_g,
            "peer_wq": peer_wq, "peer_subkeys": peer_subkeys, "peer_u": peer_u,
            "peer_v": peer_v, "final_norm_g": final_norm_g}

def second_block(x, norm_mix_g, w_in, diff_lambda, diff_subln_g, w_out, norm_ffn_g,
              peer_wq, peer_subkeys, peer_u, peer_v, final_norm_g):
    B, T, D = x.shape
    for l in range(DEPTH):
        h = rmsnorm(x, norm_mix_g[l])
        proj = h @ w_in[l]
        rq, rk, rv, rg, dq, dk, dv = jnp.split(proj, IN_OFFSETS, axis=-1)
        ry = retention(rq.reshape(B, T, RET_HEADS, RET_DK), rk.reshape(B, T, RET_HEADS, RET_DK),
                       rv.reshape(B, T, RET_HEADS, RET_DV))
        ry = rmsnorm(ry).reshape(B, T, RET_WIDTH)
        ret_out = (jax.nn.silu(rg.astype(jnp.float32)) * ry).astype(x.dtype)
        li = lambda_init(l)
        lp = diff_lambda[l].astype(jnp.float32)
        lam = jnp.exp(jnp.sum(lp[0] * lp[1])) - jnp.exp(jnp.sum(lp[2] * lp[3])) + li
        dy = diff_attention(dq.reshape(B, T, DIFF_HEADS, 2, DIFF_DQK), dk.reshape(B, T, DIFF_HEADS, 2, DIFF_DQK),
                            dv.reshape(B, T, DIFF_HEADS, DIFF_DV), lam)
        diff_out = (rmsnorm(dy, diff_subln_g[l]) * (1.0 - li)).reshape(B, T, DIFF_WIDTH).astype(x.dtype)
        x = x + jnp.concatenate([ret_out, diff_out], axis=-1) @ w_out[l]
        x = x + peer(rmsnorm(x, norm_ffn_g[l]), peer_wq[l], peer_subkeys[l], peer_u[l], peer_v[l])
    return rmsnorm(x, final_norm_g)


def setup_inputs(seed=0):
    out = dict(first_inputs(seed))
    for name, value in second_inputs(seed + 1).items():
        if name != "x":
            out[name + "_2"] = value
    return out


def reference(
    x, positions, g_mix_norm, w_in, conv_w, conv_b, b_gates, g_mlstm_out, g_cq, g_ckv, w_uq,
    w_ukv, g_q, g_k, w_out, g_ffn_norm, w_ff1, w_ff2, norm_mix_g_2, w_in_2, diff_lambda_2,
    diff_subln_g_2, w_out_2, norm_ffn_g_2, peer_wq_2, peer_subkeys_2, peer_u_2, peer_v_2,
    final_norm_g_2,
):
    x = first_block(
        x, positions, g_mix_norm, w_in, conv_w, conv_b, b_gates, g_mlstm_out, g_cq, g_ckv, w_uq,
        w_ukv, g_q, g_k, w_out, g_ffn_norm, w_ff1, w_ff2,
    )
    return second_block(
        x, norm_mix_g_2, w_in_2, diff_lambda_2, diff_subln_g_2, w_out_2, norm_ffn_g_2,
        peer_wq_2, peer_subkeys_2, peer_u_2, peer_v_2, final_norm_g_2,
    )


_drawn_inputs = setup_inputs


def setup_inputs(seed=0):
    import zlib

    import numpy as np

    out = dict(_drawn_inputs(seed))
    spreads = {}
    factors = {'g_mix_norm': 3.108,
     'conv_b': 23.535,
     'g_mlstm_out': 4.918,
     'g_cq': 8.0,
     'g_ckv': 8.0,
     'g_q': 8.0,
     'g_k': 8.0,
     'norm_mix_g_2': 3.096,
     'diff_subln_g_2': 34.26,
     'norm_ffn_g_2': 22.719,
     'final_norm_g_2': 7.124,
     'g_ffn_norm': 3.625}
    for name, (base, spread) in spreads.items():
        noise = np.random.default_rng([zlib.crc32(name.encode()), seed]).standard_normal(out[name].shape)
        drawn = base * np.exp(spread * noise) if base else spread * noise
        out[name] = __import__('jax').numpy.asarray(drawn.astype(out[name].dtype))
    for name, factor in factors.items():
        out[name] = (out[name] * factor).astype(out[name].dtype)
    return out
```

```python
from contextlib import ExitStack

import numpy as np

import concourse.bass as bass
from concourse import mybir

F32 = mybir.dt.float32
BF16 = mybir.dt.bfloat16
U32 = mybir.dt.uint32
I32 = mybir.dt.int32
ALU = mybir.AluOpType
ACT = mybir.ActivationFunctionType
AX = mybir.AxisListType

P = 128
T = 512
NT = T // P
D = 1024
KD = D // P
EPS = 1e-6

H = 4
DQK = 64
DV = 128
NC = T // P
TAPS = 5
A_NOPE, A_ROPE = 128, 64
A_DH = A_NOPE + A_ROPE
Q_LORA, KV_LORA = 256, 128
N_GATES = 16
D_FF = 4096
TAIL = N_GATES + Q_LORA + KV_LORA + A_ROPE
C_CQ, C_CKV, C_KPE = N_GATES, N_GATES + Q_LORA, N_GATES + Q_LORA + KV_LORA
ROWS = 36

RET_DK = 128
DIFF_D = 64
P_HEADS = 8
TOPK = 16
N_KEYS = 128
LAMBDA_INIT = 0.2

CW = 512
FF_GROUPS = D_FF // CW
EX_GROUPS = N_KEYS // 4
RING = 4

CONSTS = {}


def constant_table():
    i = np.arange(P, dtype=np.float64)
    parts = {}
    parts["ident"] = np.eye(P)
    parts["mask_fw"] = np.where(i[:, None] <= i[None, :], 0.0, -1e30)
    parts["mask_bw"] = np.where(i[:, None] >= i[None, :], 0.0, -1e30)
    inv_freq = (np.float32(10000.0) ** (-np.arange(0, A_ROPE, 2, dtype=np.float32) / np.float32(A_ROPE))).astype(np.float32)
    parts["inv_freq"] = np.broadcast_to(inv_freq, (P, A_ROPE // 2))
    gamma_log = np.log1p(-np.exp2(-5.0 - np.arange(H)))
    rel = i[None, :] - i[:, None]
    intra = np.where(rel[None] >= 0, np.exp(gamma_log[:, None, None] * np.maximum(rel[None], 0.0)), 0.0)
    parts["intra"] = (intra * RET_DK ** -0.5).transpose(1, 0, 2)
    parts["cross"] = np.broadcast_to(np.exp(gamma_log[:, None] * (i + 1.0)), (P, H, P))
    parts["kdec"] = (np.exp(gamma_log[:, None] * (P - 1.0 - i)) * RET_DK ** -0.5).T
    m = np.arange(T) - (T - P)
    dist = i[:, None] - m[None, :]
    parts["negdist"] = np.where(dist >= 0, -dist, -1e33)
    parts["iota"] = np.broadcast_to(i, (P, P))
    at, cols = 0, []
    for name, a in parts.items():
        a = np.ascontiguousarray(a, np.float32).reshape(P, -1)
        CONSTS[name] = (at, a.shape[1])
        at += a.shape[1]
        cols.append(a)
    return np.concatenate(cols, axis=1)


TABLE = constant_table()
GAMMA = [float(1.0 - 2.0 ** (-5.0 - h)) for h in range(H)]
CDEC = [g ** P for g in GAMMA]
SLOPES = [float(2.0 ** (-8.0 * (h + 1) / H)) for h in range(H)]

TWO_PI_A = 6.28125
TWO_PI_B = float(np.float32(2 * np.pi - TWO_PI_A))
TWO_PI_C = float(2 * np.pi - TWO_PI_A - np.float64(np.float32(2 * np.pi - TWO_PI_A)))
ROUND = 12582912.0


class Steps:

    def __init__(self, eng, sem):
        self.eng, self.sem, self.n = eng, sem, 0

    def did(self, instruction):
        instruction.then_inc(self.sem, 1)
        self.n += 1

    def wait(self):
        self.eng.wait_ge(self.sem, self.n)


def build(nc, ins, out):
    ctx = ExitStack()
    with ctx:
        def sbuf(name, shape, dt=F32):
            return ctx.enter_context(nc.sbuf_tensor(name, shape, dt))

        def sem(name):
            return ctx.enter_context(nc.semaphore(name))

        x_sb = sbuf("x_sb", [P, NT, D])
        consts = sbuf("consts", [P, TABLE.shape[1]])
        ring = sbuf("ring", [P, RING, 4096])
        split = sbuf("split", [P, 2, 2, 4096], BF16)
        arena = sbuf("arena", [P, 20480])
        gains = sbuf("gains", [P, 64])
        small = sbuf("small", [P, 640])
        bcast = sbuf("bcast", [P, 656])
        ps = ctx.enter_context(nc.psum_tensor("ps", [P, 8, 512], F32))

        def const(name, **dims):
            at, n = CONSTS[name]
            a = consts[:, at:at + n]
            return a.rearrange("p (%s) -> p %s" % (" ".join(dims), " ".join(dims)), **dims) if dims else a

        ident = const("ident")
        iota = const("iota")
        mask = [const("mask_fw"), const("mask_bw")]

        def bank(i):
            return ps[:, i, :]

        def part(base, at, *shape, dt=F32):
            n = 1
            for s in shape:
                n *= s
            words = n if dt is not BF16 else n // 2
            a = base[:, at:at + words]
            if dt is not F32:
                a = a.bitcast(dt)
            if len(shape) > 1:
                names = "abcd"[:len(shape)]
                a = a.rearrange("p (%s) -> p %s" % (" ".join(names), " ".join(names)),
                                **dict(zip(names, shape)))
            return a

        split_words = split[:, :, :, :].rearrange("p s h n -> p (s h n)").bitcast(F32)

        G_MIX, G_Y1, G_FFN, G_MIX2, G_Y2, G_FFN2, G_CQ, G_CKV, G_QN, G_KN = 0, 8, 16, 24, 32, 40, 48, 50, 51, 52
        gate_bias = bcast[:, 0:16]
        rope_gain = bcast[:, 16:144].rearrange("p (a b) -> p a b", a=2)
        lam_in = bcast[:, 144:400].rearrange("p (a b) -> p a b", a=4)
        cos_t = bcast[:, 400:528].rearrange("p (a b) -> p a b", a=NT)
        sin_t = bcast[:, 528:656].rearrange("p (a b) -> p a b", a=NT)

        sumsq = small[:, 0:32]
        mean_eps = small[:, 32:64]
        rstd = small[:, 64:96]
        minus_half = small[:, 96:128]
        prev_max = small[:, 128:132]
        dec_rows = small[:, 132:136]
        dec_cols = small[:, 136:168].rearrange("p (a b) -> p a b", a=8)
        den = small[:, 168:176].rearrange("p (a b) -> p a b", a=2)
        den_t = small[:, 176:184].rearrange("p (a b) -> p a b", a=2)
        den_r = small[:, 184:192].rearrange("p (a b) -> p a b", a=2)
        row_max = small[:, 192:224]
        row_nmax = small[:, 224:256]
        row_sum = small[:, 256:288]
        row_inv = small[:, 288:320]
        lam = small[:, 320:328]
        pos = small[:, 328:332]
        one_col = small[:, 332:333]
        pos_rows = small[:, 336:464]

        hT = part(arena, 0, KD, T)
        y1 = part(arena, 0, NT, D)
        conv_in = part(arena, 4096, 4, T + 4)
        qkT = part(arena, 6160, 4, T)
        v1 = part(arena, 8208, NT, H * DV)
        o1 = part(arena, 10256, NT, H * DV)
        k_tok = part(arena, 12304, NT, H * DQK)
        tail = part(arena, 13328, NT, TAIL)
        xn1 = part(arena, 15184, NT, D)
        decay = part(arena, 15184, 2, 2, NC * P)
        probs = part(arena, 17232, 2, 2, NC, P)
        num = part(arena, 19280, 2, NC, DV)
        rows = [part(split_words, 512 * i, T) for i in range(10)]
        lf_row, b_row, c_row, m_row, negm_row, inter_row, em_row, w_row, t_row, u_row = rows
        gate_pad = part(split_words, 5120, NT, 2, 64)
        gate_cols = part(split_words, 5632, 4, NC, ROWS)
        conv_rows = part(split_words, 6208, T)
        state = part(split_words, 6720, 2, 3, 132)
        k_dec = part(split_words, 7512, 2, 3, DQK)
        conv_w = part(split_words, 7896, 4, 8)
        ones = part(split_words, 7936, P)

        qk_sumsq = small[:, 512:544].rearrange("p (t h) -> p t h", t=NT)
        qk_rstd = small[:, 544:576].rearrange("p (t h) -> p t h", t=NT)
        qk_mean = small[:, 576:608].rearrange("p (t h) -> p t h", t=NT)

        cqT = part(split_words, 0, 2, T)
        ckvT = part(split_words, 1024, T)
        qk_tok = part(split_words, 1536, 2, 2 * H, A_DH)
        qk_sq = part(split_words, 4608, 2 * H, A_DH)
        angle = part(split_words, 6144, NT, A_ROPE // 2)
        turns = part(split_words, 6272, NT, A_ROPE // 2)
        angle_c = part(split_words, 6400, NT, A_ROPE // 2)
        pos_f = part(split_words, 6528, P)
        nopeT = part(arena, 4096, 2 * H, T)
        ropeT = part(arena, 8192, 2 * H, T)
        v2 = part(arena, 15184, NT, H, DV)
        att = part(arena, 17232, 2, T)
        attT = part(arena, 18256, 2, T)
        rot = part(arena, 19280, 2 * H, A_ROPE)
        rot_t = part(arena, 19792, 2 * H, A_ROPE // 2)

        xT_hi = part(arena, 4096, KD, T, dt=BF16)
        xT_lo = part(arena, 6144, KD, T, dt=BF16)
        xn = part(arena, 0, NT, D)

        relu = part(arena, 8192, 2, T)
        hid = part(arena, 9216, 2, T)
        hid_hi = part(arena, 10240, 2, 4, T, dt=BF16)
        hid_lo = part(arena, 12288, 2, 4, T, dt=BF16)

        rqT = part(arena, 8192, H, T)
        rkT = part(arena, 10240, H, T)
        rv = part(arena, 12288, NT, H * DV)
        rg = part(arena, 14336, NT, H * DV)
        dqT = part(arena, 16384, H, T)
        dkT = part(arena, 0, H, T)
        dv2 = part(arena, 2048, NT, H, DV)
        y2 = part(arena, 4096, NT, D)
        ret_in = part(split_words, 0, 2, NC, P)
        ret_k = part(split_words, 1024, 2, NC, P)
        ret_q = part(split_words, 2048, 2, NC, P)
        ret_s = part(split_words, 3072, 3, P)
        spare_row = part(split_words, 3456, P)
        dif = part(arena, 18432, 2, 2, T)
        difT = part(arena, 8192, 2, T)
        dif_sq = part(arena, 9216, P)
        lam_t = part(arena, 9344, 2, DIFF_D)
        y2T_hi = part(arena, 10240, KD, T, dt=BF16)
        y2T_lo = part(arena, 12288, KD, T, dt=BF16)

        top_v = part(arena, 0, NT, 2 * P_HEADS, TOPK)
        top_i = arena[:, 1024:2048].bitcast(U32).rearrange("p (t g k) -> p t g k", t=NT, g=2 * P_HEADS)
        top_f = part(arena, 2048, NT, 2 * P_HEADS, TOPK)
        pick_v = part(arena, 3072, NT, P_HEADS, TOPK)
        pick_i = arena[:, 3584:4096].bitcast(U32).rearrange("p (t g k) -> p t g k", t=NT, g=P_HEADS)
        half_q = part(arena, 8192, 2, T)
        masked = part(arena, 9216, NT, 256)
        keys = part(arena, 14336, 2 * P_HEADS, P)
        keysT = part(arena, 16384, 2 * P_HEADS, P)
        cand = part(arena, 8192 + 2048, 2, P_HEADS, TOPK, TOPK)
        match0 = part(arena, 14336, P_HEADS, TOPK, TOPK)
        match1 = part(arena, 16384, P_HEADS, TOPK, TOPK)
        pick_g = part(arena, 18432, NT, P)
        pick_1 = part(arena, 18944, NT, P)
        pick_2 = part(arena, 19456, NT, P)
        half_i = arena[:, 19968:20480].bitcast(U32).rearrange("p (t g k) -> p t g k", t=NT, g=P_HEADS)
        half_f = part(split_words, 0, 2, NT, P_HEADS, TOPK)
        gate_sum = small[:, 0:32]
        gate_inv = small[:, 32:64]
        pickT = part(arena, 0, 3, T)
        hot = part(arena, 1536, 2, 4, 2, P)
        TB = 64
        gate_block = [part(arena, 8192, P, TB), part(split_words, 0, P, TB)]
        gates = part(arena, 16384, 2, 4, T)
        uT_hi = part(arena, 8192, 2, KD, P, dt=BF16)
        uT_lo = part(arena, 9216, 2, KD, P, dt=BF16)
        gelu = part(arena, 10240, 2, T)
        act_g = part(arena, 11264, 2, T)
        ex_hi = part(arena, 12288, 2, 4, T, dt=BF16)
        ex_lo = part(arena, 14336, 2, 4, T, dt=BF16)
        out_gain = part(arena, 0, D)
        out_rows = part(arena, 4096, NT, D)

        gate_dram = nc.dram_tensor("gate_matrix", (P, N_KEYS, T), F32, kind="Internal").ap()

        x_in, const_in, small_in = sem("x_in"), sem("const_in"), sem("small_in")
        ring_in = [sem(f"ring_in{i}") for i in range(RING)]
        filled = sem("filled")
        own_v, own_a, own_p, own_t = sem("own_v"), sem("own_a"), sem("own_p"), sem("own_t")
        ssq_done, rstd_done = sem("ssq_done"), sem("rstd_done")
        xn_done, turned, turned_hi, turned_lo = sem("xn_done"), sem("turned"), sem("turned_hi"), sem("turned_lo")
        mm_done, mm_out = sem("mm_done"), sem("mm_out")
        w_hi, w_lo, w_used = sem("w_hi"), sem("w_lo"), sem("w_used")
        conv_turned, conv_ready, conv_done, qk_done = sem("conv_turned"), sem("conv_ready"), sem("conv_done"), sem("qk_done")
        ktok_turned, ktok_done = sem("ktok_turned"), sem("ktok_done")
        gates_padded, gates_turned, f_neg, f_log = sem("gates_padded"), sem("gates_turned"), sem("f_neg"), sem("f_log")
        rows_ready, rows_exp, cols_turned, cols_done = sem("rows_ready"), sem("rows_exp"), sem("cols_turned"), sem("cols_done")
        scores_done, decay_in, decay_exp, probs_done = sem("scores_done"), sem("decay_in"), sem("decay_exp"), sem("probs_done")
        kdec_done, kv_done, state_done = sem("kdec_done"), sem("kv_done"), sem("state_done")
        num_done, num_out, inter_done, head_out = sem("num_done"), sem("num_out"), sem("inter_done"), sem("head_out")
        y_ready, o_sig = sem("y_ready"), sem("o_sig")

        latent_done, qk_put, pe_put, v_put, qk_squared = sem("latent_done"), sem("qk_put"), sem("pe_put"), sem("v_put"), sem("qk_squared")
        qk_summed, qk_rstd_done, qk_rotated, qk_turned = sem("qk_summed"), sem("qk_rstd_done"), sem("qk_rotated"), sem("qk_turned")
        nope_out, rope_out, pos_turned, angles, rotary = sem("nope_out"), sem("rope_out"), sem("pos_turned"), sem("angles"), sem("rotary")
        proj_done = sem("proj_done")
        att_scores, att_max, att_exp, att_turned, att_out, att_pv, att_norm = (
            sem(f"att_{n}") for n in ("scores", "max", "exp", "turned", "out", "pv", "norm"))
        ff_a, ff_relu, ff_hi, ff_lo, ff_b, ff_add = (sem(f"ff_{n}") for n in ("a", "relu", "hi", "lo", "b", "add"))

        ret_scores, ret_kturned, ret_a, ret_kd, ret_qx, ret_kv, ret_state, ret_o, ret_y = (
            sem(f"ret_{n}") for n in ("scores", "kturned", "a", "kd", "qx", "kv", "state", "o", "y"))
        rg_silu, lam_sums, lam_exp = sem("rg_silu"), sem("lam_sums"), sem("lam_exp")
        dif_scores, dif_max, dif_exp, dif_probs, dif_turned, dif_out, dif_pv, dif_y = (
            sem(f"dif_{n}") for n in ("scores", "max", "exp", "probs", "turned", "out", "pv", "y"))
        keys_in, keys_turned, keys_out = sem("keys_in"), sem("keys_turned"), sem("keys_out")
        key_scores, key_tops, cands, picks_top, places = (
            sem("key_scores"), sem("key_tops"), sem("cands"), sem("picks_top"), sem("places"))
        gate_in, gate_exp, match_eq, match_p, match_used, picks_ready, picks_turned, picks_out = (
            sem("gate_in"), sem("gate_exp"), sem("match_eq"), sem("match_p"), sem("match_used"), sem("picks_ready"), sem("picks_turned"), sem("picks_out"))
        hot_ready, gate_mm, gate_out = sem("hot_ready"), sem("gate_mm"), sem("gate_out")
        gate_stored = [sem("gate_stored0"), sem("gate_stored1")]
        gates_in = [sem("gates_in0"), sem("gates_in1")]
        u_turned, u_hi, u_lo, ex_a, ex_gelu, ex_mul, ex_hi_done, ex_lo_done, ex_b, ex_add = (
            sem(n) for n in ("u_turned", "u_hi", "u_lo", "ex_a", "ex_gelu", "ex_mul", "ex_hi_done", "ex_lo_done", "ex_b", "ex_add"))
        out_gain_in, out_ready, out_stored = sem("out_gain_in"), sem("out_ready"), sem("out_stored")
        y2_ready = sem("y2_ready")
        ff_sq = sem("ff_sq")

        S_OUT, S_FF, S_IN2, S_OUT2, S_WQ, S_EX = 0, 2, 18, 25, 27, 31
        TURN = {"mix": 0, "latent": 8, "out": 11, "ffn": 19, "mix2": 27, "out2": 35, "peer": 43}
        TURN_LO = {"out": 0, "ffn": 8, "mix2": 16, "out2": 24, "peer": 32}
        MM = {"z": 0, "out": 16, "in2": 24, "out2": 52, "wq": 60}

        def arrived(j4, rounds):
            return 16 * rounds + 16 + (16 if j4 == 0 else 0)

        def ring_chunk(j, cols=CW):
            return ring[:, j % RING, 0:KD * cols].rearrange("p (k n) -> p k n", k=KD)

        def chunk_here(eng, j):
            eng.wait_ge(ring_in[j % RING], 16 if j < RING else arrived(j % RING, j // RING))

        def high(s2, k):
            return split[:, s2, 0, :].rearrange("p (k n) -> p k n", k=k)

        def low(s2, k):
            return split[:, s2, 1, :].rearrange("p (k n) -> p k n", k=k)

        SMALLS = 20
        block = ctx.enter_context(nc.Block())

        @block.sync
        def _(sp):
            sp.dma_start(x_sb[:, :, :], ins["x"][0].rearrange("(t p) d -> p t d", p=P)).then_inc(x_in, 16)

            w_in = ins["w_in"][0].rearrange("(p k) n -> p k n", k=KD)
            for c in range(4):
                n = CW if c < 3 else TAIL
                sp.dma_start(ring_chunk(c, n), w_in[:, :, c * CW:c * CW + n]).then_inc(ring_in[c], 16)

            sp.wait_ge(mm_done, 4)
            sp.dma_start(ring[:, 0, 0:1536].rearrange("p (k n) -> p k n", k=2),
                         ins["w_uq"][0].rearrange("(p k) n -> p k n", k=2)).then_inc(ring_in[0], 16)
            sp.dma_start(ring[:, 0, 1536:2560], ins["w_ukv"][0]).then_inc(ring_in[0], 16)
            w_out = ins["w_out"][0].rearrange("(p k) n -> p k n", k=KD)
            for c in range(2):
                sp.wait_ge(mm_done, 4 * (c + 2))
                sp.dma_start(ring_chunk(5 + c), w_out[:, :, c * CW:(c + 1) * CW]).then_inc(ring_in[1 + c], 16)

            w_ff1 = ins["w_ff1"][0].rearrange("(p k) n -> p k n", k=KD)
            w_ff2 = ins["w_ff2"][0].rearrange("(g p j) n -> g p (j n)", p=P, j=4)

            def load_ff1(g, slot):
                sp.dma_start(ring_chunk(slot), w_ff1[:, :, bass.ds(g * CW, CW)]).then_inc(ring_in[slot], 16)

            def load_ff2(g, slot):
                sp.dma_start(ring[:, slot, :], w_ff2[bass.ds(g, 1)].rearrange("g p n -> (g p) n")).then_inc(ring_in[slot], 16)

            sp.wait_ge(mm_done, 16)
            load_ff1(0, 3)
            sp.wait_ge(proj_done, NT)
            load_ff1(1, 0)
            with sp.Fori(0, 3) as i:
                for m, (load, g) in enumerate(((load_ff2, 0), (load_ff1, 2), (load_ff2, 1), (load_ff1, 3)), 1):
                    sp.wait_ge(w_lo, 4 * i + m)
                    load(2 * i + g, m % RING)
            for m, g in ((1, 6), (2, 7)):
                sp.wait_ge(w_lo, 12 + m)
                load_ff2(g, m)

            w_in_2 = ins["w_in_2"][0].rearrange("(p k) n -> p k n", k=KD)
            w_out_2 = ins["w_out_2"][0].rearrange("(p k) n -> p k n", k=KD)
            peer_wq = ins["peer_wq_2"][0].rearrange("(p k) n -> p k n", k=KD)
            later = [(w_in_2, c) for c in range(7)] + [(w_out_2, c) for c in range(2)] + [(peer_wq, c) for c in range(4)]
            for s, (w, c) in enumerate(later, S_IN2):
                sp.wait_ge(w_lo, s - 3)
                sp.dma_start(ring_chunk(s + 5), w[:, :, c * CW:(c + 1) * CW]).then_inc(ring_in[(s + 5) % RING], 16)
                if s == 28:
                    sp.wait_ge(y2_ready, NT * H)
                    sp.dma_start(keys, ins["peer_subkeys_2"][0].rearrange("h a n d -> n (h a) d")).then_inc(keys_in, 16)

            peer_u = ins["peer_u_2"][0].rearrange("(p j) d -> p (j d)", p=P)
            peer_v = ins["peer_v_2"][0].rearrange("(p j) d -> p (j d)", p=P)

            def load_rows(table, g, slot):
                sp.dma_start(ring[:, slot, :], table[:, bass.ds(g * (4 * D), 4 * D)]).then_inc(ring_in[slot], 16)

            def load_gates(g, par):
                sp.dma_start(gates[:, par, :, :], gate_dram[:, bass.ds(g * 4, 4), :]).then_inc(gates_in[par], 16)

            for q, (table, g) in enumerate(((peer_u, 0), (peer_u, 1), (peer_v, 0), (peer_u, 2))):
                sp.wait_ge(w_lo, 28 + q)
                load_rows(table, g, q)
            sp.sem_inc(gate_stored[0], 16)
            sp.sem_inc(gate_stored[1], 16)
            with sp.Fori(0, NT) as i:
                for b in range(2):
                    sp.wait_ge(gate_out, i * 32 + (16 * (b + 1) + 2))
                    sp.dma_start(gate_dram[:, :, bass.ds(i * P + b * TB, TB)], gate_block[b]).then_inc(gate_stored[b], 16)
            sp.dma_start(out_gain, ins["final_norm_g_2"].unsqueeze(0).to_broadcast([P, D])).then_inc(out_gain_in, 16)
            sp.wait_ge(gate_stored[0], 16 * NT + 16)
            sp.wait_ge(gate_stored[1], 16 * NT + 16)
            load_gates(0, 0)
            load_gates(1, 1)
            sp.wait_ge(u_turned, 8)
            load_rows(peer_v, 1, 0)
            with sp.Fori(1, 15) as i:
                sp.wait_ge(u_turned, 16 * i)
                load_rows(peer_u, 2 * i + 1, 1)
                sp.wait_ge(w_lo, 2 * i + 30)
                load_rows(peer_v, 2 * i, 2)
                sp.wait_ge(ex_mul, 8 * i - 4)
                load_gates(2 * i, 0)
                sp.wait_ge(u_turned, 16 * i + 8)
                load_rows(peer_u, 2 * i + 2, 3)
                sp.wait_ge(w_lo, 2 * i + 31)
                load_rows(peer_v, 2 * i + 1, 0)
                sp.wait_ge(ex_mul, 8 * i)
                load_gates(2 * i + 1, 1)
            sp.wait_ge(u_turned, 8 * 30)
            load_rows(peer_u, 31, 1)
            sp.wait_ge(w_lo, 31 + 29)
            load_rows(peer_v, 30, 2)
            sp.wait_ge(ex_mul, 4 * 29)
            load_gates(30, 0)
            sp.wait_ge(ex_mul, 4 * 30)
            load_gates(31, 1)
            sp.wait_ge(u_turned, 8 * 31)
            load_rows(peer_v, 31, 3)

            for t in range(NT):
                sp.wait_ge(out_ready, t + 1)
                sp.dma_start(out[0, t * P:(t + 1) * P, :], out_rows[:, t, :]).then_inc(out_stored, 16)
            sp.wait_ge(out_stored, 16 * NT)

        @block.gpsimd
        def _(pool):
            own = Steps(pool, own_p)
            pool.memset(minus_half, -0.5).then_inc(filled, 1)
            pool.memset(ones, 1.0).then_inc(filled, 1)
            pool.memset(one_col, 1.0).then_inc(filled, 1)
            pool.memset(gains[:, :], 1.0).then_inc(filled, 1)
            pool.memset(gate_pad, 0.0).then_inc(filled, 1)
            pool.memset(prev_max, 0.0).then_inc(filled, 1)
            pool.memset(dec_rows, 0.0).then_inc(filled, 1)
            pool.memset(conv_in[:, :, 0:2], 0.0).then_inc(filled, 1)
            pool.memset(conv_in[:, :, T + 2:T + 4], 0.0).then_inc(filled, 1)

            def inverse_rms(n, width, ssq_count, at=0):
                c = slice(at, at + n)
                pool.wait_ge(ssq_done, ssq_count)
                own.did(pool.tensor_scalar(mean_eps[:, c], sumsq[:, c], 1.0 / width, EPS, ALU.mult, ALU.add))
                own.wait()
                pool.tensor_tensor(rstd[:, c], mean_eps[:, c], minus_half[:, 0:n], ALU.pow).then_inc(rstd_done, 1)

            pool.wait_ge(filled, 9)
            inverse_rms(NT, D, NT)
            inverse_rms(NT * H, DV, NT + NT * H)

            pool.wait_ge(ssq_done, 28)
            own.did(pool.tensor_scalar(mean_eps[:, 16:20], sumsq[:, 16:20], 1.0 / Q_LORA, EPS, ALU.mult, ALU.add))
            own.did(pool.tensor_scalar(mean_eps[:, 20:24], sumsq[:, 20:24], 1.0 / KV_LORA, EPS, ALU.mult, ALU.add))
            own.wait()
            pool.tensor_tensor(rstd[:, 16:24], mean_eps[:, 16:24], minus_half[:, 0:8], ALU.pow).then_inc(rstd_done, 1)
            for t in range(NT):
                if t >= 2:
                    pool.wait_ge(qk_turned, t - 1)
                pool.tensor_copy(qk_tok[:, t % 2, H:2 * H, A_NOPE:A_DH],
                                 tail[:, t, C_KPE:TAIL].unsqueeze(1).to_broadcast([P, H, A_ROPE])).then_inc(pe_put, 1)
                pool.wait_ge(qk_summed, t + 1)
                own.did(pool.tensor_scalar(qk_mean[:, t, :], qk_sumsq[:, t, :], 1.0 / A_DH, EPS, ALU.mult, ALU.add))
                own.wait()
                pool.tensor_tensor(qk_rstd[:, t, :], qk_mean[:, t, :], minus_half[:, 0:2 * H], ALU.pow).then_inc(qk_rstd_done, 1)

            def split_low(s, s4):
                pool.wait_ge(w_hi, s + 1)
                pool.tensor_tensor(split[:, s4 % 2, 1, :], ring[:, (s4 + 5) % RING, :], split[:, s4 % 2, 0, :], ALU.subtract).then_inc(w_lo, 1)

            for s in range(3):
                split_low(s, s)
            inverse_rms(NT, D, 32)
            with pool.Fori(0, 3) as i:
                for m in range(4):
                    split_low(4 * i + 3 + m, (3 + m) % 4)
            for s in range(15, 18):
                split_low(s, s % 4)

            split_low(18, 2)
            inverse_rms(NT, D, 36)
            for s in range(19, 26):
                split_low(s, s % 4)
            pool.wait_ge(w_used, 25)
            pool.wait_ge(mm_out, MM["out2"])
            for h in range(H):
                if h >= 2:
                    pool.wait_ge(ret_o, h - 1)
                pool.tensor_tensor(ret_q[:, h % 2, :, :], rqT[:, h, :].rearrange("p (c i) -> p c i", c=NC),
                                   const("cross", h=H, i=P)[:, h, :].unsqueeze(1).to_broadcast([P, NC, P]), ALU.mult).then_inc(ret_qx, 1)
            inverse_rms(NT * H, RET_DK, 52)
            split_low(26, 2)
            inverse_rms(NT * H, DV, 68, 16)
            split_low(27, 3)

            inverse_rms(NT, D, 72)
            for s in range(28, 31):
                split_low(s, s % 4)

            pool.wait_ge(key_tops, 2 * P_HEADS)

            def sums(t):
                if t >= 2:
                    pool.wait_ge(picks_top, 2 * t - 2)
                four = [P, P_HEADS, TOPK, TOPK]
                pool.tensor_tensor(cand[:, t % 2, :, :, :], top_v[:, t, 0::2, :].unsqueeze(3).to_broadcast(four),
                                   top_v[:, t, 1::2, :].unsqueeze(2).to_broadcast(four), ALU.add).then_inc(cands, 1)

            def lookup(t):
                four = [P, P_HEADS, TOPK, TOPK]
                pool.wait_ge(match_eq, t + 1)
                pool.tensor_tensor(match1, match1, top_f[:, t, 1::2, :].unsqueeze(2).to_broadcast(four), ALU.mult).then_inc(match_p, 1)

            for t in range(NT):
                sums(t)
            for t in range(NT):
                lookup(t)

            def v_low(g, slot, s2):
                pool.wait_ge(w_hi, g + (S_EX + 1))
                pool.tensor_tensor(split[:, s2, 1, :], ring[:, slot, :], split[:, s2, 0, :], ALU.subtract).then_inc(w_lo, 1)

            v_low(0, 2, 1)
            v_low(1, 0, 0)
            with pool.Fori(1, 15) as i:
                v_low(2 * i, 2, 1)
                v_low(2 * i + 1, 0, 0)
            v_low(30, 2, 1)
            v_low(31, 3, 0)
            inverse_rms(NT, D, 76)

        @block.scalar
        def _(act):
            own = Steps(act, own_a)
            act.dma_start(consts[:, :], ins["table"]).then_inc(const_in, 16)
            act.dma_start(conv_rows[0:TAPS, :], ins["conv_w"][0]).then_inc(small_in, 16)
            act.dma_start(conv_rows[TAPS:TAPS + 1, :], ins["conv_b"]).then_inc(small_in, 16)
            act.dma_start(gate_bias, ins["b_gates"].to_broadcast([P, 16])).then_inc(small_in, 16)
            act.wait_ge(filled, 4)
            for at, name, parts, cols in (
                (G_MIX, "g_mix_norm", (0, P), KD), (G_Y1, "g_mlstm_out", (0, 64), KD), (G_FFN, "g_ffn_norm", (0, P), KD),
                (G_MIX2, "norm_mix_g_2", (0, P), KD), (G_FFN2, "norm_ffn_g_2", (0, P), KD),
                (G_CQ, "g_cq", (0, P), 2), (G_CKV, "g_ckv", (0, P), 1),
            ):
                act.dma_start(gains[parts[0]:parts[1], at:at + cols],
                              ins[name][0].rearrange("(p k) -> p k", k=cols)).then_inc(small_in, 16)
            act.dma_start(gains[:, G_QN:G_QN + 1], ins["g_q"][0, 0:P].rearrange("(p k) -> p k", k=1)).then_inc(small_in, 16)
            act.dma_start(gains[:, G_KN:G_KN + 1], ins["g_k"][0, 0:P].rearrange("(p k) -> p k", k=1)).then_inc(small_in, 16)
            for h in range(H):
                act.dma_start(gains[64 + 16 * h:80 + 16 * h, G_Y2:G_Y2 + KD],
                              ins["diff_subln_g_2"][0].rearrange("(p k) -> p k", k=KD)).then_inc(small_in, 16)
            act.dma_start(rope_gain[:, 0, :], ins["g_q"][0:1, P:A_DH].to_broadcast([P, A_ROPE])).then_inc(small_in, 16)
            act.dma_start(rope_gain[:, 1, :], ins["g_k"][0:1, P:A_DH].to_broadcast([P, A_ROPE])).then_inc(small_in, 16)
            act.dma_start(lam_in, ins["diff_lambda_2"].to_broadcast([P, 4, DIFF_D])).then_inc(small_in, 16)
            act.dma_start(pos_rows[0:NT, :].bitcast(I32), ins["positions"][0].rearrange("(t p) -> t p", p=P)).then_inc(small_in, 16)


            squares = Steps(act, ssq_done)

            def sum_squares(src, spare, column):
                if squares.n:
                    squares.wait()
                squares.did(act.activation(spare, src, ACT.Square, accum_out=sumsq[:, column:column + 1]))

            act.wait_ge(x_in, 16)
            for t in range(NT):
                sum_squares(x_sb[:, t, :], ps[:, 6:8, :].rearrange("p a b -> p (a b)"), t)

            act.wait_ge(small_in, 16 * SMALLS)
            for k in range(KD):
                act.wait_ge(turned, k + 1)
                act.activation(hT[:, k, :], bank(k % 2), ACT.Copy, scale=gains[:, G_MIX + k:G_MIX + k + 1]).then_inc(turned_hi, 1)

            for f in range(4):
                act.wait_ge(conv_done, f + 1)
                act.activation(qkT[:, f, :], qkT[:, f, :], ACT.Silu).then_inc(qk_done, 1)
            for f in range(2):
                act.wait_ge(ktok_turned, f + 1)
                act.activation(k_tok[:, :, f * P:(f + 1) * P], bank(f).rearrange("p (t c) -> p t c", t=NT), ACT.Copy).then_inc(ktok_done, 1)

            act.wait_ge(f_neg, 1)
            own.did(act.activation(t_row[0:ROWS, :], u_row[0:ROWS, :], ACT.Exp))
            own.wait()
            act.activation(t_row[0:ROWS, :], t_row[0:ROWS, :], ACT.Ln, bias=1.0).then_inc(f_log, 1)
            for i, r in enumerate((inter_row, em_row, w_row)):
                act.wait_ge(rows_ready, 2 + i)
                act.activation(r[0:ROWS, :], r[0:ROWS, :], ACT.Exp).then_inc(rows_exp, 1)

            for h in range(H):
                act.wait_ge(decay_in, h + 1)
                act.activation(decay[:, h % 2, :, :], decay[:, h % 2, :, :], ACT.Exp).then_inc(decay_exp, 1)
                act.wait_ge(num_done, h + 1)
                if h >= 1:
                    act.wait_ge(head_out, h)
                for d in range(2):
                    act.activation(num[:, d, :, :], bank(4 + d).rearrange("p (c v) -> p c v", c=NC), ACT.Copy).then_inc(num_out, 1)
                act.wait_ge(head_out, h + 1)
                for t in range(NT):
                    sum_squares(y1[:, t, h * DV:(h + 1) * DV], decay[:, h % 2, 0, 0:P], t * H + h)
            act.activation(o1, o1, ACT.Sigmoid).then_inc(o_sig, 1)

            for t in range(NT):
                sum_squares(tail[:, t, C_CQ:C_CKV], att[:, 0, 0:Q_LORA], 16 + t)
            for t in range(NT):
                sum_squares(tail[:, t, C_CKV:C_KPE], att[:, 0, 0:KV_LORA], 20 + t)
            act.wait_ge(angles, 2)
            act.activation(sin_t, angle, ACT.Sin).then_inc(rotary, 1)
            act.activation(cos_t, angle_c, ACT.Sin).then_inc(rotary, 1)
            for k, b in enumerate((0, 1, 4)):
                act.wait_ge(turned, TURN["latent"] + k + 1)
                dst, gain = (cqT[:, k, :], G_CQ + k) if k < 2 else (ckvT, G_CKV)
                act.activation(dst, bank(b), ACT.Copy, scale=gains[:, gain:gain + 1]).then_inc(turned_hi, 1)
            for t in range(NT):
                act.wait_ge(qk_put, t + 1)
                for b in range(2):
                    act.activation(v2[:, t, 2 * b:2 * b + 2, :], bank(4 + b).rearrange("p (h n) -> p h n", h=2)[:, :, A_NOPE:],
                                   ACT.Copy).then_inc(v_put, 1)
                act.wait_ge(pe_put, t + 1)
                if t >= 1:
                    act.wait_ge(qk_summed, t)
                act.activation(qk_sq, qk_tok[:, t % 2, :, :], ACT.Square).then_inc(qk_squared, 1)
                act.wait_ge(qk_turned, t + 1)
                for b in range(2):
                    act.activation(nopeT[:, b * H:(b + 1) * H, t * P:(t + 1) * P], bank(b).rearrange("p (h n) -> p h n", h=H), ACT.Copy,
                                   scale=gains[:, G_QN + b:G_QN + b + 1]).then_inc(nope_out, 1)

            def split_high(s, s4, rounds):
                j4 = (s4 + 5) % RING
                act.wait_ge(ring_in[j4], arrived(j4, rounds))
                act.wait_ge(w_used, s - 1)
                act.activation(split[:, s4 % 2, 0, :], ring[:, j4, :], ACT.Copy).then_inc(w_hi, 1)

            for i in range(H * NT):
                act.wait_ge(att_max, i + 1)
                if i >= 2:
                    act.wait_ge(att_turned, i - 1)
                act.activation(att[:, i % 2, :], bank(2 + i % 2), ACT.Exp, bias=row_nmax[:, i:i + 1], scale=A_DH ** -0.5,
                               accum_out=row_sum[:, i:i + 1]).then_inc(att_exp, 1)
                if i in (3, 7):
                    s = i // 4
                    act.wait_ge(rope_out, 2 * NT)
                    act.wait_ge(ring_in[1 + s], arrived(1 + s, 1))
                    act.activation(split[:, s, 0, :], ring[:, 1 + s, :], ACT.Copy).then_inc(w_hi, 1)

            def turned_high(stage, gain, hi=xT_hi):
                for k in range(KD):
                    act.wait_ge(turned, TURN[stage] + k + 1)
                    act.activation(hi[:, k, :], bank(k % 2), ACT.Copy, scale=gains[:, gain + k:gain + k + 1]).then_inc(turned_hi, 1)

            turned_high("out", G_Y1)
            split_high(2, 2, 1)
            act.wait_ge(mm_out, MM["out"] + 8)
            for t in range(NT):
                sum_squares(x_sb[:, t, :], ps[:, 6:8, :].rearrange("p a b -> p (a b)"), t)
            turned_high("ffn", G_FFN)

            def square_high(g, par):
                for j in range(4):
                    act.wait_ge(ff_relu, 4 * g + j + 1)
                    act.activation(hid_hi[:, par, j, :], relu[:, j % 2, :], ACT.Square).then_inc(ff_hi, 1)

            split_high(3, 3, 2)
            square_high(0, 0)
            with act.Fori(0, 3) as i:
                split_high(4 * i + 4, 0, i + 2)
                square_high(2 * i + 1, 1)
                split_high(4 * i + 5, 1, i + 2)
                split_high(4 * i + 6, 2, i + 2)
                square_high(2 * i + 2, 0)
                split_high(4 * i + 7, 3, i + 3)
            split_high(16, 0, 5)
            square_high(7, 1)
            split_high(17, 1, 5)

            split_high(18, 2, 5)
            act.wait_ge(ff_add, 8 * FF_GROUPS + 2)
            for t in range(NT):
                sum_squares(x_sb[:, t, :], ps[:, 6:8, :].rearrange("p a b -> p (a b)"), t)
            turned_high("mix2", G_MIX2)
            for s in range(19, 26):
                split_high(s, s % 4, (s + 5) // 4)

            kdec = const("kdec")
            for h in range(H):
                act.wait_ge(ret_kturned, h + 1)
                if h >= 2:
                    act.wait_ge(ret_kv, h - 1)
                act.activation(ret_k[:, h % 2, :, :], bank(1).rearrange("p (c d) -> p c d", c=NC), ACT.Copy, scale=kdec[:, h:h + 1]).then_inc(ret_kd, 1)
                if h == 0:
                    act.activation(rg, rg, ACT.Silu).then_inc(rg_silu, 1)
                act.wait_ge(ret_y, h + 1)
                for t in range(NT):
                    sum_squares(y2[:, t, h * DV:(h + 1) * DV], spare_row, t * H + h)
            act.wait_ge(lam_sums, 1)
            act.activation(lam[:, 2:4], lam[:, 0:2], ACT.Exp).then_inc(lam_exp, 1)

            for i in range(H * NT + 1):
                if i < H * NT:
                    n_keys = (i % NT + 1) * P
                    for m in range(2):
                        act.wait_ge(dif_max, 2 * i + m + 1)
                        act.activation(dif[:, i % 2, m, 0:n_keys], dif[:, i % 2, m, 0:n_keys], ACT.Exp, bias=row_nmax[:, 2 * i + m:2 * i + m + 1],
                                       accum_out=row_sum[:, 2 * i + m:2 * i + m + 1]).then_inc(dif_exp, 1)
                if i == 4:
                    split_high(26, 2, 7)
                if i >= 3:
                    n = i - 3
                    h, q = divmod(n, NT)
                    act.wait_ge(dif_y, n + 1)
                    sum_squares(y2[:, q, 512 + h * DV:512 + (h + 1) * DV], dif_sq, 16 + q * H + h)
            for n in (14, 15):
                h, q = divmod(n, NT)
                act.wait_ge(dif_y, n + 1)
                sum_squares(y2[:, q, 512 + h * DV:512 + (h + 1) * DV], dif_sq, 16 + q * H + h)
            turned_high("out2", G_Y2, y2T_hi)
            split_high(27, 3, 8)

            act.wait_ge(mm_out, MM["wq"])
            for t in range(NT):
                sum_squares(x_sb[:, t, :], ps[:, 6:8, :].rearrange("p a b -> p (a b)"), t)
            for b in range(4):
                act.wait_ge(keys_turned, b + 1)
                act.activation(keysT[:, 4 * b:4 * b + 4, :], bank(4 + b % 2).rearrange("p (g n) -> p g n", g=4), ACT.Copy).then_inc(keys_out, 1)
            turned_high("peer", G_FFN2)
            for n in range(16):
                if n % 4 == 0 and n < 12:
                    split_high(28 + n // 4, (28 + n // 4) % 4, (33 + n // 4) // 4)
                act.wait_ge(mm_done, MM["wq"] + n + 1)
                if n >= 2:
                    act.wait_ge(key_scores, n - 1)
                act.activation(half_q[:, n % 2, :], bank(2 + n % 2), ACT.Copy).then_inc(mm_out, 1)
            act.wait_ge(gate_in, 1)
            act.activation(pick_g, pick_g, ACT.Exp).then_inc(gate_exp, 1)
            act.sem_inc(gate_out, 2)
            with act.Fori(0, NT) as i:
                for k in range(32):
                    b = k // 16
                    act.wait_ge(gate_mm, i * 32 + (k + 3))
                    if k % 16 == 0:
                        act.wait_ge(gate_stored[b], i * 16 + 16)
                    at = 4 * (k % 16)
                    act.activation(gate_block[b][:, :, at:at + 4].rearrange("p n t -> p t n"),
                                   bank(k % 2).rearrange("p (t n) -> p t n", t=4), ACT.Copy).then_inc(gate_out, 1)

            def u_high(g, j):
                for b in range(2):
                    act.wait_ge(u_turned, 8 * g + (2 * j + b + 1))
                    act.activation(uT_hi[:, j % 2, 4 * b:4 * b + 4, :], bank((0, 6)[j % 2] + b).rearrange("p (k n) -> p k n", k=4),
                                   ACT.Copy).then_inc(u_hi, 1)

            def expert_tiles(g, par):
                act.wait_ge(w_used, g + 30)
                for j in range(4):
                    if j < 3:
                        u_high(g, j + 1)
                    act.wait_ge(ex_a, 4 * g + (j + 1))
                    act.wait_ge(ex_mul, 4 * g + max(j - 1, 0))
                    act.activation(gelu[:, j % 2, :], bank(2 + j % 2), ACT.Gelu).then_inc(ex_gelu, 1)
                    act.wait_ge(ex_mul, 4 * g + (j + 1))
                    act.activation(ex_hi[:, par, j, :], act_g[:, j % 2, :], ACT.Copy).then_inc(ex_hi_done, 1)

            def v_high(g, slot, rounds, s2):
                act.wait_ge(ring_in[slot], arrived(slot, rounds))
                act.wait_ge(w_used, g + 30)
                act.activation(split[:, s2, 0, :], ring[:, slot, :], ACT.Copy).then_inc(w_hi, 1)

            act.wait_ge(gate_stored[0], 16 * NT + 16)
            act.wait_ge(gate_stored[1], 16 * NT + 16)
            u_high(0, 0)
            expert_tiles(0, 0)
            v_high(0, 2, 9, 1)
            u_high(1, 0)
            with act.Fori(0, 15) as i:
                expert_tiles(2 * i + 1, 1)
                v_high(2 * i + 1, 0, i + 10, 0)
                u_high(2 * i + 2, 0)
                expert_tiles(2 * i + 2, 0)
                v_high(2 * i + 2, 2, i + 10, 1)
                u_high(2 * i + 3, 0)
            expert_tiles(31, 1)
            v_high(31, 3, 24, 0)

            act.wait_ge(ex_add, 8 * EX_GROUPS + 2)
            for t in range(NT):
                sum_squares(x_sb[:, t, :], ps[:, 6:8, :].rearrange("p a b -> p (a b)"), t)

        @block.tensor
        def _(pe):
            def turn(n, dst_bank, src):
                for t in range(NT):
                    mm = pe.transpose(bank(dst_bank)[:, t * P:(t + 1) * P], src(t), ident)
                mm.then_inc(turned, 1)

            pe.wait_ge(const_in, 16)
            pe.wait_ge(xn_done, NT)
            xn_k = xn1.rearrange("p t (c k) -> p t c k", k=KD)
            for k in range(KD):
                if k >= 2:
                    pe.wait_ge(turned_hi, k - 1)
                turn(k, k % 2, lambda t: xn_k[:, t, :, k])

            pe.wait_ge(turned_hi, KD)
            for c in range(4):
                chunk_here(pe, c)
                w = ring_chunk(c, CW if c < 3 else TAIL)
                for r in range(4):
                    n = 4 * c + r
                    if n >= 2:
                        pe.wait_ge(mm_out, n - 1)
                    for k in range(KD):
                        if c == 0:
                            mm = pe.matmul(bank(2 + n % 2), w[:, k, r * P:(r + 1) * P], hT[:, k, :], start=k == 0, stop=k == KD - 1)
                        else:
                            mm = pe.matmul(bank(2 + n % 2)[:, 0:(CW if c < 3 else TAIL)], hT[:, k, r * P:(r + 1) * P], w[:, k, :],
                                           start=k == 0, stop=k == KD - 1)
                    mm.then_inc(mm_done, 1)

            pe.wait_ge(small_in, 16 * SMALLS)
            for f in range(4):
                mm = pe.transpose(bank(4)[:, f * 8:f * 8 + 6], conv_rows[0:6, f * P:(f + 1) * P], ident[0:6, 0:6])
            mm.then_inc(conv_turned, 1)

            for f in range(2):
                pe.wait_ge(qk_done, 3 + f)
                for t in range(NT):
                    mm = pe.transpose(bank(f)[:, t * P:(t + 1) * P], qkT[:, 2 + f, t * P:(t + 1) * P], ident)
                mm.then_inc(ktok_turned, 1)

            pe.wait_ge(gates_padded, 4)
            for kind in range(2):
                for t in range(NT):
                    mm = pe.transpose(bank(5 + kind)[0:ROWS, t * P:(t + 1) * P], gate_pad[:, t, kind, 0:ROWS], ident)
                mm.then_inc(gates_turned, 1)

            pe.wait_ge(rows_exp, 3)
            for i, r in enumerate((c_row, inter_row, em_row, w_row)):
                for c in range(NC):
                    mm = pe.transpose(bank(4 + i // 2)[:, ((i % 2) * NC + c) * ROWS:((i % 2) * NC + c + 1) * ROWS],
                                      r[0:ROWS, c * P:(c + 1) * P], ident[0:ROWS, 0:ROWS])
                mm.then_inc(cols_turned, 1)
            pe.wait_ge(rows_ready, 5)
            for d in range(2):
                for h in range(H):
                    r = 32 * d + h
                    mm = pe.matmul(bank(6)[:, (d * H + h) * NC:(d * H + h + 1) * NC], ident[0:ROWS, r:r + 1].to_broadcast([ROWS, P]),
                                   dec_rows[0:ROWS, :], start=True, stop=True)
            mm.then_inc(cols_turned, 1)

            def mlstm_scores(h):
                at = (h % 2) * DQK
                for c in range(NC):
                    mm = pe.matmul(bank(0)[:, c * P:(c + 1) * P], qkT[at:at + DQK, 2 + h // 2, c * P:(c + 1) * P],
                                   qkT[at:at + DQK, h // 2, c * P:(c + 1) * P], start=True, stop=True)
                for d in range(2):
                    r = 32 * d + h
                    mm = pe.matmul(bank(2 + d), ident[0:ROWS, r:r + 1].to_broadcast([ROWS, P]), negm_row[0:ROWS, :], start=True, stop=True)
                mm.then_inc(scores_done, 1)

            pe.wait_ge(cols_done, 4)
            pe.wait_ge(ktok_done, 2)
            for h in range(H):
                at = (h % 2) * DQK
                mlstm_scores(h)
                pe.wait_ge(kdec_done, h + 1)
                for d in range(2):
                    for i in range(3):
                        c = i + d
                        pe.matmul(bank(6 + d)[at:at + DQK, i * 129:i * 129 + P], k_dec[:, d, i, :], v1[:, c, h * DV:(h + 1) * DV],
                                  start=True, stop=True)
                        mm = pe.matmul(bank(6 + d)[at:at + DQK, i * 129 + P:i * 129 + 129], k_dec[:, d, i, :], one_col,
                                       start=True, stop=True)
                mm.then_inc(kv_done, 1)
                pe.wait_ge(probs_done, 2 * h + 2)
                for d in range(2):
                    for c in range(NC):
                        pe.matmul(bank(4 + d)[:, c * P:(c + 1) * P], probs[:, h % 2, d, c, :], v1[:, c, h * DV:(h + 1) * DV],
                                  start=True, stop=True)
                        mm = pe.matmul(bank(1)[:, d * NC + c:d * NC + c + 1], probs[:, h % 2, d, c, :], one_col, start=True, stop=True)
                mm.then_inc(num_done, 1)
                pe.wait_ge(state_done, h + 1)
                for d in range(2):
                    for i in range(3):
                        c = i + 1 - d
                        mm = pe.matmul(bank(2 + d)[:, i * 129:(i + 1) * 129], qkT[at:at + DQK, h // 2, c * P:(c + 1) * P],
                                       state[at:at + DQK, d, i, 0:129], start=True, stop=True)
                mm.then_inc(inter_done, 1)
                if h < H - 1:
                    pe.wait_ge(head_out, h + 1)

            pe.wait_ge(pos_turned, 1)
            pe.transpose(bank(6)[:, 0:NT], pos_f[0:NT, :], ident[0:NT, 0:NT]).then_inc(pos_turned, 1)
            pe.wait_ge(latent_done, 2 * NT)
            cq_k = tail[:, :, C_CQ:C_CKV].rearrange("p t (c k) -> p t c k", k=2)
            turn(0, 0, lambda t: cq_k[:, t, :, 0])
            turn(1, 1, lambda t: cq_k[:, t, :, 1])
            turn(2, 4, lambda t: tail[:, t, C_CKV:C_KPE])

            w_uq = ring[:, 0, 0:1536].rearrange("p (k n) -> p k n", k=2)
            w_ukv = ring[:, 0, 1536:2560]

            def project(t):
                if t >= 1:
                    pe.wait_ge(qk_put, t)
                    pe.wait_ge(v_put, 2 * t)
                for b, (at, n) in enumerate(((0, 512), (512, 256))):
                    for k in range(2):
                        pe.matmul(bank(2 + b)[:, 0:n], cqT[:, k, t * P:(t + 1) * P], w_uq[:, k, at:at + n], start=k == 0, stop=k == 1)
                for b in range(2):
                    mm = pe.matmul(bank(4 + b), ckvT[:, t * P:(t + 1) * P], w_ukv[:, b * 512:(b + 1) * 512], start=True, stop=True)
                mm.then_inc(proj_done, 1)

            pe.wait_ge(turned_hi, TURN["latent"] + 3)
            chunk_here(pe, 4)
            project(0)
            for t in range(NT):
                if t < NT - 1:
                    project(t + 1)
                pe.wait_ge(qk_rotated, t + 1)
                if t >= 1:
                    pe.wait_ge(nope_out, 2 * t)
                    pe.wait_ge(rope_out, 2 * t)
                for i in range(2 * H):
                    pe.transpose(bank(i // H)[:, (i % H) * P:(i % H + 1) * P], qk_tok[:, t % 2, i, 0:A_NOPE], ident)
                    mm = pe.transpose(bank(6 + i // H)[0:A_ROPE, (i % H) * P:(i % H + 1) * P], rot[:, i, :], ident)
                mm.then_inc(qk_turned, 1)

            pe.wait_ge(nope_out, 2 * NT)
            pe.wait_ge(rope_out, 2 * NT)
            pe.wait_ge(v_put, 2 * NT)
            for i in range(H * NT + 2):
                if i < H * NT:
                    h, q = divmod(i, NT)
                    if i >= 2:
                        pe.wait_ge(att_exp, i - 1)
                    pe.matmul(bank(2 + i % 2), nopeT[:, h, q * P:(q + 1) * P], nopeT[:, H + h, :], start=True, stop=False)
                    pe.matmul(bank(2 + i % 2), ropeT[0:A_ROPE, h, q * P:(q + 1) * P], ropeT[0:A_ROPE, H + h, :],
                              start=False, stop=True).then_inc(att_scores, 1)
                if 1 <= i <= H * NT:
                    n = i - 1
                    pe.wait_ge(att_exp, n + 1)
                    if n >= 2:
                        pe.wait_ge(att_out, n - 1)
                    for k in range(NT):
                        mm = pe.transpose(bank(4 + n % 2)[:, k * P:(k + 1) * P], att[:, n % 2, k * P:(k + 1) * P], ident)
                    mm.then_inc(att_turned, 1)
                if i >= 2:
                    n = i - 2
                    h, q = divmod(n, NT)
                    pe.wait_ge(att_out, n + 1)
                    if n >= 2:
                        pe.wait_ge(att_norm, n - 1)
                    for k in range(NT):
                        mm = pe.matmul(bank(6 + n % 2)[:, 0:DV], attT[:, n % 2, k * P:(k + 1) * P], v2[:, k, h, :],
                                       start=k == 0, stop=k == NT - 1)
                    mm.then_inc(att_pv, 1)

            def turn_features(stage, src):
                src_k = src.rearrange("p t (c k) -> p t c k", k=KD)
                for k in range(KD):
                    if k >= 2:
                        pe.wait_ge(turned_lo, TURN_LO[stage] + k - 1)
                    turn(k, k % 2, lambda t: src_k[:, t, :, k])

            def three_pass(dst, hi, lo, w_hi_, w_lo_, steps):
                terms = [(a, b, k) for a, b in ((hi, w_hi_), (hi, w_lo_), (lo, w_hi_)) for k in range(steps)]
                for n, (a, b, k) in enumerate(terms):
                    mm = pe.matmul(dst, a(k), b(k), start=n == 0, stop=n == len(terms) - 1)
                return mm

            def linear_chunk(s, done_before, feature_rows, hi=xT_hi, lo=xT_lo):
                pe.wait_ge(w_hi, s + 1)
                pe.wait_ge(w_lo, s + 1)
                wh, wl = high(s % 2, KD), low(s % 2, KD)
                for r in range(4):
                    n = done_before + r
                    pe.wait_ge(mm_out, n - 1)
                    at = slice(r * P, (r + 1) * P)
                    if feature_rows:
                        mm = three_pass(bank(2 + n % 2), lambda k: wh[:, k, at], lambda k: wl[:, k, at],
                                        lambda k: hi[:, k, :], lambda k: lo[:, k, :], KD)
                    else:
                        mm = three_pass(bank(2 + n % 2), lambda k: hi[:, k, at], lambda k: lo[:, k, at],
                                        lambda k: wh[:, k, :], lambda k: wl[:, k, :], KD)
                    mm.then_inc(mm_done, 1)
                pe.wait_ge(mm_done, done_before + 4)
                pe.sem_inc(w_used, 1)

            pe.wait_ge(y_ready, NT * H)
            pe.wait_ge(att_norm, H * NT)
            turn_features("out", y1)
            pe.wait_ge(turned_lo, TURN_LO["out"] + KD)
            for c in range(2):
                linear_chunk(S_OUT + c, MM["out"] + 4 * c, False)

            pe.wait_ge(xn_done, 2 * NT)
            turn_features("ffn", xn)
            pe.wait_ge(turned_lo, TURN_LO["ffn"] + KD)

            def ff_up(g, par, s, s2):
                pe.wait_ge(w_hi, s + 1)
                pe.wait_ge(w_lo, s + 1)
                wh = split[:, s2, 0, :].rearrange("p (k c j) -> p k c j", k=KD, j=4)
                wl = split[:, s2, 1, :].rearrange("p (k c j) -> p k c j", k=KD, j=4)
                for j in range(4):
                    pe.wait_ge(ff_relu, 4 * g + max(j - 1, 0))
                    three_pass(bank(2 + j % 2), lambda k: wh[:, k, :, j], lambda k: wl[:, k, :, j],
                               lambda k: xT_hi[:, k, :], lambda k: xT_lo[:, k, :], KD).then_inc(ff_a, 1)
                pe.wait_ge(ff_a, 4 * g + 4)
                pe.sem_inc(w_used, 1)

            def ff_down(g, par, s, s2):
                pe.wait_ge(w_hi, s + 1)
                pe.wait_ge(w_lo, s + 1)
                pe.wait_ge(ff_lo, 4 * g + 4)
                wh, wl = high(s2, 4), low(s2, 4)
                for b in range(8):
                    t, c = divmod(b, 2)
                    rows_, cols = slice(t * P, (t + 1) * P), slice(c * 512, (c + 1) * 512)
                    pe.wait_ge(ff_add, 8 * g + (b + 1))
                    three_pass(bank(4 + b % 2), lambda j: hid_hi[:, par, j, rows_], lambda j: hid_lo[:, par, j, rows_],
                               lambda j: wh[:, j, cols], lambda j: wl[:, j, cols], 4).then_inc(ff_b, 1)
                pe.wait_ge(ff_b, 8 * g + 8)
                pe.sem_inc(w_used, 1)

            ff_up(0, 0, 2, 0)
            with pe.Fori(0, 3) as i:
                ff_up(2 * i + 1, 1, 4 * i + 3, 1)
                ff_down(2 * i, 0, 4 * i + 4, 0)
                ff_up(2 * i + 2, 0, 4 * i + 5, 1)
                ff_down(2 * i + 1, 1, 4 * i + 6, 0)
            ff_up(7, 1, 15, 1)
            ff_down(6, 0, 16, 0)
            ff_down(7, 1, 17, 1)

            pe.wait_ge(xn_done, 3 * NT)
            turn_features("mix2", xn)
            pe.wait_ge(turned_lo, TURN_LO["mix2"] + KD)
            for c in range(7):
                linear_chunk(S_IN2 + c, MM["in2"] + 4 * c, c in (0, 1, 4, 5))

            pe.wait_ge(mm_out, MM["out2"])
            for h in range(H):
                if h >= 1:
                    pe.wait_ge(ret_a, h)
                    pe.wait_ge(ret_kd, h)
                for c in range(NC):
                    mm = pe.matmul(bank(0)[:, c * P:(c + 1) * P], rkT[:, h, c * P:(c + 1) * P], rqT[:, h, c * P:(c + 1) * P], start=True, stop=True)
                mm.then_inc(ret_scores, 1)
                for c in range(NC):
                    mm = pe.transpose(bank(1)[:, c * P:(c + 1) * P], rkT[:, h, c * P:(c + 1) * P], ident)
                mm.then_inc(ret_kturned, 1)
                pe.wait_ge(ret_kd, h + 1)
                if h >= 1:
                    pe.wait_ge(ret_state, h)
                for c in range(NC - 1):
                    mm = pe.matmul(bank(4)[:, c * P:(c + 1) * P], ret_k[:, h % 2, c, :], rv[:, c, h * DV:(h + 1) * DV], start=True, stop=True)
                mm.then_inc(ret_kv, 1)
                pe.wait_ge(ret_a, h + 1)
                pe.wait_ge(ret_qx, h + 1)
                pe.wait_ge(ret_state, h + 1)
                if h >= 1:
                    pe.wait_ge(ret_y, h)
                for c in range(NC):
                    dst = bank(5)[:, c * P:(c + 1) * P]
                    mm = pe.matmul(dst, ret_in[:, h % 2, c, :], rv[:, c, h * DV:(h + 1) * DV], start=True, stop=c == 0)
                    if c >= 1:
                        mm = pe.matmul(dst, ret_q[:, h % 2, c, :], ret_s[:, c - 1, :], start=False, stop=True)
                mm.then_inc(ret_o, 1)

            for i in range(H * NT + 2):
                if i < H * NT:
                    h, q = divmod(i, NT)
                    if i >= 2:
                        pe.wait_ge(dif_max, 2 * (i - 1))
                    if i < 2:
                        pe.wait_ge(ret_a, H)
                        pe.wait_ge(ret_kd, H)
                    for m in range(2):
                        at = slice(m * DIFF_D, (m + 1) * DIFF_D)
                        pe.matmul(bank(2 * (i % 2) + m)[:, 0:(q + 1) * P], dqT[at, h, q * P:(q + 1) * P], dkT[at, h, 0:(q + 1) * P],
                                  start=True, stop=True).then_inc(dif_scores, 1)
                if 1 <= i <= H * NT:
                    n = i - 1
                    q = n % NT
                    pe.wait_ge(dif_probs, n + 1)
                    pe.wait_ge(ret_state, H)
                    pe.wait_ge(ret_y, H)
                    if n >= 2:
                        pe.wait_ge(dif_out, n - 1)
                    for k in range(q + 1):
                        mm = pe.transpose(bank(4 + n % 2)[:, k * P:(k + 1) * P], dif[:, n % 2, 0, k * P:(k + 1) * P], ident)
                    mm.then_inc(dif_turned, 1)
                if i >= 2:
                    n = i - 2
                    h, q = divmod(n, NT)
                    pe.wait_ge(dif_out, n + 1)
                    if n >= 2:
                        pe.wait_ge(dif_y, n - 1)
                    for k in range(q + 1):
                        mm = pe.matmul(bank(6 + n % 2)[:, 0:DV], difT[:, n % 2, k * P:(k + 1) * P], dv2[:, k, h, :], start=k == 0, stop=k == q)
                    mm.then_inc(dif_pv, 1)

            pe.wait_ge(y2_ready, 2 * NT * H)
            turn_features("out2", y2)
            pe.wait_ge(turned_lo, TURN_LO["out2"] + KD)
            for c in range(2):
                linear_chunk(S_OUT2 + c, MM["out2"] + 4 * c, False, y2T_hi, y2T_lo)

            pe.wait_ge(keys_in, 16)
            for b in range(4):
                if b >= 2:
                    pe.wait_ge(keys_out, b - 1)
                for i in range(4):
                    mm = pe.transpose(bank(4 + b % 2)[:, i * P:(i + 1) * P], keys[:, 4 * b + i, :], ident)
                mm.then_inc(keys_turned, 1)

            pe.wait_ge(xn_done, 4 * NT)
            turn_features("peer", xn)
            pe.wait_ge(turned_lo, TURN_LO["peer"] + KD)
            for n in range(17):
                if n < 16:
                    s = S_WQ + n // 4
                    if n % 4 == 0:
                        pe.wait_ge(w_hi, s + 1)
                        pe.wait_ge(w_lo, s + 1)
                    wh, wl = high(s % 2, KD), low(s % 2, KD)
                    at = slice((n % 4) * P, (n % 4 + 1) * P)
                    pe.wait_ge(mm_out, MM["wq"] + n - 1)
                    three_pass(bank(2 + n % 2), lambda k: wh[:, k, at], lambda k: wl[:, k, at],
                               lambda k: xT_hi[:, k, :], lambda k: xT_lo[:, k, :], KD).then_inc(mm_done, 1)
                if n >= 1:
                    m = n - 1
                    pe.wait_ge(mm_out, MM["wq"] + m + 1)
                    if m == 0:
                        pe.wait_ge(keys_out, 4)
                    if m >= 2:
                        pe.wait_ge(key_tops, m - 1)
                    for t in range(NT):
                        mm = pe.matmul(bank(4 + m % 2)[:, t * P:(t + 1) * P], half_q[:, m % 2, t * P:(t + 1) * P], keysT[:, m, :],
                                       start=True, stop=True)
                    mm.then_inc(key_scores, 1)
                if n % 4 == 3:
                    pe.wait_ge(mm_done, MM["wq"] + n + 1)
                    pe.sem_inc(w_used, 1)

            for i, src in enumerate((pick_g, pick_1, pick_2)):
                pe.wait_ge(picks_ready, i + 1)
                for t in range(NT):
                    mm = pe.transpose(bank((6, 7, 4)[i])[:, t * P:(t + 1) * P], src[:, t, :], ident)
                mm.then_inc(picks_turned, 1)

            pe.sem_inc(gate_mm, 2)
            with pe.Fori(0, NT) as i:
                for k in range(32):
                    pe.wait_ge(hot_ready, i * 256 + 8 * (k + 1))
                    pe.wait_ge(gate_out, i * 32 + (k + 1))
                    for t in range(4):
                        mm = pe.matmul(bank(k % 2)[:, t * P:(t + 1) * P], hot[:, k % 2, t, 0, :], hot[:, k % 2, t, 1, :], start=True, stop=True)
                    mm.then_inc(gate_mm, 1)

            def u_turn(g, j, slot):
                u = ring[:, slot, j * D:(j + 1) * D].rearrange("p (c k) -> p c k", k=KD)
                for b in range(2):
                    if j >= 2:
                        pe.wait_ge(u_lo, 8 * g + 2 * (j - 2) + b + 1)
                    else:
                        pe.wait_ge(u_lo, 8 * g + (0 if isinstance(g, int) and g == 0 else 2 * (j - 2) + b + 1))
                    for k in range(4):
                        mm = pe.transpose(bank((0, 6)[j % 2] + b)[:, k * P:(k + 1) * P], u[:, :, 4 * b + k], ident)
                    mm.then_inc(u_turned, 1)

            def expert_up(g, slot):
                for j in range(4):
                    if j < 3:
                        u_turn(g, j + 1, slot)
                    pe.wait_ge(u_lo, 8 * g + (2 * j + 2))
                    pe.wait_ge(ex_gelu, 4 * g + max(j - 1, 0))
                    three_pass(bank(2 + j % 2), lambda k: uT_hi[:, j % 2, k, :], lambda k: uT_lo[:, j % 2, k, :],
                               lambda k: xT_hi[:, k, :], lambda k: xT_lo[:, k, :], KD).then_inc(ex_a, 1)

            def expert_down(g, par, s2):
                pe.wait_ge(w_hi, g + (S_EX + 1))
                pe.wait_ge(w_lo, g + (S_EX + 1))
                pe.wait_ge(ex_lo_done, 4 * g + 4)
                wh, wl = high(s2, 4), low(s2, 4)
                for b in range(8):
                    t, c = divmod(b, 2)
                    rows_, cols = slice(t * P, (t + 1) * P), slice(c * 512, (c + 1) * 512)
                    pe.wait_ge(ex_add, 8 * g + (b + 1))
                    three_pass(bank(4 + b % 2), lambda j: ex_hi[:, par, j, rows_], lambda j: ex_lo[:, par, j, rows_],
                               lambda j: wh[:, j, cols], lambda j: wl[:, j, cols], 4).then_inc(ex_b, 1)
                pe.wait_ge(ex_b, 8 * g + 8)
                pe.sem_inc(w_used, 1)

            pe.wait_ge(gate_out, 32 * NT + 2)
            pe.wait_ge(ring_in[0], arrived(0, 9))
            u_turn(0, 0, 0)
            expert_up(0, 0)
            pe.wait_ge(ring_in[1], arrived(1, 9))
            u_turn(1, 0, 1)
            with pe.Fori(0, 15) as i:
                expert_up(2 * i + 1, 1)
                pe.wait_ge(ring_in[3], arrived(3, 9) + i * 16)
                u_turn(2 * i + 2, 0, 3)
                expert_down(2 * i, 0, 1)
                expert_up(2 * i + 2, 3)
                pe.wait_ge(ring_in[1], arrived(1, 10) + i * 16)
                u_turn(2 * i + 3, 0, 1)
                expert_down(2 * i + 1, 1, 0)
            expert_up(31, 1)
            expert_down(30, 0, 1)
            expert_down(31, 1, 0)

        @block.vector
        def _(dve):
            own = Steps(dve, own_v)
            dve.wait_ge(rstd_done, 1)
            for t in range(NT):
                dve.tensor_scalar(xn1[:, t, :], x_sb[:, t, :], rstd[:, t:t + 1], None, ALU.mult).then_inc(xn_done, 1)

            for n in range(16):
                c, r = divmod(n, 4)
                dve.wait_ge(mm_done, n + 1)
                dst = (conv_in[:, r, 2:T + 2], v1[:, r, :], o1[:, r, :], tail[:, r, :])[c]
                dve.tensor_copy(dst, bank(2 + n % 2)[:, 0:(CW if c < 3 else TAIL)]).then_inc(mm_out, 1)

            dve.wait_ge(conv_turned, 1)
            own.did(dve.tensor_copy(conv_w[:, :, 0:6], bank(4)[:, 0:32].rearrange("p (f t) -> p f t", f=4)[:, :, 0:6]))
            own.wait()
            dve.wait_ge(mm_out, 4)
            for f in range(4):
                own.did(dve.tensor_scalar(qkT[:, f, :], conv_in[:, f, 0:T], conv_w[:, f, 0:1], conv_w[:, f, 5:6], ALU.mult, ALU.add))
                for i in range(1, TAPS):
                    own.wait()
                    step = dve.scalar_tensor_tensor(qkT[:, f, :], conv_in[:, f, i:i + T], conv_w[:, f, i:i + 1], qkT[:, f, :], ALU.mult, ALU.add)
                    if i < TAPS - 1:
                        own.did(step)
                    else:
                        step.then_inc(conv_done, 1)

            dve.wait_ge(mm_out, 16)
            for d in range(2):
                for kind in range(2):
                    at = (2 * d + kind) * H
                    dve.tensor_tensor(gate_pad[:, :, kind, 32 * d:32 * d + H], tail[:, :, at:at + H],
                                      gate_bias[:, at:at + H].unsqueeze(1).to_broadcast([P, NT, H]), ALU.add).then_inc(gates_padded, 1)
            R = slice(0, ROWS)
            DIR = (slice(0, H), slice(32, 32 + H))
            dve.wait_ge(gates_turned, 2)
            own.did(dve.tensor_copy(lf_row[R, :], bank(6)[R, :]))
            own.wait()
            dve.scalar_tensor_tensor(u_row[R, :], lf_row[R, :], -1.0, lf_row[R, :], ALU.mult, ALU.min).then_inc(f_neg, 1)
            dve.wait_ge(f_log, 1)
            own.did(dve.scalar_tensor_tensor(lf_row[R, :], lf_row[R, :], 0.0, t_row[R, :], ALU.min, ALU.subtract))
            own.wait()
            own.did(dve.memset(b_row[R, :], 0.0))
            own.wait()
            for d in range(2):
                for c in range(NC):
                    s = slice(c * P, (c + 1) * P)
                    rev = (lambda a: a) if d == 0 else (lambda a: a[:, ::-1])
                    own.did(dve.tensor_tensor_scan(rev(b_row[DIR[d], s]), ones[DIR[d], :], rev(lf_row[DIR[d], s]), 0.0, ALU.mult, ALU.add))
            own.wait()
            own.did(dve.tensor_tensor(c_row[R, :], bank(5)[R, :], b_row[R, :], ALU.subtract))
            own.did(dve.memset(m_row[R, :], 0.0))
            own.wait()
            for i in range(NC):
                for d in range(2):
                    c = i if d == 0 else NC - 1 - i
                    s = slice(c * P, (c + 1) * P)
                    rev = (lambda a: a) if d == 0 else (lambda a: a[:, ::-1])
                    own.did(dve.tensor_tensor_scan(rev(m_row[DIR[d], s]), rev(c_row[DIR[d], s]), rev(c_row[DIR[d], s]),
                                                   prev_max[DIR[d], c:c + 1], ALU.max, ALU.max))
                own.wait()
                if i < NC - 1:
                    for d in range(2):
                        c = i if d == 0 else NC - 1 - i
                        last = c * P + (P - 1 if d == 0 else 0)
                        nxt = c + 1 if d == 0 else c - 1
                        own.did(dve.tensor_tensor(prev_max[DIR[d], nxt:nxt + 1], b_row[DIR[d], last:last + 1], m_row[DIR[d], last:last + 1], ALU.add))
                    own.wait()
            dve.tensor_scalar(negm_row[R, :], m_row[R, :], -1.0, None, ALU.mult).then_inc(rows_ready, 1)
            for c in range(NC):
                s = slice(c * P, (c + 1) * P)
                step = dve.tensor_scalar(inter_row[R, s], m_row[R, s], -1.0, prev_max[R, c:c + 1], ALU.mult, ALU.add)
                if c < NC - 1:
                    own.did(step)
                else:
                    step.then_inc(rows_ready, 1)
            dve.wait_ge(rows_ready, 1)
            dve.tensor_tensor(em_row[R, :], negm_row[R, :], b_row[R, :], ALU.subtract).then_inc(rows_ready, 1)
            own.did(dve.memset(w_row[R, :], 0.0))
            own.wait()
            for d in range(2):
                for c in range(NC):
                    s = slice(c * P, (c + 1) * P)
                    last = c * P + (P - 1 if d == 0 else 0)
                    step = dve.tensor_scalar(w_row[DIR[d], s], c_row[DIR[d], s], m_row[DIR[d], last:last + 1], None, ALU.subtract)
                    if (d, c) != (1, NC - 1):
                        own.did(step)
                    else:
                        step.then_inc(rows_ready, 1)
            dve.wait_ge(rows_exp, 1)
            own.did(dve.tensor_copy(dec_rows[DIR[0], :], inter_row[DIR[0], P - 1:T:P]))
            dve.tensor_copy(dec_rows[DIR[1], :], inter_row[DIR[1], 0:T:P]).then_inc(rows_ready, 1)
            dve.wait_ge(cols_turned, 5)
            w = NC * ROWS
            dve.tensor_copy(gate_cols[:, 0, :, :], bank(4)[:, 0:w].rearrange("p (c r) -> p c r", c=NC)).then_inc(cols_done, 1)
            dve.tensor_scalar(gate_cols[:, 1, :, :], bank(4)[:, w:2 * w].rearrange("p (c r) -> p c r", c=NC), DQK ** -0.5, None, ALU.mult).then_inc(cols_done, 1)
            dve.tensor_copy(gate_cols[:, 2:4, :, :], bank(5)[:, 0:2 * w].rearrange("p (a c r) -> p a c r", a=2, c=NC)).then_inc(cols_done, 1)
            dve.tensor_copy(dec_cols, bank(6)[:, 0:32].rearrange("p (a b) -> p a b", a=8)).then_inc(cols_done, 1)
            dve.wait_ge(cols_done, 4)
            dve.wait_ge(ktok_done, 2)

            for h in range(H):
                at = (h % 2) * DQK
                dirs = (h, 32 + h)
                if h >= 1:
                    dve.wait_ge(kv_done, h)
                for d in range(2):
                    for i in range(3):
                        step = dve.tensor_scalar(k_dec[:, d, i, :], k_tok[:, i + d, h * DQK:(h + 1) * DQK],
                                                 gate_cols[:, 3, i + d, dirs[d]:dirs[d] + 1], None, ALU.mult)
                step.then_inc(kdec_done, 1)
                dve.wait_ge(scores_done, h + 1)
                for d in range(2):
                    for c in range(NC):
                        step = dve.scalar_tensor_tensor(decay[:, h % 2, d, c * P:(c + 1) * P], bank(2 + d)[:, c * P:(c + 1) * P],
                                                        gate_cols[:, 0, c, dirs[d]:dirs[d] + 1], mask[d], ALU.add, ALU.add)
                step.then_inc(decay_in, 1)
                dve.wait_ge(kv_done, h + 1)
                if h >= 1:
                    dve.wait_ge(inter_done, h)
                for i in range(3):
                    for d in range(2):
                        j = i if d == 0 else 2 - i
                        src = bank(6 + d)[at:at + DQK, j * 129:(j + 1) * 129]
                        dst = state[at:at + DQK, d, j, 0:129]
                        if i == 0:
                            step = dve.tensor_copy(dst, src)
                        else:
                            before = j - 1 if d == 0 else j + 1
                            chunk = j if d == 0 else j + 1
                            step = dve.scalar_tensor_tensor(dst, state[at:at + DQK, d, before, 0:129],
                                                            dec_cols[at:at + DQK, d * H + h, chunk:chunk + 1], src, ALU.mult, ALU.add)
                        if (i, d) == (2, 1):
                            step.then_inc(state_done, 1)
                        else:
                            own.did(step)
                    if i < 2:
                        own.wait()
                dve.wait_ge(decay_exp, h + 1)
                for d in range(2):
                    dve.scalar_tensor_tensor(probs[:, h % 2, d, :, :].rearrange("p c t -> p (c t)"), bank(0), DQK ** -0.5, decay[:, h % 2, d, :],
                                             ALU.mult, ALU.mult).then_inc(probs_done, 1)
                dve.wait_ge(num_out, 2 * h + 2)
                dve.wait_ge(num_done, h + 1)
                own.did(dve.tensor_copy(den, bank(1)[:, 0:8].rearrange("p (a b) -> p a b", a=2)))
                dve.wait_ge(inter_done, h + 1)
                for d in range(2):
                    first = 1 - d
                    inter = bank(2 + d)[:, 0:387].rearrange("p (i v) -> p i v", i=3)
                    col = gate_cols[:, 1, :, dirs[d]]
                    own.did(dve.tensor_tensor(den_t[:, d, first:first + 3], inter[:, :, P], col[:, first:first + 3], ALU.mult))
                    for i in range(3):
                        c = i + first
                        own.did(dve.scalar_tensor_tensor(num[:, d, c, :], inter[:, i, 0:P], gate_cols[:, 1, c, dirs[d]:dirs[d] + 1],
                                                         num[:, d, c, :], ALU.mult, ALU.add))
                own.wait()
                for d in range(2):
                    first = 1 - d
                    own.did(dve.tensor_tensor(den[:, d, first:first + 3], den[:, d, first:first + 3], den_t[:, d, first:first + 3], ALU.add))
                own.wait()
                own.did(dve.scalar_tensor_tensor(den_t, den, -1.0, den, ALU.mult, ALU.max))
                own.wait()
                for d in range(2):
                    own.did(dve.tensor_tensor(den_t[:, d, :], den_t[:, d, :], gate_cols[:, 2, :, dirs[d]], ALU.max))
                own.wait()
                own.did(dve.reciprocal(den_r, den_t))
                own.wait()
                for c in range(NC):
                    own.did(dve.tensor_scalar(y1[:, c, h * DV:(h + 1) * DV], num[:, 0, c, :], den_r[:, 0, c:c + 1], None, ALU.mult))
                own.wait()
                for c in range(NC):
                    step = dve.scalar_tensor_tensor(y1[:, c, h * DV:(h + 1) * DV], num[:, 1, c, :], den_r[:, 1, c:c + 1],
                                                    y1[:, c, h * DV:(h + 1) * DV], ALU.mult, ALU.add)
                step.then_inc(head_out, 1)
            dve.wait_ge(rstd_done, 2)
            dve.wait_ge(o_sig, 1)
            for t in range(NT):
                for h in range(H):
                    v = slice(h * DV, (h + 1) * DV)
                    dve.scalar_tensor_tensor(y1[:, t, v], y1[:, t, v], rstd[:, t * H + h:t * H + h + 1], o1[:, t, v],
                                             ALU.mult, ALU.mult).then_inc(y_ready, 1)

            dve.wait_ge(rstd_done, 3)
            for t in range(NT):
                dve.tensor_scalar(tail[:, t, C_CQ:C_CKV], tail[:, t, C_CQ:C_CKV], rstd[:, 16 + t:17 + t], None, ALU.mult).then_inc(latent_done, 1)
                dve.tensor_scalar(tail[:, t, C_CKV:C_KPE], tail[:, t, C_CKV:C_KPE], rstd[:, 20 + t:21 + t], None, ALU.mult).then_inc(latent_done, 1)

            dve.wait_ge(small_in, 16 * SMALLS)
            dve.tensor_copy(pos_f[0:NT, :], pos_rows[0:NT, :].bitcast(I32)).then_inc(pos_turned, 1)
            dve.wait_ge(pos_turned, 2)
            own.did(dve.tensor_copy(pos, bank(6)[:, 0:NT]))
            own.wait()
            for t in range(NT):
                own.did(dve.tensor_scalar(angle[:, t, :], const("inv_freq"), pos[:, t:t + 1], None, ALU.mult))
            own.wait()
            own.did(dve.tensor_scalar(turns, angle, float(1.0 / (2.0 * np.pi)), ROUND, ALU.mult, ALU.add))
            own.wait()
            own.did(dve.tensor_scalar(turns, turns, ROUND, None, ALU.subtract))
            for c in (TWO_PI_A, TWO_PI_B, TWO_PI_C):
                own.wait()
                own.did(dve.scalar_tensor_tensor(angle, turns, -c, angle, ALU.mult, ALU.add))
            own.wait()
            own.did(dve.tensor_scalar(angle_c, angle, float(np.pi / 2), None, ALU.add))
            own.wait()
            own.did(dve.tensor_scalar(turns, angle_c, float(np.pi), None, ALU.is_gt))
            own.wait()
            own.did(dve.scalar_tensor_tensor(angle_c, turns, float(-2.0 * np.pi), angle_c, ALU.mult, ALU.add))
            own.wait()
            PI_IN = 3.1415925
            dve.tensor_scalar(angle, angle, PI_IN, -PI_IN, ALU.min, ALU.max).then_inc(angles, 1)
            dve.tensor_scalar(angle_c, angle_c, PI_IN, -PI_IN, ALU.min, ALU.max).then_inc(angles, 1)

            for t in range(NT):
                qk = qk_tok[:, t % 2, :, :]
                q_flat = qk[:, 0:H, :].rearrange("p h n -> p (h n)")
                dve.wait_ge(proj_done, t + 1)
                if t >= 2:
                    dve.wait_ge(qk_turned, t - 1)
                own.did(dve.tensor_copy(q_flat[:, 0:512], bank(2)))
                own.did(dve.tensor_copy(q_flat[:, 512:768], bank(3)[:, 0:256]))
                own.did(dve.tensor_copy(qk[:, H:H + 2, 0:A_NOPE], bank(4).rearrange("p (h n) -> p h n", h=2)[:, :, 0:A_NOPE]))
                dve.tensor_copy(qk[:, H + 2:2 * H, 0:A_NOPE], bank(5).rearrange("p (h n) -> p h n", h=2)[:, :, 0:A_NOPE]).then_inc(qk_put, 1)
                dve.wait_ge(qk_squared, t + 1)
                dve.tensor_reduce(qk_sumsq[:, t, :], qk_sq, AX.X, ALU.add).then_inc(qk_summed, 1)
                dve.wait_ge(qk_rstd_done, t + 1)
                own.did(dve.tensor_tensor(qk, qk, qk_rstd[:, t, :].unsqueeze(2).to_broadcast([P, 2 * H, A_DH]), ALU.mult))
                own.wait()
                r4 = qk.rearrange("p (a h) n -> p a h n", a=2)[:, :, :, A_NOPE:]
                own.did(dve.tensor_tensor(r4, r4, rope_gain.unsqueeze(2).to_broadcast([P, 2, H, A_ROPE]), ALU.mult))
                own.wait()
                if t == 0:
                    dve.wait_ge(rotary, 2)
                if t >= 1:
                    dve.wait_ge(qk_turned, t)
                half = A_ROPE // 2
                cs = cos_t[:, t, :].unsqueeze(1).to_broadcast([P, 2 * H, half])
                sn = sin_t[:, t, :].unsqueeze(1).to_broadcast([P, 2 * H, half])
                x1, x2 = qk[:, :, A_NOPE:A_NOPE + half], qk[:, :, A_NOPE + half:]
                own.did(dve.tensor_tensor(rot[:, :, 0:half], x1, cs, ALU.mult))
                own.did(dve.tensor_tensor(rot_t, x2, sn, ALU.mult))
                own.did(dve.tensor_tensor(rot[:, :, half:], x2, cs, ALU.mult))
                own.wait()
                own.did(dve.tensor_tensor(rot[:, :, 0:half], rot[:, :, 0:half], rot_t, ALU.subtract))
                own.wait()
                own.did(dve.tensor_tensor(rot_t, x1, sn, ALU.mult))
                own.wait()
                dve.tensor_tensor(rot[:, :, half:], rot[:, :, half:], rot_t, ALU.add).then_inc(qk_rotated, 1)
                dve.wait_ge(qk_turned, t + 1)
                for b in range(2):
                    dve.tensor_copy(ropeT[0:A_ROPE, b * H:(b + 1) * H, t * P:(t + 1) * P],
                                    bank(6 + b)[0:A_ROPE, :].rearrange("p (h n) -> p h n", h=H)).then_inc(rope_out, 1)

            for i in range(H * NT + 2):
                if i < H * NT:
                    dve.wait_ge(att_scores, i + 1)
                    own.did(dve.tensor_reduce(row_max[:, i:i + 1], bank(2 + i % 2), AX.X, ALU.max))
                    own.wait()
                    dve.tensor_scalar(row_nmax[:, i:i + 1], row_max[:, i:i + 1], -(A_DH ** -0.5), None, ALU.mult).then_inc(att_max, 1)
                if 1 <= i <= H * NT:
                    n = i - 1
                    dve.wait_ge(att_turned, n + 1)
                    if n >= 2:
                        dve.wait_ge(att_pv, n - 1)
                    dve.tensor_copy(attT[:, n % 2, :], bank(4 + n % 2)).then_inc(att_out, 1)
                if i >= 2:
                    n = i - 2
                    h, q = divmod(n, NT)
                    own.did(dve.reciprocal(row_inv[:, n:n + 1], row_sum[:, n:n + 1]))
                    dve.wait_ge(att_pv, n + 1)
                    own.wait()
                    dve.tensor_scalar(y1[:, q, 512 + h * DV:512 + (h + 1) * DV], bank(6 + n % 2)[:, 0:DV],
                                      row_inv[:, n:n + 1], None, ALU.mult).then_inc(att_norm, 1)

            def turned_low(stage, gain, hi=xT_hi, lo=xT_lo):
                for k in range(KD):
                    dve.wait_ge(turned_hi, TURN[stage] + k + 1)
                    dve.scalar_tensor_tensor(lo[:, k, :], bank(k % 2), gains[:, gain + k:gain + k + 1], hi[:, k, :],
                                             ALU.mult, ALU.subtract).then_inc(turned_lo, 1)

            def add_linear(done_before):
                for n in range(8):
                    c, t = divmod(n, NT)
                    dve.wait_ge(mm_done, done_before + n + 1)
                    dst = x_sb[:, t, c * CW:(c + 1) * CW]
                    dve.tensor_tensor(dst, bank(2 + (done_before + n) % 2), dst, ALU.add).then_inc(mm_out, 1)

            def norm_rows(rstd_count):
                dve.wait_ge(rstd_done, rstd_count)
                for t in range(NT):
                    dve.tensor_scalar(xn[:, t, :], x_sb[:, t, :], rstd[:, t:t + 1], None, ALU.mult).then_inc(xn_done, 1)

            turned_low("out", G_Y1)
            add_linear(MM["out"])
            norm_rows(4)
            turned_low("ffn", G_FFN)

            def ff_square(g, par):
                for j in range(4):
                    dve.wait_ge(ff_a, 4 * g + j + 1)
                    dve.tensor_scalar(relu[:, j % 2, :], bank(2 + j % 2), 0.0, None, ALU.max).then_inc(ff_relu, 1)
                    dve.wait_ge(ff_relu, 4 * g + j + 1)
                    dve.tensor_tensor(hid[:, j % 2, :], relu[:, j % 2, :], relu[:, j % 2, :], ALU.mult).then_inc(ff_sq, 1)
                    dve.wait_ge(ff_sq, 4 * g + j + 1)
                    dve.wait_ge(ff_hi, 4 * g + j + 1)
                    dve.tensor_tensor(hid_lo[:, par, j, :], hid[:, j % 2, :], hid_hi[:, par, j, :], ALU.subtract).then_inc(ff_lo, 1)

            def ff_accumulate(g):
                for b in range(8):
                    t, c = divmod(b, 2)
                    dve.wait_ge(ff_b, 8 * g + b + 1)
                    dst = x_sb[:, t, c * 512:(c + 1) * 512]
                    dve.tensor_tensor(dst, bank(4 + b % 2), dst, ALU.add).then_inc(ff_add, 1)

            dve.sem_inc(ff_add, 2)
            ff_square(0, 0)
            with dve.Fori(0, 3) as i:
                ff_square(2 * i + 1, 1)
                ff_accumulate(2 * i)
                ff_square(2 * i + 2, 0)
                ff_accumulate(2 * i + 1)
            ff_square(7, 1)
            ff_accumulate(6)
            ff_accumulate(7)

            own.did(dve.tensor_scalar(gains[64:P, G_Y2:G_Y2 + KD], gains[64:P, G_Y2:G_Y2 + KD], 1.0 - LAMBDA_INIT, None, ALU.mult))
            own.wait()
            norm_rows(5)
            turned_low("mix2", G_MIX2)
            for n in range(28):
                c, r = divmod(n, 4)
                dve.wait_ge(mm_done, MM["in2"] + n + 1)
                src = bank(2 + n % 2)
                dst = (rqT[:, r, :], rkT[:, r, :], rv[:, r, :], rg[:, r, :], dqT[:, r, :], dkT[:, r, :],
                       dv2[:, r, :, :].rearrange("p h v -> p (h v)"))[c]
                if c == 4:
                    step = dve.tensor_scalar(dst, src, DIFF_D ** -0.5, None, ALU.mult)
                else:
                    step = dve.tensor_copy(dst, src)
                step.then_inc(mm_out, 1)

            intra = const("intra", h=H, i=P)
            for h in range(H):
                dve.wait_ge(ret_scores, h + 1)
                if h >= 2:
                    dve.wait_ge(ret_o, h - 1)
                dve.tensor_tensor(ret_in[:, h % 2, :, :], bank(0).rearrange("p (c i) -> p c i", c=NC),
                                  intra[:, h, :].unsqueeze(1).to_broadcast([P, NC, P]), ALU.mult).then_inc(ret_a, 1)
                dve.wait_ge(ret_kv, h + 1)
                if h >= 1:
                    dve.wait_ge(ret_o, h)
                own.did(dve.tensor_copy(ret_s[:, 0, :], bank(4)[:, 0:P]))
                own.wait()
                own.did(dve.scalar_tensor_tensor(ret_s[:, 1, :], ret_s[:, 0, :], CDEC[h], bank(4)[:, P:2 * P], ALU.mult, ALU.add))
                own.wait()
                dve.scalar_tensor_tensor(ret_s[:, 2, :], ret_s[:, 1, :], CDEC[h], bank(4)[:, 2 * P:3 * P], ALU.mult, ALU.add).then_inc(ret_state, 1)
                dve.wait_ge(ret_o, h + 1)
                dve.tensor_copy(y2[:, :, h * DV:(h + 1) * DV], bank(5).rearrange("p (t v) -> p t v", t=NT)).then_inc(ret_y, 1)

            own.did(dve.tensor_tensor(lam_t, lam_in[:, 0:4:2, :], lam_in[:, 1:4:2, :], ALU.mult))
            own.wait()
            dve.tensor_reduce(lam[:, 0:2], lam_t, AX.X, ALU.add).then_inc(lam_sums, 1)
            dve.wait_ge(lam_exp, 1)
            own.did(dve.tensor_tensor(lam[:, 4:5], lam[:, 3:4], lam[:, 2:3], ALU.subtract))
            own.wait()
            own.did(dve.tensor_scalar(lam[:, 5:6], lam[:, 4:5], -LAMBDA_INIT, None, ALU.add))

            negdist = const("negdist")
            for i in range(H * NT + 3):
                if i < H * NT:
                    h, q = divmod(i, NT)
                    n_keys = (q + 1) * P
                    if i >= 2:
                        dve.wait_ge(dif_turned, i - 1)
                    for m in range(2):
                        dve.wait_ge(dif_scores, 2 * i + m + 1)
                        own.did(dve.scalar_tensor_tensor(dif[:, i % 2, m, 0:n_keys], negdist[:, T - n_keys:T], SLOPES[h],
                                                         bank(2 * (i % 2) + m)[:, 0:n_keys], ALU.mult, ALU.add))
                    own.wait()
                    for m in range(2):
                        own.did(dve.tensor_reduce(row_max[:, 2 * i + m:2 * i + m + 1], dif[:, i % 2, m, 0:n_keys], AX.X, ALU.max))
                    own.wait()
                    for m in range(2):
                        dve.tensor_scalar(row_nmax[:, 2 * i + m:2 * i + m + 1], row_max[:, 2 * i + m:2 * i + m + 1], -1.0, None, ALU.mult).then_inc(dif_max, 1)
                if 1 <= i <= H * NT:
                    n = i - 1
                    n_keys = (n % NT + 1) * P
                    dve.wait_ge(dif_exp, 2 * n + 2)
                    own.did(dve.reciprocal(row_inv[:, 2 * n:2 * n + 2], row_sum[:, 2 * n:2 * n + 2]))
                    own.wait()
                    own.did(dve.tensor_tensor(row_inv[:, 2 * n + 1:2 * n + 2], row_inv[:, 2 * n + 1:2 * n + 2], lam[:, 5:6], ALU.mult))
                    own.did(dve.tensor_scalar(dif[:, n % 2, 0, 0:n_keys], dif[:, n % 2, 0, 0:n_keys], row_inv[:, 2 * n:2 * n + 1], None, ALU.mult))
                    own.wait()
                    dve.scalar_tensor_tensor(dif[:, n % 2, 0, 0:n_keys], dif[:, n % 2, 1, 0:n_keys], row_inv[:, 2 * n + 1:2 * n + 2],
                                             dif[:, n % 2, 0, 0:n_keys], ALU.mult, ALU.add).then_inc(dif_probs, 1)
                if 2 <= i <= H * NT + 1:
                    n = i - 2
                    n_keys = (n % NT + 1) * P
                    dve.wait_ge(dif_turned, n + 1)
                    if n >= 2:
                        dve.wait_ge(dif_pv, n - 1)
                    dve.tensor_copy(difT[:, n % 2, 0:n_keys], bank(4 + n % 2)[:, 0:n_keys]).then_inc(dif_out, 1)
                if i >= 3:
                    n = i - 3
                    h, q = divmod(n, NT)
                    dve.wait_ge(dif_pv, n + 1)
                    dve.tensor_copy(y2[:, q, 512 + h * DV:512 + (h + 1) * DV], bank(6 + n % 2)[:, 0:DV]).then_inc(dif_y, 1)
                if i == 2:
                    dve.wait_ge(rstd_done, 6)
                    dve.wait_ge(rg_silu, 1)
                    for t in range(NT):
                        for h in range(H):
                            v = slice(h * DV, (h + 1) * DV)
                            dve.scalar_tensor_tensor(y2[:, t, v], y2[:, t, v], rstd[:, t * H + h:t * H + h + 1], rg[:, t, v],
                                                     ALU.mult, ALU.mult).then_inc(y2_ready, 1)
            dve.wait_ge(rstd_done, 7)
            for t in range(NT):
                for h in range(H):
                    v = slice(512 + h * DV, 512 + (h + 1) * DV)
                    dve.tensor_scalar(y2[:, t, v], y2[:, t, v], rstd[:, 16 + t * H + h:17 + t * H + h], None, ALU.mult).then_inc(y2_ready, 1)
            turned_low("out2", G_Y2, y2T_hi, y2T_lo)
            add_linear(MM["out2"])

            norm_rows(8)
            turned_low("peer", G_FFN2)

            def top16(values, best, index, rest, groups, wait_for, signal, in_place):
                dve.wait_ge(*wait_for)
                for g in range(groups):
                    own.did(dve.max(best(g)[:, 0:8], values(g)))
                own.wait()
                for g in range(groups):
                    own.did(dve.max_index(index(g)[:, 0:8], best(g)[:, 0:8], values(g)))
                    own.did(dve.match_replace(rest(g), best(g)[:, 0:8], values(g), -3e38))
                own.wait()
                for g in range(groups):
                    own.did(dve.max(best(g)[:, 8:16], rest(g)))
                own.wait()
                for g in range(groups):
                    step = dve.max_index(index(g)[:, 8:16], best(g)[:, 8:16], rest(g))
                step.then_inc(signal, 1)

            for n in range(2 * P_HEADS):
                if n >= 1:
                    dve.wait_ge(key_tops, n)
                top16(lambda t: bank(4 + n % 2)[:, t * P:(t + 1) * P], lambda t: top_v[:, t, n, :], lambda t: top_i[:, t, n, :],
                      lambda t: masked[:, t, 0:P], NT, (key_scores, n + 1), key_tops, False)
            dve.wait_ge(key_tops, 2 * P_HEADS)
            own.did(dve.tensor_copy(top_f, top_i))
            for t in range(NT):
                for half in range(2):
                    g0 = 4 * half
                    if t or half:
                        dve.wait_ge(picks_top, 2 * t + half)
                    top16(lambda g: cand[:, t % 2, g0 + g, :, :].rearrange("p a b -> p (a b)"), lambda g: pick_v[:, t, g0 + g, :],
                          lambda g: pick_i[:, t, g0 + g, :], lambda g: masked[:, g, :], 4, (cands, t + 1), picks_top, False)
            dve.wait_ge(picks_top, 2 * NT)
            own.did(dve.tensor_scalar(half_i, pick_i, 4, None, ALU.logical_shift_right))
            own.wait()
            own.did(dve.tensor_copy(half_f[:, 0, :, :, :], half_i))
            own.wait()
            own.did(dve.tensor_scalar(half_i, pick_i, 15, None, ALU.bitwise_and))
            own.wait()
            dve.tensor_copy(half_f[:, 1, :, :, :], half_i).then_inc(places, 1)
            dve.tensor_tensor(pick_g.rearrange("p t (h k) -> p t h k", h=P_HEADS), pick_v,
                              pick_v[:, :, :, 0:1].to_broadcast([P, NT, P_HEADS, TOPK]), ALU.subtract).then_inc(gate_in, 1)
            dve.wait_ge(places, 1)

            def first_keys(t):
                four = [P, P_HEADS, TOPK, TOPK]
                iota16 = iota[:, 0:TOPK].unsqueeze(1).unsqueeze(1).to_broadcast(four)
                if t >= 1:
                    dve.wait_ge(match_used, t)
                dve.tensor_tensor(match1, half_f[:, 1, t, :, :].unsqueeze(3).to_broadcast(four), iota16, ALU.is_equal).then_inc(match_eq, 1)
                own.did(dve.tensor_tensor(match0, half_f[:, 0, t, :, :].unsqueeze(3).to_broadcast(four), iota16, ALU.is_equal))
                own.wait()
                own.did(dve.tensor_tensor(match0, match0, top_f[:, t, 0::2, :].unsqueeze(2).to_broadcast(four), ALU.mult))
                own.wait()
                return dve.tensor_reduce(pick_1[:, t, :].rearrange("p (h k) -> p h k", h=P_HEADS), match0, AX.X, ALU.add)

            def second_keys(t):
                dve.wait_ge(match_p, t + 1)
                return dve.tensor_reduce(pick_2[:, t, :].rearrange("p (h k) -> p h k", h=P_HEADS), match1, AX.X, ALU.add)

            dve.wait_ge(gate_exp, 1)
            gate_rows = pick_g.rearrange("p t (h k) -> p (t h) k", h=P_HEADS)
            own.did(dve.tensor_reduce(gate_sum, gate_rows, AX.X, ALU.add))
            own.wait()
            own.did(dve.reciprocal(gate_inv, gate_sum))
            own.wait()
            dve.tensor_tensor(gate_rows, gate_rows, gate_inv.unsqueeze(2).to_broadcast([P, NT * P_HEADS, TOPK]), ALU.mult).then_inc(picks_ready, 1)
            for t in range(NT):
                step = first_keys(t)
                if t < NT - 1:
                    own.did(step)
                    own.wait()
                    second_keys(t).then_inc(match_used, 1)
                else:
                    step.then_inc(picks_ready, 1)
            second_keys(NT - 1).then_inc(picks_ready, 1)
            for i in range(3):
                dve.wait_ge(picks_turned, i + 1)
                dve.tensor_copy(pickT[:, i, :], bank((6, 7, 4)[i])).then_inc(picks_out, 1)

            dve.wait_ge(picks_out, 3)
            with dve.Fori(0, NT) as i:
                for k in range(32):
                    dve.wait_ge(gate_mm, i * 32 + (k + 1))
                    for t in range(4):
                        token = i * P + (4 * k + t)
                        dve.tensor_scalar(hot[:, k % 2, t, 0, :], iota, pickT[:, 1, bass.ds(token, 1)], None, ALU.is_equal).then_inc(hot_ready, 1)
                        dve.tensor_scalar(hot[:, k % 2, t, 1, :], iota, pickT[:, 2, bass.ds(token, 1)], pickT[:, 0, bass.ds(token, 1)],
                                          ALU.is_equal, ALU.mult).then_inc(hot_ready, 1)

            def u_low(g, j):
                for b in range(2):
                    dve.wait_ge(u_hi, 8 * g + (2 * j + b + 1))
                    dve.tensor_tensor(uT_lo[:, j % 2, 4 * b:4 * b + 4, :], bank((0, 6)[j % 2] + b).rearrange("p (k n) -> p k n", k=4),
                                      uT_hi[:, j % 2, 4 * b:4 * b + 4, :], ALU.subtract).then_inc(u_lo, 1)

            def expert_hidden(g, par, gate_loads):
                dve.wait_ge(gates_in[par], gate_loads)
                dve.wait_ge(w_used, g + 30)
                for j in range(4):
                    if j < 3:
                        u_low(g, j + 1)
                    dve.wait_ge(ex_gelu, 4 * g + (j + 1))
                    dve.tensor_tensor(act_g[:, j % 2, :], gelu[:, j % 2, :], gates[:, par, j, :], ALU.mult).then_inc(ex_mul, 1)
                    dve.wait_ge(ex_mul, 4 * g + (j + 1))
                    dve.wait_ge(ex_hi_done, 4 * g + (j + 1))
                    dve.tensor_tensor(ex_lo[:, par, j, :], act_g[:, j % 2, :], ex_hi[:, par, j, :], ALU.subtract).then_inc(ex_lo_done, 1)

            def expert_add(g):
                for b in range(8):
                    t, c = divmod(b, 2)
                    dve.wait_ge(ex_b, 8 * g + (b + 1))
                    dst = x_sb[:, t, c * 512:(c + 1) * 512]
                    dve.tensor_tensor(dst, bank(4 + b % 2), dst, ALU.add).then_inc(ex_add, 1)

            dve.sem_inc(ex_add, 2)
            u_low(0, 0)
            expert_hidden(0, 0, 16)
            u_low(1, 0)
            with dve.Fori(0, 15) as i:
                expert_hidden(2 * i + 1, 1, i * 16 + 16)
                u_low(2 * i + 2, 0)
                expert_add(2 * i)
                expert_hidden(2 * i + 2, 0, i * 16 + 32)
                u_low(2 * i + 3, 0)
                expert_add(2 * i + 1)
            expert_hidden(31, 1, 16 * 16)
            expert_add(30)
            expert_add(31)

            dve.wait_ge(rstd_done, 9)
            dve.wait_ge(out_gain_in, 16)
            for t in range(NT):
                dve.scalar_tensor_tensor(out_rows[:, t, :], x_sb[:, t, :], rstd[:, t:t + 1], out_gain, ALU.mult, ALU.mult).then_inc(out_ready, 1)


_INS = ["x", "positions", "g_mix_norm", "w_in", "conv_w", "conv_b", "b_gates", "g_mlstm_out", "g_cq", "g_ckv",
        "w_uq", "w_ukv", "g_q", "g_k", "w_out", "g_ffn_norm", "w_ff1", "w_ff2", "norm_mix_g_2", "w_in_2",
        "diff_lambda_2", "diff_subln_g_2", "w_out_2", "norm_ffn_g_2", "peer_wq_2", "peer_subkeys_2", "peer_u_2",
        "peer_v_2", "final_norm_g_2"]


def kernel(**inputs):
    import concourse.bacc as bacc
    from concourse.bass_utils import run_bass_kernel_spmd

    nc = bacc.Bacc("TRN2", target_bir_lowering=False, num_devices=1)
    arrays = {f"in_{name}": np.ascontiguousarray(inputs[name]) for name in _INS}
    arrays["in_table"] = TABLE
    ins = {name[3:]: nc.dram_tensor(name, a.shape, mybir.dt.from_np(a.dtype), kind="ExternalInput").ap()
           for name, a in arrays.items()}
    out = nc.dram_tensor("out", (1, T, D), F32, kind="ExternalOutput").ap()
    build(nc, ins, out)
    r = run_bass_kernel_spmd(nc, [arrays], core_ids=[0])
    return r.results[0]["out"]
```

```python
from contextlib import ExitStack

import numpy as np

import concourse.bass as bass
from concourse import mybir

F32 = mybir.dt.float32
BF16 = mybir.dt.bfloat16
U32 = mybir.dt.uint32
I32 = mybir.dt.int32
ALU = mybir.AluOpType
ACT = mybir.ActivationFunctionType
AX = mybir.AxisListType

P = 128
T = 512
NT = T // P
D = 1024
KD = D // P
EPS = 1e-6

H = 4
DQK = 64
DV = 128
NC = T // P
TAPS = 5
A_NOPE, A_ROPE = 128, 64
A_DH = A_NOPE + A_ROPE
Q_LORA, KV_LORA = 256, 128
N_GATES = 16
D_FF = 4096
TAIL = N_GATES + Q_LORA + KV_LORA + A_ROPE
C_CQ, C_CKV, C_KPE = N_GATES, N_GATES + Q_LORA, N_GATES + Q_LORA + KV_LORA
ROWS = 36

RET_DK = 128
DIFF_D = 64
P_HEADS = 8
TOPK = 16
N_KEYS = 128
LAMBDA_INIT = 0.2

CW = 512
FF_GROUPS = D_FF // CW
EX_GROUPS = N_KEYS // 4
RING = 4

CONSTS = {}


def constant_table():
    i = np.arange(P, dtype=np.float64)
    parts = {}
    parts["ident"] = np.eye(P)
    parts["mask_fw"] = np.where(i[:, None] <= i[None, :], 0.0, -1e30)
    parts["mask_bw"] = np.where(i[:, None] >= i[None, :], 0.0, -1e30)
    inv_freq = (np.float32(10000.0) ** (-np.arange(0, A_ROPE, 2, dtype=np.float32) / np.float32(A_ROPE))).astype(np.float32)
    parts["inv_freq"] = np.broadcast_to(inv_freq, (P, A_ROPE // 2))
    gamma_log = np.log1p(-np.exp2(-5.0 - np.arange(H)))
    rel = i[None, :] - i[:, None]
    intra = np.where(rel[None] >= 0, np.exp(gamma_log[:, None, None] * np.maximum(rel[None], 0.0)), 0.0)
    parts["intra"] = (intra * RET_DK ** -0.5).transpose(1, 0, 2)
    parts["cross"] = np.broadcast_to(np.exp(gamma_log[:, None] * (i + 1.0)), (P, H, P))
    parts["kdec"] = (np.exp(gamma_log[:, None] * (P - 1.0 - i)) * RET_DK ** -0.5).T
    m = np.arange(T) - (T - P)
    dist = i[:, None] - m[None, :]
    parts["negdist"] = np.where(dist >= 0, -dist, -1e33)
    parts["iota"] = np.broadcast_to(i, (P, P))
    at, cols = 0, []
    for name, a in parts.items():
        a = np.ascontiguousarray(a, np.float32).reshape(P, -1)
        CONSTS[name] = (at, a.shape[1])
        at += a.shape[1]
        cols.append(a)
    return np.concatenate(cols, axis=1)


TABLE = constant_table()
GAMMA = [float(1.0 - 2.0 ** (-5.0 - h)) for h in range(H)]
CDEC = [g ** P for g in GAMMA]
SLOPES = [float(2.0 ** (-8.0 * (h + 1) / H)) for h in range(H)]

TWO_PI_A = 6.28125
TWO_PI_B = float(np.float32(2 * np.pi - TWO_PI_A))
TWO_PI_C = float(2 * np.pi - TWO_PI_A - np.float64(np.float32(2 * np.pi - TWO_PI_A)))
ROUND = 12582912.0


class Steps:

    def __init__(self, eng, sem):
        self.eng, self.sem, self.n = eng, sem, 0

    def did(self, instruction):
        instruction.then_inc(self.sem, 1)
        self.n += 1

    def wait(self):
        self.eng.wait_ge(self.sem, self.n)


def build(nc, ins, out):
    ctx = ExitStack()
    with ctx:
        def sbuf(name, shape, dt=F32):
            return ctx.enter_context(nc.sbuf_tensor(name, shape, dt))

        def sem(name):
            return ctx.enter_context(nc.semaphore(name))

        x_sb = sbuf("x_sb", [P, NT, D])
        consts = sbuf("consts", [P, TABLE.shape[1]])
        ring = sbuf("ring", [P, RING, 4096])
        split = sbuf("split", [P, 2, 2, 4096], BF16)
        arena = sbuf("arena", [P, 20480])
        gains = sbuf("gains", [P, 64])
        small = sbuf("small", [P, 640])
        bcast = sbuf("bcast", [P, 656])
        ps = ctx.enter_context(nc.psum_tensor("ps", [P, 8, 512], F32))

        def const(name, **dims):
            at, n = CONSTS[name]
            a = consts[:, at:at + n]
            return a.rearrange("p (%s) -> p %s" % (" ".join(dims), " ".join(dims)), **dims) if dims else a

        ident = const("ident")
        iota = const("iota")
        mask = [const("mask_fw"), const("mask_bw")]

        def bank(i):
            return ps[:, i, :]

        def part(base, at, *shape, dt=F32):
            n = 1
            for s in shape:
                n *= s
            words = n if dt is not BF16 else n // 2
            a = base[:, at:at + words]
            if dt is not F32:
                a = a.bitcast(dt)
            if len(shape) > 1:
                names = "abcd"[:len(shape)]
                a = a.rearrange("p (%s) -> p %s" % (" ".join(names), " ".join(names)),
                                **dict(zip(names, shape)))
            return a

        split_words = split[:, :, :, :].rearrange("p s h n -> p (s h n)").bitcast(F32)

        G_MIX, G_Y1, G_FFN, G_MIX2, G_Y2, G_FFN2, G_CQ, G_CKV, G_QN, G_KN = 0, 8, 16, 24, 32, 40, 48, 50, 51, 52
        gate_bias = bcast[:, 0:16]
        rope_gain = bcast[:, 16:144].rearrange("p (a b) -> p a b", a=2)
        lam_in = bcast[:, 144:400].rearrange("p (a b) -> p a b", a=4)
        cos_t = bcast[:, 400:528].rearrange("p (a b) -> p a b", a=NT)
        sin_t = bcast[:, 528:656].rearrange("p (a b) -> p a b", a=NT)

        sumsq = small[:, 0:32]
        mean_eps = small[:, 32:64]
        rstd = small[:, 64:96]
        minus_half = small[:, 96:128]
        prev_max = small[:, 128:132]
        dec_rows = small[:, 132:136]
        dec_cols = small[:, 136:168].rearrange("p (a b) -> p a b", a=8)
        den = small[:, 168:176].rearrange("p (a b) -> p a b", a=2)
        den_t = small[:, 176:184].rearrange("p (a b) -> p a b", a=2)
        den_r = small[:, 184:192].rearrange("p (a b) -> p a b", a=2)
        row_max = small[:, 192:224]
        row_nmax = small[:, 224:256]
        row_sum = small[:, 256:288]
        row_inv = small[:, 288:320]
        lam = small[:, 320:328]
        pos = small[:, 328:332]
        one_col = small[:, 332:333]
        pos_rows = small[:, 336:464]

        hT = part(arena, 0, KD, T)
        y1 = part(arena, 0, NT, D)
        conv_in = part(arena, 4096, 4, T + 4)
        qkT = part(arena, 6160, 4, T)
        v1 = part(arena, 8208, NT, H * DV)
        o1 = part(arena, 10256, NT, H * DV)
        k_tok = part(arena, 12304, NT, H * DQK)
        tail = part(arena, 13328, NT, TAIL)
        xn1 = part(arena, 15184, NT, D)
        decay = part(arena, 15184, 2, 2, NC * P)
        probs = part(arena, 17232, 2, 2, NC, P)
        num = part(arena, 19280, 2, NC, DV)
        rows = [part(split_words, 512 * i, T) for i in range(10)]
        lf_row, b_row, c_row, m_row, negm_row, inter_row, em_row, w_row, t_row, u_row = rows
        gate_pad = part(split_words, 5120, NT, 2, 64)
        gate_cols = part(split_words, 5632, 4, NC, ROWS)
        conv_rows = part(split_words, 6208, T)
        state = part(split_words, 6720, 2, 3, 132)
        k_dec = part(split_words, 7512, 2, 3, DQK)
        conv_w = part(split_words, 7896, 4, 8)
        ones = part(split_words, 7936, P)

        qk_sumsq = small[:, 512:544].rearrange("p (t h) -> p t h", t=NT)
        qk_rstd = small[:, 544:576].rearrange("p (t h) -> p t h", t=NT)
        qk_mean = small[:, 576:608].rearrange("p (t h) -> p t h", t=NT)

        cqT = part(split_words, 0, 2, T)
        ckvT = part(split_words, 1024, T)
        qk_tok = part(split_words, 1536, 2, 2 * H, A_DH)
        qk_sq = part(split_words, 4608, 2 * H, A_DH)
        angle = part(split_words, 6144, NT, A_ROPE // 2)
        turns = part(split_words, 6272, NT, A_ROPE // 2)
        angle_c = part(split_words, 6400, NT, A_ROPE // 2)
        pos_f = part(split_words, 6528, P)
        nopeT = part(arena, 4096, 2 * H, T)
        ropeT = part(arena, 8192, 2 * H, T)
        v2 = part(arena, 15184, NT, H, DV)
        att = part(arena, 17232, 2, T)
        attT = part(arena, 18256, 2, T)
        rot = part(arena, 19280, 2 * H, A_ROPE)
        rot_t = part(arena, 19792, 2 * H, A_ROPE // 2)

        xT_hi = part(arena, 4096, KD, T, dt=BF16)
        xT_lo = part(arena, 6144, KD, T, dt=BF16)
        xn = part(arena, 0, NT, D)

        relu = part(arena, 8192, 2, T)
        hid = part(arena, 9216, 2, T)
        hid_hi = part(arena, 10240, 2, 4, T, dt=BF16)
        hid_lo = part(arena, 12288, 2, 4, T, dt=BF16)

        rqT = part(arena, 8192, H, T)
        rkT = part(arena, 10240, H, T)
        rv = part(arena, 12288, NT, H * DV)
        rg = part(arena, 14336, NT, H * DV)
        dqT = part(arena, 16384, H, T)
        dkT = part(arena, 0, H, T)
        dv2 = part(arena, 2048, NT, H, DV)
        y2 = part(arena, 4096, NT, D)
        ret_in = part(split_words, 0, 2, NC, P)
        ret_k = part(split_words, 1024, 2, NC, P)
        ret_q = part(split_words, 2048, 2, NC, P)
        ret_s = part(split_words, 3072, 3, P)
        spare_row = part(split_words, 3456, P)
        dif = part(arena, 18432, 2, 2, T)
        difT = part(arena, 8192, 2, T)
        dif_sq = part(arena, 9216, P)
        lam_t = part(arena, 9344, 2, DIFF_D)
        y2T_hi = part(arena, 10240, KD, T, dt=BF16)
        y2T_lo = part(arena, 12288, KD, T, dt=BF16)

        top_v = part(arena, 0, NT, 2 * P_HEADS, TOPK)
        top_i = arena[:, 1024:2048].bitcast(U32).rearrange("p (t g k) -> p t g k", t=NT, g=2 * P_HEADS)
        top_f = part(arena, 2048, NT, 2 * P_HEADS, TOPK)
        pick_v = part(arena, 3072, NT, P_HEADS, TOPK)
        pick_i = arena[:, 3584:4096].bitcast(U32).rearrange("p (t g k) -> p t g k", t=NT, g=P_HEADS)
        half_q = part(arena, 8192, 2, T)
        masked = part(arena, 9216, NT, 256)
        keys = part(arena, 14336, 2 * P_HEADS, P)
        keysT = part(arena, 16384, 2 * P_HEADS, P)
        cand = part(arena, 8192 + 2048, 2, P_HEADS, TOPK, TOPK)
        match0 = part(arena, 14336, P_HEADS, TOPK, TOPK)
        match1 = part(arena, 16384, P_HEADS, TOPK, TOPK)
        pick_g = part(arena, 18432, NT, P)
        pick_1 = part(arena, 18944, NT, P)
        pick_2 = part(arena, 19456, NT, P)
        half_i = arena[:, 19968:20480].bitcast(U32).rearrange("p (t g k) -> p t g k", t=NT, g=P_HEADS)
        half_f = part(split_words, 0, 2, NT, P_HEADS, TOPK)
        gate_sum = small[:, 0:32]
        gate_inv = small[:, 32:64]
        gateT = part(arena, 0, 2, T, dt=BF16)
        keyT = part(arena, 512, 2, T, dt=BF16)
        HB = 8
        iota8 = part(arena, 1024, P, HB, dt=BF16)
        hot_1 = part(arena, 8192, 4, P, HB, dt=BF16)
        hot_2 = part(arena, 10240, 4, P, HB, dt=BF16)
        hot_hi = part(arena, 12288, 4, P, HB, dt=BF16)
        hot_lo = part(arena, 14336, 4, P, HB, dt=BF16)
        LOW_KEYS = 112
        TB = 32
        gate_block = [part(split_words, 0, P, TB), part(split_words, 4096, P, TB)]
        EARLY = 6
        SORTING = 5
        u_copy = part(split_words, 5120, 2, KD, P)
        uT_pre = [part(split_words, 1024, 2, KD, P, dt=BF16), part(split_words, 2048, 2, KD, P, dt=BF16)]
        gelu_pre = part(split_words, 3072, 4, T)
        gelu_back = part(arena, 0, 2, 4, T)
        gates = part(arena, 16384, 2, T // TB, 4, TB)
        uT_hi = part(arena, 8192, 2, KD, P, dt=BF16)
        uT_lo = part(arena, 9216, 2, KD, P, dt=BF16)
        gelu = part(arena, 10240, 2, T)
        act_g = part(arena, 11264, 2, T)
        ex_hi = part(arena, 12288, 2, 4, T, dt=BF16)
        ex_lo = part(arena, 14336, 2, 4, T, dt=BF16)
        out_gain = part(arena, 0, D)
        out_rows = part(arena, 4096, NT, D)

        gelu_dram = nc.dram_tensor("early_activations", (P, EARLY, 4, T), F32, kind="Internal").ap()
        gate_dram = nc.dram_tensor("gate_matrix", (P, T // TB, N_KEYS, TB), F32, kind="Internal").ap()

        x_in = [sem(f"x_in{t}") for t in range(NT)]
        const_in, small_in = sem("const_in"), sem("small_in")
        ring_in = [sem(f"ring_in{i}") for i in range(RING)]
        filled = sem("filled")
        own_v, own_a, own_p = sem("own_v"), sem("own_a"), sem("own_p")
        ssq_done, rstd_done = sem("ssq_done"), sem("rstd_done")
        xn_done, turned, turned_hi, turned_lo = sem("xn_done"), sem("turned"), sem("turned_hi"), sem("turned_lo")
        mm_done, mm_out = sem("mm_done"), sem("mm_out")
        w_hi, w_lo, w_used = sem("w_hi"), sem("w_lo"), sem("w_used")
        conv_turned, conv_done, qk_done = sem("conv_turned"), sem("conv_done"), sem("qk_done")
        ktok_turned, ktok_done = sem("ktok_turned"), sem("ktok_done")
        gates_padded, gates_turned, f_neg, f_log = sem("gates_padded"), sem("gates_turned"), sem("f_neg"), sem("f_log")
        rows_ready, rows_exp, cols_turned, cols_done = sem("rows_ready"), sem("rows_exp"), sem("cols_turned"), sem("cols_done")
        scores_done, decay_in, decay_exp, probs_done = sem("scores_done"), sem("decay_in"), sem("decay_exp"), sem("probs_done")
        kdec_done, kv_done, state_done = sem("kdec_done"), sem("kv_done"), sem("state_done")
        num_done, num_out, inter_done, head_out = sem("num_done"), sem("num_out"), sem("inter_done"), sem("head_out")
        head_read = sem("head_read")
        y_ready, o_sig = sem("y_ready"), sem("o_sig")

        latent_done, qk_put, pe_put, v_put, qk_squared = sem("latent_done"), sem("qk_put"), sem("pe_put"), sem("v_put"), sem("qk_squared")
        qk_summed, qk_rstd_done, qk_rotated, qk_turned = sem("qk_summed"), sem("qk_rstd_done"), sem("qk_rotated"), sem("qk_turned")
        nope_out, rope_out, pos_turned, angles, rotary = sem("nope_out"), sem("rope_out"), sem("pos_turned"), sem("angles"), sem("rotary")
        proj_done = sem("proj_done")
        att_scores, att_max, att_exp, att_turned, att_out, att_pv, att_norm = (
            sem(f"att_{n}") for n in ("scores", "max", "exp", "turned", "out", "pv", "norm"))
        ff_a, ff_relu, ff_hi, ff_lo, ff_b, ff_add = (sem(f"ff_{n}") for n in ("a", "relu", "hi", "lo", "b", "add"))

        ret_scores, ret_kturned, ret_a, ret_kd, ret_qx, ret_kv, ret_state, ret_o, ret_y = (
            sem(f"ret_{n}") for n in ("scores", "kturned", "a", "kd", "qx", "kv", "state", "o", "y"))
        rg_silu, lam_sums, lam_exp = sem("rg_silu"), sem("lam_sums"), sem("lam_exp")
        dif_scores, dif_max, dif_exp, dif_probs, dif_turned, dif_out, dif_pv, dif_y = (
            sem(f"dif_{n}") for n in ("scores", "max", "exp", "probs", "turned", "out", "pv", "y"))
        keys_in, keys_turned, keys_out = sem("keys_in"), sem("keys_turned"), sem("keys_out")
        key_scores, key_tops, cands, picks_top, places = (
            sem("key_scores"), sem("key_tops"), sem("cands"), sem("picks_top"), sem("places"))
        gate_in, gate_exp, match_eq, match_p, match_used, picks_ready, picks_turned, picks_out = (
            sem("gate_in"), sem("gate_exp"), sem("match_eq"), sem("match_p"), sem("match_used"), sem("picks_ready"), sem("picks_turned"), sem("picks_out"))
        hot_keys, hot_hi_done, hot_lo_done, gate_mm, gate_out = (
            sem("hot_keys"), sem("hot_hi_done"), sem("hot_lo_done"), sem("gate_mm"), sem("gate_out"))
        gate_stored = [sem("gate_stored0"), sem("gate_stored1")]
        gates_in = [sem("gates_in0"), sem("gates_in1")]
        u_turned, u_hi, u_lo, ex_a, ex_gelu, ex_mul, ex_hi_done, ex_lo_done, ex_b, ex_add = (
            sem(n) for n in ("u_turned", "u_hi", "u_lo", "ex_a", "ex_gelu", "ex_mul", "ex_hi_done", "ex_lo_done", "ex_b", "ex_add"))
        u_copied = sem("u_copied")
        gelu_stored = [sem(f"gelu_stored{j}") for j in range(4)]
        late_stored = [sem("late_stored0"), sem("late_stored1")]
        gelu_in = [sem("gelu_in0"), sem("gelu_in1")]
        out_gain_in, out_ready, out_stored = sem("out_gain_in"), sem("out_ready"), sem("out_stored")
        y2_ready = sem("y2_ready")
        ff_sq = sem("ff_sq")

        S_OUT, S_FF, S_IN2, S_OUT2, S_WQ, S_EX = 0, 2, 18, 25, 27, 31
        TURN = {"mix": 0, "latent": 8, "out": 11, "ffn": 19, "mix2": 27, "out2": 35, "peer": 43}
        TURN_LO = {"out": 0, "ffn": 8, "mix2": 16, "out2": 24, "peer": 32}
        MM = {"z": 0, "out": 16, "in2": 24, "out2": 52, "wq": 60}

        Z_ORDER = (0, 3, 1, 2)

        def z_width(c):
            return CW if c < 3 else TAIL

        def arrived(j4, rounds):
            return 16 * rounds + 16 + (16 if j4 == 0 else 0)

        def ring_chunk(j, cols=CW):
            return ring[:, j % RING, 0:KD * cols].rearrange("p (k n) -> p k n", k=KD)

        def chunk_here(eng, j):
            eng.wait_ge(ring_in[j % RING], 16 if j < RING else arrived(j % RING, j // RING))

        def high(s2, k):
            return split[:, s2, 0, :].rearrange("p (k n) -> p k n", k=k)

        def low(s2, k):
            return split[:, s2, 1, :].rearrange("p (k n) -> p k n", k=k)

        def early_place(c):
            return c % RING, 9 + c // RING

        def group_summed(eng, g):
            if not isinstance(g, int) or g >= 2:
                eng.wait_ge(ex_b, 8 * g - 7)

        def z_place(n):
            p, r = divmod(n, 4)
            return (conv_in[:, r, 2:T + 2], v1[:, r, :], o1[:, r, :], tail[:, r, :])[Z_ORDER[p]]

        TURN_BANKS = (0, 1, 4, 5)

        def gate_banks(k):
            return ps[:, 2 * (k % 2):2 * (k % 2) + 2, :].rearrange("p b (t n) -> p (b t) n", t=4)

        SMALLS = 20
        block = ctx.enter_context(nc.Block())

        @block.sync
        def _(sp):
            for t in range(NT):
                sp.dma_start(x_sb[:, t, :], ins["x"][0, t * P:(t + 1) * P, :]).then_inc(x_in[t], 16)

            sp.dma_start(consts[:, :], ins["table"]).then_inc(const_in, 16)

            w_in = ins["w_in"][0].rearrange("(p k) n -> p k n", k=KD)
            for p, c in enumerate(Z_ORDER):
                n = z_width(c)
                sp.dma_start(ring_chunk(p, n), w_in[:, :, c * CW:c * CW + n]).then_inc(ring_in[p], 16)
                if p == 0:
                    sp.dma_start(conv_rows[0:TAPS, :], ins["conv_w"][0]).then_inc(small_in, 16)
                    sp.dma_start(conv_rows[TAPS:TAPS + 1, :], ins["conv_b"]).then_inc(small_in, 16)
                    sp.dma_start(gate_bias, ins["b_gates"].to_broadcast([P, 16])).then_inc(small_in, 16)
                    sp.wait_ge(filled, 4)
                    for at, name, parts, cols in (
                        (G_MIX, "g_mix_norm", (0, P), KD), (G_Y1, "g_mlstm_out", (0, 64), KD), (G_FFN, "g_ffn_norm", (0, P), KD),
                        (G_MIX2, "norm_mix_g_2", (0, P), KD), (G_FFN2, "norm_ffn_g_2", (0, P), KD),
                        (G_CQ, "g_cq", (0, P), 2), (G_CKV, "g_ckv", (0, P), 1),
                    ):
                        sp.dma_start(gains[parts[0]:parts[1], at:at + cols],
                                      ins[name][0].rearrange("(p k) -> p k", k=cols)).then_inc(small_in, 16)
                    sp.dma_start(gains[:, G_QN:G_QN + 1], ins["g_q"][0, 0:P].rearrange("(p k) -> p k", k=1)).then_inc(small_in, 16)
                    sp.dma_start(gains[:, G_KN:G_KN + 1], ins["g_k"][0, 0:P].rearrange("(p k) -> p k", k=1)).then_inc(small_in, 16)
                    for h in range(H):
                        sp.dma_start(gains[64 + 16 * h:80 + 16 * h, G_Y2:G_Y2 + KD],
                                      ins["diff_subln_g_2"][0].rearrange("(p k) -> p k", k=KD)).then_inc(small_in, 16)
                    sp.dma_start(rope_gain[:, 0, :], ins["g_q"][0:1, P:A_DH].to_broadcast([P, A_ROPE])).then_inc(small_in, 16)
                    sp.dma_start(rope_gain[:, 1, :], ins["g_k"][0:1, P:A_DH].to_broadcast([P, A_ROPE])).then_inc(small_in, 16)
                    sp.dma_start(lam_in, ins["diff_lambda_2"].to_broadcast([P, 4, DIFF_D])).then_inc(small_in, 16)
                    sp.dma_start(pos_rows[0:NT, :].bitcast(I32), ins["positions"][0].rearrange("(t p) -> t p", p=P)).then_inc(small_in, 16)

            sp.wait_ge(mm_done, 4)
            sp.dma_start(ring[:, 0, 0:1536].rearrange("p (k n) -> p k n", k=2),
                         ins["w_uq"][0].rearrange("(p k) n -> p k n", k=2)).then_inc(ring_in[0], 16)
            sp.dma_start(ring[:, 0, 1536:2560], ins["w_ukv"][0]).then_inc(ring_in[0], 16)
            w_out = ins["w_out"][0].rearrange("(p k) n -> p k n", k=KD)
            for c in range(2):
                sp.wait_ge(mm_done, 4 * (c + 2))
                sp.dma_start(ring_chunk(5 + c), w_out[:, :, c * CW:(c + 1) * CW]).then_inc(ring_in[1 + c], 16)

            w_ff1 = ins["w_ff1"][0].rearrange("(p k) n -> p k n", k=KD)
            w_ff2 = ins["w_ff2"][0].rearrange("(g p j) n -> g p (j n)", p=P, j=4)

            def load_ff1(g, slot):
                sp.dma_start(ring_chunk(slot), w_ff1[:, :, bass.ds(g * CW, CW)]).then_inc(ring_in[slot], 16)

            def load_ff2(g, slot):
                sp.dma_start(ring[:, slot, :], w_ff2[bass.ds(g, 1)].rearrange("g p n -> (g p) n")).then_inc(ring_in[slot], 16)

            sp.wait_ge(mm_done, 16)
            load_ff1(0, 3)
            sp.wait_ge(proj_done, NT)
            load_ff1(1, 0)
            with sp.Fori(0, 3) as i:
                for m, (load, g) in enumerate(((load_ff2, 0), (load_ff1, 2), (load_ff2, 1), (load_ff1, 3)), 1):
                    sp.wait_ge(w_lo, 4 * i + m)
                    load(2 * i + g, m % RING)
            for m, g in ((1, 6), (2, 7)):
                sp.wait_ge(w_lo, 12 + m)
                load_ff2(g, m)

            w_in_2 = ins["w_in_2"][0].rearrange("(p k) n -> p k n", k=KD)
            w_out_2 = ins["w_out_2"][0].rearrange("(p k) n -> p k n", k=KD)
            peer_wq = ins["peer_wq_2"][0].rearrange("(p k) n -> p k n", k=KD)
            later = [(w_in_2, c) for c in range(7)] + [(w_out_2, c) for c in range(2)] + [(peer_wq, c) for c in range(4)]
            for s, (w, c) in enumerate(later, S_IN2):
                sp.wait_ge(w_lo, s - 3)
                sp.dma_start(ring_chunk(s + 5), w[:, :, c * CW:(c + 1) * CW]).then_inc(ring_in[(s + 5) % RING], 16)
                if s == 28:
                    sp.wait_ge(y2_ready, NT * H)
                    sp.dma_start(keys, ins["peer_subkeys_2"][0].rearrange("h a n d -> n (h a) d")).then_inc(keys_in, 16)

            peer_u = ins["peer_u_2"][0].rearrange("(p j) d -> p (j d)", p=P)
            peer_v = ins["peer_v_2"][0].rearrange("(p j) d -> p (j d)", p=P)

            def load_rows(table, g, slot):
                sp.dma_start(ring[:, slot, :], table[:, bass.ds(g * (4 * D), 4 * D)]).then_inc(ring_in[slot], 16)

            def load_gates(g, par):
                sp.dma_start(gates[:, par, :, :, :], gate_dram[:, :, bass.ds(g * 4, 4), :]).then_inc(gates_in[par], 16)

            def load_gelu(g):
                sp.dma_start(gelu_back[:, g % 2, :, :], gelu_dram[:, g, :, :]).then_inc(gelu_in[g % 2], 16)

            for g in range(RING):
                sp.wait_ge(w_lo, 28 + g)
                load_rows(peer_u, g, g)
            for q, (table, g) in enumerate(((peer_u, 4), (peer_u, 5), (peer_v, 0), (peer_v, 1), (peer_v, 2))):
                sp.wait_ge(u_turned, 8 * (q + 1))
                load_rows(table, g, q % RING)
            sp.sem_inc(gate_stored[0], 16)
            sp.sem_inc(gate_stored[1], 16)
            with sp.Fori(0, NT) as i:
                for q in range(P // TB):
                    sp.wait_ge(gate_out, i * 16 + (4 * (q + 1) + 2))
                    sp.dma_start(gate_dram[:, bass.ds(i * 4 + q, 1), :, :].rearrange("p b n t -> p (b n t)"),
                                 gate_block[q % 2].rearrange("p n t -> p (n t)")).then_inc(gate_stored[q % 2], 16)
            sp.wait_ge(gate_stored[0], 32 * NT + 16)
            sp.wait_ge(gate_stored[1], 32 * NT + 16)
            for j in range(4):
                sp.wait_ge(gelu_stored[j], 16 * SORTING)
            for g in range(2):
                load_gates(g, g)
                load_gelu(g)
            sp.wait_ge(u_turned, 8 * 6)
            load_rows(peer_v, 3, 1)
            for g in (2, 3):
                sp.wait_ge(ex_mul, 4 * (g - 1))
                load_gates(g, g % 2)
                load_gelu(g)
            sp.wait_ge(w_lo, S_EX + 1)
            load_rows(peer_v, 4, 2)
            sp.wait_ge(w_lo, S_EX + 2)
            load_rows(peer_u, 6, 3)
            sp.wait_ge(ex_mul, 12)
            load_gates(4, 0)
            load_gelu(4)
            sp.wait_ge(w_lo, S_EX + 3)
            load_rows(peer_v, 5, 0)
            sp.wait_ge(ex_mul, 16)
            load_gates(5, 1)
            sp.wait_ge(late_stored[0], 32)
            sp.wait_ge(late_stored[1], 32)
            load_gelu(5)
            sp.wait_ge(w_lo, S_EX + 4)
            load_rows(peer_u, 7, 1)
            sp.wait_ge(w_lo, S_EX + 5)
            load_rows(peer_v, 6, 2)
            sp.wait_ge(ex_mul, 20)
            load_gates(6, 0)
            with sp.Fori(1, 13) as i:
                sp.wait_ge(u_turned, 16 * i + 40)
                load_rows(peer_u, 2 * i + 6, 3)
                sp.wait_ge(w_lo, 2 * i + (S_EX + 4))
                load_rows(peer_v, 2 * i + 5, 0)
                sp.wait_ge(ex_mul, 8 * i + 16)
                load_gates(2 * i + 5, 1)
                sp.wait_ge(u_turned, 16 * i + 48)
                load_rows(peer_u, 2 * i + 7, 1)
                sp.wait_ge(w_lo, 2 * i + (S_EX + 5))
                load_rows(peer_v, 2 * i + 6, 2)
                sp.wait_ge(ex_mul, 8 * i + 20)
                load_gates(2 * i + 6, 0)
            sp.wait_ge(w_lo, S_EX + 30)
            load_rows(peer_v, 31, 0)
            sp.wait_ge(ex_mul, 4 * 30)
            load_gates(31, 1)
            sp.dma_start(out_gain, ins["final_norm_g_2"].unsqueeze(0).to_broadcast([P, D])).then_inc(out_gain_in, 16)

            for t in range(NT):
                sp.wait_ge(out_ready, t + 1)
                sp.dma_start(out[0, t * P:(t + 1) * P, :], out_rows[:, t, :]).then_inc(out_stored, 16)
            sp.wait_ge(out_stored, 16 * NT)

        @block.gpsimd
        def _(pool):
            own = Steps(pool, own_p)
            pool.memset(minus_half, -0.5).then_inc(filled, 1)
            pool.memset(ones, 1.0).then_inc(filled, 1)
            pool.memset(one_col, 1.0).then_inc(filled, 1)
            pool.memset(gains[:, :], 1.0).then_inc(filled, 1)
            pool.memset(gate_pad, 0.0).then_inc(filled, 1)
            pool.memset(prev_max, 0.0).then_inc(filled, 1)
            pool.memset(dec_rows, 0.0).then_inc(filled, 1)
            pool.memset(conv_in[:, :, 0:2], 0.0).then_inc(filled, 1)
            pool.memset(conv_in[:, :, T + 2:T + 4], 0.0).then_inc(filled, 1)

            def inverse_rms(n, width, ssq_count, at=0):
                c = slice(at, at + n)
                pool.wait_ge(ssq_done, ssq_count)
                own.did(pool.tensor_scalar(mean_eps[:, c], sumsq[:, c], 1.0 / width, EPS, ALU.mult, ALU.add))
                own.wait()
                pool.tensor_tensor(rstd[:, c], mean_eps[:, c], minus_half[:, 0:n], ALU.pow).then_inc(rstd_done, 1)

            pool.wait_ge(filled, 9)
            inverse_rms(NT, D, NT)
            pool.wait_ge(ssq_done, 3 * NT)
            own.did(pool.tensor_scalar(mean_eps[:, 16:20], sumsq[:, 16:20], 1.0 / Q_LORA, EPS, ALU.mult, ALU.add))
            own.did(pool.tensor_scalar(mean_eps[:, 20:24], sumsq[:, 20:24], 1.0 / KV_LORA, EPS, ALU.mult, ALU.add))
            own.wait()
            pool.tensor_tensor(rstd[:, 16:24], mean_eps[:, 16:24], minus_half[:, 0:8], ALU.pow).then_inc(rstd_done, 1)
            inverse_rms(NT * H, DV, 3 * NT + NT * H)

            for t in range(NT):
                if t >= 2:
                    pool.wait_ge(qk_turned, t - 1)
                pool.tensor_copy(qk_tok[:, t % 2, H:2 * H, A_NOPE:A_DH],
                                 tail[:, t, C_KPE:TAIL].unsqueeze(1).to_broadcast([P, H, A_ROPE])).then_inc(pe_put, 1)
                pool.wait_ge(qk_summed, t + 1)
                own.did(pool.tensor_scalar(qk_mean[:, t, :], qk_sumsq[:, t, :], 1.0 / A_DH, EPS, ALU.mult, ALU.add))
                own.wait()
                pool.tensor_tensor(qk_rstd[:, t, :], qk_mean[:, t, :], minus_half[:, 0:2 * H], ALU.pow).then_inc(qk_rstd_done, 1)

            def split_low(s, s4):
                pool.wait_ge(w_hi, s + 1)
                pool.tensor_tensor(split[:, s4 % 2, 1, :], ring[:, (s4 + 5) % RING, :], split[:, s4 % 2, 0, :], ALU.subtract).then_inc(w_lo, 1)

            for s in range(3):
                split_low(s, s)
            inverse_rms(NT, D, 32)
            with pool.Fori(0, 3) as i:
                for m in range(4):
                    split_low(4 * i + 3 + m, (3 + m) % 4)
            for s in range(15, 18):
                split_low(s, s % 4)

            split_low(18, 2)
            inverse_rms(NT, D, 36)
            for s in range(19, 26):
                split_low(s, s % 4)
            pool.wait_ge(w_used, 25)
            pool.wait_ge(mm_out, MM["out2"])
            for h in range(H):
                if h >= 2:
                    pool.wait_ge(ret_o, h - 1)
                pool.tensor_tensor(ret_q[:, h % 2, :, :], rqT[:, h, :].rearrange("p (c i) -> p c i", c=NC),
                                   const("cross", h=H, i=P)[:, h, :].unsqueeze(1).to_broadcast([P, NC, P]), ALU.mult).then_inc(ret_qx, 1)
            inverse_rms(NT * H, RET_DK, 52)
            split_low(26, 2)
            inverse_rms(NT * H, DV, 68, 16)
            split_low(27, 3)

            inverse_rms(NT, D, 72)
            for s in range(28, 31):
                split_low(s, s % 4)


            def sums(t):
                if t >= 2:
                    pool.wait_ge(picks_top, 2 * t - 2)
                four = [P, P_HEADS, TOPK, TOPK]
                pool.tensor_tensor(cand[:, t % 2, :, :, :], top_v[:, t, 0::2, :].unsqueeze(3).to_broadcast(four),
                                   top_v[:, t, 1::2, :].unsqueeze(2).to_broadcast(four), ALU.add).then_inc(cands, 1)

            def lookup(t):
                four = [P, P_HEADS, TOPK, TOPK]
                pool.wait_ge(match_eq, t + 1)
                pool.tensor_tensor(match1, match1, top_f[:, t, 1::2, :].unsqueeze(2).to_broadcast(four), ALU.mult).then_inc(match_p, 1)

            def u_low_early(n):
                for b in range(2):
                    pool.wait_ge(u_copied, 2 * n + b + 1)
                    pool.tensor_tensor(uT_pre[1][:, n % 2, 4 * b:4 * b + 4, :], u_copy[:, n % 2, 4 * b:4 * b + 4, :],
                                       uT_pre[0][:, n % 2, 4 * b:4 * b + 4, :], ALU.subtract).then_inc(u_lo, 1)

            for n in range(4 * SORTING):
                u_low_early(n)
                if n == 1:
                    pool.wait_ge(key_tops, 2 * P_HEADS)
                    sums(0)
                    sums(1)
                if n in (3, 5):
                    sums((n + 1) // 2)
                if n in (10, 12, 14, 16):
                    lookup((n - 10) // 2)

            pool.wait_ge(picks_out, 3)
            with pool.Fori(0, NT) as i:
                for k in range(P // HB):
                    pool.wait_ge(hot_keys, i * 48 + (3 * k + 1))
                    pool.tensor_tensor(hot_lo[:, k % 4, 0:LOW_KEYS, :], hot_2[:, k % 4, 0:LOW_KEYS, :],
                                       gateT[:, 1, bass.ds(i * P + HB * k, HB)].unsqueeze(1).to_broadcast([P, LOW_KEYS, HB]), ALU.mult).then_inc(hot_lo_done, 1)

            def v_low(g, slot, s2):
                pool.wait_ge(w_hi, g + (S_EX + 1))
                pool.tensor_tensor(split[:, s2, 1, :], ring[:, slot, :], split[:, s2, 0, :], ALU.subtract).then_inc(w_lo, 1)

            for g in range(EARLY - 1):
                v_low(g, early_place(EARLY + g)[0], (g + 1) % 2)
            v_low(5, 0, 0)
            with pool.Fori(0, 13) as i:
                v_low(2 * i + 6, 2, 1)
                v_low(2 * i + 7, 0, 0)
            inverse_rms(NT, D, 76)

        @block.scalar
        def _(act):
            own = Steps(act, own_a)
            squares = Steps(act, ssq_done)

            def sum_squares(src, spare, column):
                if squares.n:
                    squares.wait()
                squares.did(act.activation(spare, src, ACT.Square, accum_out=sumsq[:, column:column + 1]))

            for t in range(NT):
                act.wait_ge(x_in[t], 16)
                sum_squares(x_sb[:, t, :], ps[:, 6:8, :].rearrange("p a b -> p (a b)"), t)

            act.wait_ge(small_in, 16 * SMALLS)
            for k in range(KD):
                act.wait_ge(turned, k + 1)
                act.activation(hT[:, k, :], bank(k % 2), ACT.Copy, scale=gains[:, G_MIX + k:G_MIX + k + 1]).then_inc(turned_hi, 1)

            for f in range(4):
                act.wait_ge(conv_done, f + 1)
                act.activation(qkT[:, f, :], qkT[:, f, :], ACT.Silu).then_inc(qk_done, 1)
            act.wait_ge(mm_out, 8)
            for n in range(8, 16):
                act.wait_ge(mm_done, n + 1)
                act.activation(z_place(n), bank(2 + n % 2), ACT.Copy).then_inc(mm_out, 1)
                if n == 9:
                    for f in range(2):
                        act.wait_ge(ktok_turned, f + 1)
                        act.activation(k_tok[:, :, f * P:(f + 1) * P], bank(f).rearrange("p (t c) -> p t c", t=NT), ACT.Copy).then_inc(ktok_done, 1)
                if n == 10:
                    act.wait_ge(f_neg, 1)
                    own.did(act.activation(t_row[0:ROWS, :], u_row[0:ROWS, :], ACT.Exp))
                    own.wait()
                    act.activation(t_row[0:ROWS, :], t_row[0:ROWS, :], ACT.Ln, bias=1.0).then_inc(f_log, 1)
                if n in (11, 12):
                    for t in range(NT):
                        if n == 11:
                            sum_squares(tail[:, t, C_CQ:C_CKV], att[:, 0, 0:Q_LORA], 16 + t)
                        else:
                            sum_squares(tail[:, t, C_CKV:C_KPE], att[:, 0, 0:KV_LORA], 20 + t)
                if n >= 13:
                    i = n - 13
                    r = (inter_row, em_row, w_row)[i]
                    act.wait_ge(rows_ready, 2 + i)
                    act.activation(r[0:ROWS, :], r[0:ROWS, :], ACT.Exp).then_inc(rows_exp, 1)

            for h in range(H):
                act.wait_ge(decay_in, h + 1)
                act.activation(decay[:, h % 2, :, :], decay[:, h % 2, :, :], ACT.Exp).then_inc(decay_exp, 1)
                act.wait_ge(num_done, h + 1)
                if h >= 1:
                    act.wait_ge(head_out, h)
                for d in range(2):
                    act.activation(num[:, d, :, :], bank(4 + d).rearrange("p (c v) -> p c v", c=NC), ACT.Copy).then_inc(num_out, 1)
                act.wait_ge(head_out, h + 1)
                for t in range(NT):
                    sum_squares(y1[:, t, h * DV:(h + 1) * DV], decay[:, h % 2, 0, 0:P], t * H + h)
            act.activation(o1, o1, ACT.Sigmoid).then_inc(o_sig, 1)

            act.wait_ge(angles, 2)
            act.activation(sin_t, angle, ACT.Sin).then_inc(rotary, 1)
            act.activation(cos_t, angle_c, ACT.Sin).then_inc(rotary, 1)
            for k, b in enumerate((0, 1, 4)):
                act.wait_ge(turned, TURN["latent"] + k + 1)
                dst, gain = (cqT[:, k, :], G_CQ + k) if k < 2 else (ckvT, G_CKV)
                act.activation(dst, bank(b), ACT.Copy, scale=gains[:, gain:gain + 1]).then_inc(turned_hi, 1)
            for t in range(NT):
                act.wait_ge(qk_put, t + 1)
                for b in range(2):
                    act.activation(v2[:, t, 2 * b:2 * b + 2, :], bank(4 + b).rearrange("p (h n) -> p h n", h=2)[:, :, A_NOPE:],
                                   ACT.Copy).then_inc(v_put, 1)
                act.wait_ge(pe_put, t + 1)
                if t >= 1:
                    act.wait_ge(qk_summed, t)
                act.activation(qk_sq, qk_tok[:, t % 2, :, :], ACT.Square).then_inc(qk_squared, 1)
                act.wait_ge(qk_turned, t + 1)
                for b in range(2):
                    act.activation(nopeT[:, b * H:(b + 1) * H, t * P:(t + 1) * P], bank(b).rearrange("p (h n) -> p h n", h=H), ACT.Copy,
                                   scale=gains[:, G_QN + b:G_QN + b + 1]).then_inc(nope_out, 1)

            def split_high(s, s4, rounds):
                j4 = (s4 + 5) % RING
                act.wait_ge(ring_in[j4], arrived(j4, rounds))
                act.wait_ge(w_used, s - 1)
                act.activation(split[:, s4 % 2, 0, :], ring[:, j4, :], ACT.Copy).then_inc(w_hi, 1)

            for i in range(H * NT):
                act.wait_ge(att_max, i + 1)
                if i >= 2:
                    act.wait_ge(att_turned, i - 1)
                act.activation(att[:, i % 2, :], bank(2 + i % 2), ACT.Exp, bias=row_nmax[:, i:i + 1], scale=A_DH ** -0.5,
                               accum_out=row_sum[:, i:i + 1]).then_inc(att_exp, 1)
                if i in (3, 7):
                    s = i // 4
                    act.wait_ge(rope_out, 2 * NT)
                    act.wait_ge(ring_in[1 + s], arrived(1 + s, 1))
                    act.activation(split[:, s, 0, :], ring[:, 1 + s, :], ACT.Copy).then_inc(w_hi, 1)

            def turned_high(stage, gain, hi=xT_hi):
                for k in range(KD):
                    act.wait_ge(turned, TURN[stage] + k + 1)
                    act.activation(hi[:, k, :], bank(TURN_BANKS[k % 4]), ACT.Copy, scale=gains[:, gain + k:gain + k + 1]).then_inc(turned_hi, 1)

            turned_high("out", G_Y1)
            split_high(2, 2, 1)
            for t in range(NT):
                act.wait_ge(mm_out, MM["out"] + NT + t + 1)
                sum_squares(x_sb[:, t, :], ps[:, 6:8, :].rearrange("p a b -> p (a b)"), t)
            turned_high("ffn", G_FFN)

            def square_high(g, par):
                for j in range(4):
                    act.wait_ge(ff_relu, 4 * g + j + 1)
                    act.activation(hid_hi[:, par, j, :], relu[:, j % 2, :], ACT.Square).then_inc(ff_hi, 1)

            split_high(3, 3, 2)
            square_high(0, 0)
            with act.Fori(0, 3) as i:
                split_high(4 * i + 4, 0, i + 2)
                square_high(2 * i + 1, 1)
                split_high(4 * i + 5, 1, i + 2)
                split_high(4 * i + 6, 2, i + 2)
                square_high(2 * i + 2, 0)
                split_high(4 * i + 7, 3, i + 3)
            split_high(16, 0, 5)
            square_high(7, 1)
            split_high(17, 1, 5)

            split_high(18, 2, 5)
            for t in range(NT):
                act.wait_ge(ff_add, 8 * (FF_GROUPS - 1) + 2 * t + 4)
                sum_squares(x_sb[:, t, :], ps[:, 6:8, :].rearrange("p a b -> p (a b)"), t)
            turned_high("mix2", G_MIX2)
            for s in range(19, 26):
                split_high(s, s % 4, (s + 5) // 4)

            kdec = const("kdec")
            for i in range(H + 1):
                if i < H:
                    act.wait_ge(ret_kturned, i + 1)
                    if i >= 2:
                        act.wait_ge(ret_kv, i - 1)
                    act.activation(ret_k[:, i % 2, :, :], bank(1).rearrange("p (c d) -> p c d", c=NC), ACT.Copy, scale=kdec[:, i:i + 1]).then_inc(ret_kd, 1)
                if i == 0:
                    act.activation(rg, rg, ACT.Silu).then_inc(rg_silu, 1)
                if i >= 1:
                    h = i - 1
                    act.wait_ge(ret_y, h + 1)
                    for t in range(NT):
                        sum_squares(y2[:, t, h * DV:(h + 1) * DV], spare_row, t * H + h)
            act.wait_ge(lam_sums, 1)
            act.activation(lam[:, 2:4], lam[:, 0:2], ACT.Exp).then_inc(lam_exp, 1)

            for i in range(H * NT + 1):
                if i < H * NT:
                    n_keys = (i % NT + 1) * P
                    for m in range(2):
                        act.wait_ge(dif_max, 2 * i + m + 1)
                        act.activation(dif[:, i % 2, m, 0:n_keys], dif[:, i % 2, m, 0:n_keys], ACT.Exp, bias=row_nmax[:, 2 * i + m:2 * i + m + 1],
                                       accum_out=row_sum[:, 2 * i + m:2 * i + m + 1]).then_inc(dif_exp, 1)
                if i == 4:
                    split_high(26, 2, 7)
                if i >= 3:
                    n = i - 3
                    h, q = divmod(n, NT)
                    act.wait_ge(dif_y, n + 1)
                    sum_squares(y2[:, q, 512 + h * DV:512 + (h + 1) * DV], dif_sq, 16 + q * H + h)
            for n in (14, 15):
                h, q = divmod(n, NT)
                act.wait_ge(dif_y, n + 1)
                sum_squares(y2[:, q, 512 + h * DV:512 + (h + 1) * DV], dif_sq, 16 + q * H + h)
            turned_high("out2", G_Y2, y2T_hi)
            split_high(27, 3, 8)

            for t in range(NT):
                act.wait_ge(mm_out, MM["wq"] - NT + t + 1)
                sum_squares(x_sb[:, t, :], ps[:, 6:8, :].rearrange("p a b -> p (a b)"), t)
            for b in range(4):
                act.wait_ge(keys_turned, b + 1)
                act.activation(keysT[:, 4 * b:4 * b + 4, :], bank(4 + b % 2).rearrange("p (g n) -> p g n", g=4), ACT.Copy).then_inc(keys_out, 1)
            turned_high("peer", G_FFN2)
            for n in range(16):
                if n % 4 == 0 and n < 12:
                    split_high(28 + n // 4, (28 + n // 4) % 4, (33 + n // 4) // 4)
                act.wait_ge(mm_done, MM["wq"] + n + 1)
                if n >= 2:
                    act.wait_ge(key_scores, n - 1)
                act.activation(half_q[:, n % 2, :], bank(2 + n % 2), ACT.Copy).then_inc(mm_out, 1)
            def u_high(g, j, hi=uT_hi, copy=None):
                for b in range(2):
                    act.wait_ge(u_turned, 8 * g + (2 * j + b + 1))
                    turned_u = bank((0, 6)[j % 2] + b).rearrange("p (k n) -> p k n", k=4)
                    act.activation(hi[:, j % 2, 4 * b:4 * b + 4, :], turned_u, ACT.Copy).then_inc(u_hi, 1)
                    if copy is not None:
                        act.wait_ge(u_hi, 8 * g + (2 * j + b + 1))
                        if 4 * g + j >= 2:
                            act.wait_ge(u_lo, 8 * g + (2 * (j - 2) + b + 1))
                        act.activation(copy[:, j % 2, 4 * b:4 * b + 4, :], turned_u, ACT.Copy).then_inc(u_copied, 1)

            act.wait_ge(w_used, 31)
            for n in range(4 * SORTING + 1):
                if n < 4 * SORTING:
                    u_high(n // 4, n % 4, uT_pre[0], u_copy)
                if n >= 1:
                    m = n - 1
                    act.wait_ge(ex_a, m + 1)
                    if m >= 4:
                        act.wait_ge(gelu_stored[m % 4], 16 * (m // 4))
                    act.activation(gelu_pre[:, m % 4, :], bank(2 + m % 2), ACT.Gelu).then_inc(ex_gelu, 1)
                    act.wait_ge(ex_gelu, m + 1)
                    act.dma_start(gelu_dram[:, m // 4, m % 4, :], gelu_pre[:, m % 4, :]).then_inc(gelu_stored[m % 4], 16)
                if n == 4 * SORTING - 4:
                    act.wait_ge(gate_in, 1)
                    act.activation(pick_g, pick_g, ACT.Exp).then_inc(gate_exp, 1)
            for j in range(4):
                act.wait_ge(gelu_stored[j], 16 * SORTING)
            act.sem_inc(gate_out, 2)
            with act.Fori(0, NT) as i:
                for k in range(P // HB):
                    q = k // 4
                    act.wait_ge(gate_mm, i * 16 + (k + 5))
                    if k % 4 == 0:
                        act.wait_ge(gate_stored[q % 2], i * 32 + (16 * (q // 2) + 16))
                    at = HB * (k % 4)
                    act.activation(gate_block[q % 2][:, :, at:at + HB].rearrange("p n t -> p t n"),
                                   gate_banks(k), ACT.Copy).then_inc(gate_out, 1)

            def expert_tiles(g, par):
                group_summed(act, g)
                for j in range(4):
                    if j < 3:
                        u_high(g, j + 1)
                    act.wait_ge(ex_a, 4 * g + (j + 1))
                    act.wait_ge(ex_mul, 4 * g + max(j - 1, 0))
                    act.activation(gelu[:, j % 2, :], bank(2 + j % 2), ACT.Gelu).then_inc(ex_gelu, 1)
                    act.wait_ge(ex_mul, 4 * g + (j + 1))
                    act.activation(ex_hi[:, par, j, :], act_g[:, j % 2, :], ACT.Copy).then_inc(ex_hi_done, 1)

            def v_high(g, slot, rounds, s2):
                act.wait_ge(ring_in[slot], arrived(slot, rounds))
                group_summed(act, g)
                act.activation(split[:, s2, 0, :], ring[:, slot, :], ACT.Copy).then_inc(w_hi, 1)

            for n in range(5):
                if n < 4:
                    u_high(5, n)
                if n >= 1:
                    m = n - 1
                    act.wait_ge(ex_a, 4 * SORTING + m + 1)
                    if m >= 2:
                        act.wait_ge(late_stored[m % 2], 16)
                    act.activation(gelu[:, m % 2, :], bank(2 + m % 2), ACT.Gelu).then_inc(ex_gelu, 1)
                    act.wait_ge(ex_gelu, 4 * SORTING + m + 1)
                    act.dma_start(gelu_dram[:, 5, m, :], gelu[:, m % 2, :]).then_inc(late_stored[m % 2], 16)
                if n == 2:
                    act.wait_ge(gate_stored[0], 32 * NT + 16)
                    act.wait_ge(gate_stored[1], 32 * NT + 16)
                    v_high(0, *early_place(EARLY), 1)

            def early_high(g):
                group_summed(act, g)
                for j in range(4):
                    act.wait_ge(ex_mul, 4 * g + j + 1)
                    act.activation(ex_hi[:, g % 2, j, :], act_g[:, j % 2, :], ACT.Copy).then_inc(ex_hi_done, 1)

            for g in range(EARLY - 1):
                early_high(g)
                if g >= 1:
                    v_high(g, *early_place(EARLY + g), (g + 1) % 2)
            u_high(6, 0)
            early_high(5)
            v_high(5, 0, 12, 0)
            act.wait_ge(late_stored[0], 32)
            act.wait_ge(late_stored[1], 32)
            with act.Fori(0, 12) as i:
                expert_tiles(2 * i + 6, 0)
                u_high(2 * i + 7, 0)
                v_high(2 * i + 6, 2, i + 12, 1)
                expert_tiles(2 * i + 7, 1)
                u_high(2 * i + 8, 0)
                v_high(2 * i + 7, 0, i + 13, 0)
            expert_tiles(30, 0)
            u_high(31, 0)
            v_high(30, 2, 24, 1)
            expert_tiles(31, 1)
            v_high(31, 0, 25, 0)

            for t in range(NT):
                act.wait_ge(ex_add, 8 * (EX_GROUPS - 1) + 2 * t + 4)
                sum_squares(x_sb[:, t, :], ps[:, 6:8, :].rearrange("p a b -> p (a b)"), t)

        @block.tensor
        def _(pe):
            def turn(n, dst_bank, src):
                for t in range(NT):
                    mm = pe.transpose(bank(dst_bank)[:, t * P:(t + 1) * P], src(t), ident)
                mm.then_inc(turned, 1)

            pe.wait_ge(const_in, 16)
            pe.wait_ge(xn_done, NT)
            xn_k = xn1.rearrange("p t (c k) -> p t c k", k=KD)
            for k in range(KD):
                if k >= 2:
                    pe.wait_ge(turned_hi, k - 1)
                turn(k, k % 2, lambda t: xn_k[:, t, :, k])

            pe.wait_ge(turned_hi, KD)
            for n in range(16):
                p, r = divmod(n, 4)
                c = Z_ORDER[p]
                w = ring_chunk(p, z_width(c))
                if r == 0:
                    chunk_here(pe, p)
                if n >= 2:
                    pe.wait_ge(mm_out, n - 1)
                for k in range(KD):
                    if c == 0:
                        mm = pe.matmul(bank(2 + n % 2), w[:, k, r * P:(r + 1) * P], hT[:, k, :], start=k == 0, stop=k == KD - 1)
                    else:
                        mm = pe.matmul(bank(2 + n % 2)[:, 0:z_width(c)], hT[:, k, r * P:(r + 1) * P], w[:, k, :],
                                       start=k == 0, stop=k == KD - 1)
                mm.then_inc(mm_done, 1)
                if n == 3:
                    pe.wait_ge(small_in, 16 * SMALLS)
                    for f in range(4):
                        mm = pe.transpose(bank(4)[:, f * 8:f * 8 + 6], conv_rows[0:6, f * P:(f + 1) * P], ident[0:6, 0:6])
                    mm.then_inc(conv_turned, 1)
                if n == 8:
                    for f in range(2):
                        pe.wait_ge(qk_done, 3 + f)
                        for t in range(NT):
                            mm = pe.transpose(bank(f)[:, t * P:(t + 1) * P], qkT[:, 2 + f, t * P:(t + 1) * P], ident)
                        mm.then_inc(ktok_turned, 1)
                if n == 9:
                    pe.wait_ge(gates_padded, 4)
                    for kind in range(2):
                        for t in range(NT):
                            mm = pe.transpose(bank(5 + kind)[0:ROWS, t * P:(t + 1) * P], gate_pad[:, t, kind, 0:ROWS], ident)
                        mm.then_inc(gates_turned, 1)

            pe.wait_ge(rows_exp, 3)
            for i, r in enumerate((c_row, inter_row, em_row, w_row)):
                for c in range(NC):
                    mm = pe.transpose(bank(4 + i // 2)[:, ((i % 2) * NC + c) * ROWS:((i % 2) * NC + c + 1) * ROWS],
                                      r[0:ROWS, c * P:(c + 1) * P], ident[0:ROWS, 0:ROWS])
                mm.then_inc(cols_turned, 1)
            pe.wait_ge(rows_ready, 5)
            for d in range(2):
                for h in range(H):
                    r = 32 * d + h
                    mm = pe.matmul(bank(6)[:, (d * H + h) * NC:(d * H + h + 1) * NC], ident[0:ROWS, r:r + 1].to_broadcast([ROWS, P]),
                                   dec_rows[0:ROWS, :], start=True, stop=True)
            mm.then_inc(cols_turned, 1)

            def mlstm_scores(h):
                at = (h % 2) * DQK
                for c in range(NC):
                    mm = pe.matmul(bank(0)[:, c * P:(c + 1) * P], qkT[at:at + DQK, 2 + h // 2, c * P:(c + 1) * P],
                                   qkT[at:at + DQK, h // 2, c * P:(c + 1) * P], start=True, stop=True)
                for d in range(2):
                    r = 32 * d + h
                    mm = pe.matmul(bank(2 + d), ident[0:ROWS, r:r + 1].to_broadcast([ROWS, P]), negm_row[0:ROWS, :], start=True, stop=True)
                mm.then_inc(scores_done, 1)

            pe.wait_ge(mm_out, 16)
            pe.wait_ge(cols_done, 4)
            pe.wait_ge(ktok_done, 2)
            for h in range(H):
                at = (h % 2) * DQK
                mlstm_scores(h)
                pe.wait_ge(kdec_done, h + 1)
                for d in range(2):
                    for i in range(3):
                        c = i + d
                        pe.matmul(bank(6 + d)[at:at + DQK, i * 129:i * 129 + P], k_dec[:, d, i, :], v1[:, c, h * DV:(h + 1) * DV],
                                  start=True, stop=True)
                        mm = pe.matmul(bank(6 + d)[at:at + DQK, i * 129 + P:i * 129 + 129], k_dec[:, d, i, :], one_col,
                                       start=True, stop=True)
                mm.then_inc(kv_done, 1)
                pe.wait_ge(probs_done, 2 * h + 2)
                for d in range(2):
                    for c in range(NC):
                        pe.matmul(bank(4 + d)[:, c * P:(c + 1) * P], probs[:, h % 2, d, c, :], v1[:, c, h * DV:(h + 1) * DV],
                                  start=True, stop=True)
                        mm = pe.matmul(bank(1)[:, d * NC + c:d * NC + c + 1], probs[:, h % 2, d, c, :], one_col, start=True, stop=True)
                mm.then_inc(num_done, 1)
                pe.wait_ge(state_done, h + 1)
                for d in range(2):
                    for i in range(3):
                        c = i + 1 - d
                        mm = pe.matmul(bank(2 + d)[:, i * 129:(i + 1) * 129], qkT[at:at + DQK, h // 2, c * P:(c + 1) * P],
                                       state[at:at + DQK, d, i, 0:129], start=True, stop=True)
                mm.then_inc(inter_done, 1)
                if h < H - 1:
                    pe.wait_ge(head_read, h + 1)

            pe.wait_ge(pos_turned, 1)
            pe.transpose(bank(6)[:, 0:NT], pos_f[0:NT, :], ident[0:NT, 0:NT]).then_inc(pos_turned, 1)
            pe.wait_ge(latent_done, 2 * NT)
            cq_k = tail[:, :, C_CQ:C_CKV].rearrange("p t (c k) -> p t c k", k=2)
            turn(0, 0, lambda t: cq_k[:, t, :, 0])
            turn(1, 1, lambda t: cq_k[:, t, :, 1])
            turn(2, 4, lambda t: tail[:, t, C_CKV:C_KPE])

            w_uq = ring[:, 0, 0:1536].rearrange("p (k n) -> p k n", k=2)
            w_ukv = ring[:, 0, 1536:2560]

            def project(t):
                if t >= 1:
                    pe.wait_ge(qk_put, t)
                    pe.wait_ge(v_put, 2 * t)
                for b, (at, n) in enumerate(((0, 512), (512, 256))):
                    for k in range(2):
                        pe.matmul(bank(2 + b)[:, 0:n], cqT[:, k, t * P:(t + 1) * P], w_uq[:, k, at:at + n], start=k == 0, stop=k == 1)
                for b in range(2):
                    mm = pe.matmul(bank(4 + b), ckvT[:, t * P:(t + 1) * P], w_ukv[:, b * 512:(b + 1) * 512], start=True, stop=True)
                mm.then_inc(proj_done, 1)

            pe.wait_ge(turned_hi, TURN["latent"] + 3)
            chunk_here(pe, 4)
            project(0)
            for t in range(NT):
                if t < NT - 1:
                    project(t + 1)
                pe.wait_ge(qk_rotated, t + 1)
                if t >= 1:
                    pe.wait_ge(nope_out, 2 * t)
                    pe.wait_ge(rope_out, 2 * t)
                for i in range(2 * H):
                    pe.transpose(bank(i // H)[:, (i % H) * P:(i % H + 1) * P], qk_tok[:, t % 2, i, 0:A_NOPE], ident)
                    mm = pe.transpose(bank(6 + i // H)[0:A_ROPE, (i % H) * P:(i % H + 1) * P], rot[:, i, :], ident)
                mm.then_inc(qk_turned, 1)

            pe.wait_ge(nope_out, 2 * NT)
            pe.wait_ge(rope_out, 2 * NT)
            pe.wait_ge(v_put, 2 * NT)
            for i in range(H * NT + 2):
                if i < H * NT:
                    h, q = divmod(i, NT)
                    if i >= 2:
                        pe.wait_ge(att_exp, i - 1)
                    pe.matmul(bank(2 + i % 2), nopeT[:, h, q * P:(q + 1) * P], nopeT[:, H + h, :], start=True, stop=False)
                    pe.matmul(bank(2 + i % 2), ropeT[0:A_ROPE, h, q * P:(q + 1) * P], ropeT[0:A_ROPE, H + h, :],
                              start=False, stop=True).then_inc(att_scores, 1)
                if 1 <= i <= H * NT:
                    n = i - 1
                    pe.wait_ge(att_exp, n + 1)
                    if n >= 2:
                        pe.wait_ge(att_out, n - 1)
                    for k in range(NT):
                        mm = pe.transpose(bank(4 + n % 2)[:, k * P:(k + 1) * P], att[:, n % 2, k * P:(k + 1) * P], ident)
                    mm.then_inc(att_turned, 1)
                if i >= 2:
                    n = i - 2
                    h, q = divmod(n, NT)
                    pe.wait_ge(att_out, n + 1)
                    if n >= 2:
                        pe.wait_ge(att_norm, n - 1)
                    for k in range(NT):
                        mm = pe.matmul(bank(6 + n % 2)[:, 0:DV], attT[:, n % 2, k * P:(k + 1) * P], v2[:, k, h, :],
                                       start=k == 0, stop=k == NT - 1)
                    mm.then_inc(att_pv, 1)

            def turn_features(stage, src):
                src_k = src.rearrange("p t (c k) -> p t c k", k=KD)
                for k in range(KD):
                    if k >= 4:
                        pe.wait_ge(turned_lo, TURN_LO[stage] + k - 3)
                    turn(k, TURN_BANKS[k % 4], lambda t: src_k[:, t, :, k])

            def three_pass(dst, hi, lo, w_hi_, w_lo_, steps):
                terms = [(a, b, k) for a, b in ((hi, w_hi_), (hi, w_lo_), (lo, w_hi_)) for k in range(steps)]
                for n, (a, b, k) in enumerate(terms):
                    mm = pe.matmul(dst, a(k), b(k), start=n == 0, stop=n == len(terms) - 1)
                return mm

            def linear_chunk(s, done_before, feature_rows, hi=xT_hi, lo=xT_lo):
                pe.wait_ge(w_hi, s + 1)
                pe.wait_ge(w_lo, s + 1)
                wh, wl = high(s % 2, KD), low(s % 2, KD)
                for r in range(4):
                    n = done_before + r
                    pe.wait_ge(mm_out, n - 1)
                    at = slice(r * P, (r + 1) * P)
                    if feature_rows:
                        mm = three_pass(bank(2 + n % 2), lambda k: wh[:, k, at], lambda k: wl[:, k, at],
                                        lambda k: hi[:, k, :], lambda k: lo[:, k, :], KD)
                    else:
                        mm = three_pass(bank(2 + n % 2), lambda k: hi[:, k, at], lambda k: lo[:, k, at],
                                        lambda k: wh[:, k, :], lambda k: wl[:, k, :], KD)
                    mm.then_inc(mm_done, 1)
                pe.wait_ge(mm_done, done_before + 4)
                pe.sem_inc(w_used, 1)

            pe.wait_ge(y_ready, NT * H)
            pe.wait_ge(att_norm, H * NT)
            turn_features("out", y1)
            pe.wait_ge(turned_lo, TURN_LO["out"] + KD)
            for c in range(2):
                linear_chunk(S_OUT + c, MM["out"] + 4 * c, False)

            pe.wait_ge(xn_done, 2 * NT)
            turn_features("ffn", xn)
            pe.wait_ge(turned_lo, TURN_LO["ffn"] + KD)

            def ff_up(g, par, s, s2):
                pe.wait_ge(w_hi, s + 1)
                pe.wait_ge(w_lo, s + 1)
                wh = split[:, s2, 0, :].rearrange("p (k c j) -> p k c j", k=KD, j=4)
                wl = split[:, s2, 1, :].rearrange("p (k c j) -> p k c j", k=KD, j=4)
                for j in range(4):
                    pe.wait_ge(ff_relu, 4 * g + max(j - 1, 0))
                    three_pass(bank(2 + j % 2), lambda k: wh[:, k, :, j], lambda k: wl[:, k, :, j],
                               lambda k: xT_hi[:, k, :], lambda k: xT_lo[:, k, :], KD).then_inc(ff_a, 1)
                pe.wait_ge(ff_a, 4 * g + 4)
                pe.sem_inc(w_used, 1)

            def ff_down(g, par, s, s2):
                pe.wait_ge(w_hi, s + 1)
                pe.wait_ge(w_lo, s + 1)
                pe.wait_ge(ff_lo, 4 * g + 4)
                wh, wl = high(s2, 4), low(s2, 4)
                for b in range(8):
                    t, c = divmod(b, 2)
                    rows_, cols = slice(t * P, (t + 1) * P), slice(c * 512, (c + 1) * 512)
                    pe.wait_ge(ff_add, 8 * g + (b + 1))
                    three_pass(bank(4 + b % 2), lambda j: hid_hi[:, par, j, rows_], lambda j: hid_lo[:, par, j, rows_],
                               lambda j: wh[:, j, cols], lambda j: wl[:, j, cols], 4).then_inc(ff_b, 1)
                pe.wait_ge(ff_b, 8 * g + 8)
                pe.sem_inc(w_used, 1)

            ff_up(0, 0, 2, 0)
            with pe.Fori(0, 3) as i:
                ff_up(2 * i + 1, 1, 4 * i + 3, 1)
                ff_down(2 * i, 0, 4 * i + 4, 0)
                ff_up(2 * i + 2, 0, 4 * i + 5, 1)
                ff_down(2 * i + 1, 1, 4 * i + 6, 0)
            ff_up(7, 1, 15, 1)
            ff_down(6, 0, 16, 0)
            ff_down(7, 1, 17, 1)

            pe.wait_ge(xn_done, 3 * NT)
            turn_features("mix2", xn)
            pe.wait_ge(turned_lo, TURN_LO["mix2"] + KD)
            for c in range(7):
                linear_chunk(S_IN2 + c, MM["in2"] + 4 * c, c in (0, 1, 4, 5))

            pe.wait_ge(mm_out, MM["out2"])
            for i in range(H + 1):
                if i < H:
                    if i >= 1:
                        pe.wait_ge(ret_a, i)
                        pe.wait_ge(ret_kd, i)
                    for c in range(NC):
                        mm = pe.matmul(bank(0)[:, c * P:(c + 1) * P], rkT[:, i, c * P:(c + 1) * P], rqT[:, i, c * P:(c + 1) * P], start=True, stop=True)
                    mm.then_inc(ret_scores, 1)
                    for c in range(NC):
                        mm = pe.transpose(bank(1)[:, c * P:(c + 1) * P], rkT[:, i, c * P:(c + 1) * P], ident)
                    mm.then_inc(ret_kturned, 1)
                if i >= 1:
                    h = i - 1
                    pe.wait_ge(ret_a, h + 1)
                    pe.wait_ge(ret_qx, h + 1)
                    pe.wait_ge(ret_state, h + 1)
                    if h >= 1:
                        pe.wait_ge(ret_y, h)
                    for c in range(NC):
                        dst = bank(5)[:, c * P:(c + 1) * P]
                        mm = pe.matmul(dst, ret_in[:, h % 2, c, :], rv[:, c, h * DV:(h + 1) * DV], start=True, stop=c == 0)
                        if c >= 1:
                            mm = pe.matmul(dst, ret_q[:, h % 2, c, :], ret_s[:, c - 1, :], start=False, stop=True)
                    mm.then_inc(ret_o, 1)
                if i < H:
                    pe.wait_ge(ret_kd, i + 1)
                    if i >= 1:
                        pe.wait_ge(ret_state, i)
                    for c in range(NC - 1):
                        mm = pe.matmul(bank(4)[:, c * P:(c + 1) * P], ret_k[:, i % 2, c, :], rv[:, c, i * DV:(i + 1) * DV], start=True, stop=True)
                    mm.then_inc(ret_kv, 1)

            def dif_score(i):
                h, q = divmod(i, NT)
                if i >= 2:
                    pe.wait_ge(dif_max, 2 * (i - 1))
                for m in range(2):
                    at = slice(m * DIFF_D, (m + 1) * DIFF_D)
                    pe.matmul(bank(2 * (i % 2) + m)[:, 0:(q + 1) * P], dqT[at, h, q * P:(q + 1) * P], dkT[at, h, 0:(q + 1) * P],
                              start=True, stop=True).then_inc(dif_scores, 1)

            pe.wait_ge(ret_a, H)
            pe.wait_ge(ret_kd, H)
            dif_score(0)
            for i in range(H * NT + 2):
                if i + 1 < H * NT:
                    dif_score(i + 1)
                if 1 <= i <= H * NT:
                    n = i - 1
                    q = n % NT
                    pe.wait_ge(dif_probs, n + 1)
                    pe.wait_ge(ret_state, H)
                    pe.wait_ge(ret_y, H)
                    if n >= 2:
                        pe.wait_ge(dif_out, n - 1)
                    for k in range(q + 1):
                        mm = pe.transpose(bank(4 + n % 2)[:, k * P:(k + 1) * P], dif[:, n % 2, 0, k * P:(k + 1) * P], ident)
                    mm.then_inc(dif_turned, 1)
                if i >= 2:
                    n = i - 2
                    h, q = divmod(n, NT)
                    pe.wait_ge(dif_out, n + 1)
                    if n >= 2:
                        pe.wait_ge(dif_y, n - 1)
                    for k in range(q + 1):
                        mm = pe.matmul(bank(6 + n % 2)[:, 0:DV], difT[:, n % 2, k * P:(k + 1) * P], dv2[:, k, h, :], start=k == 0, stop=k == q)
                    mm.then_inc(dif_pv, 1)

            pe.wait_ge(y2_ready, 2 * NT * H)
            turn_features("out2", y2)
            pe.wait_ge(turned_lo, TURN_LO["out2"] + KD)
            for c in range(2):
                linear_chunk(S_OUT2 + c, MM["out2"] + 4 * c, False, y2T_hi, y2T_lo)

            pe.wait_ge(keys_in, 16)
            for b in range(4):
                if b >= 2:
                    pe.wait_ge(keys_out, b - 1)
                for i in range(4):
                    mm = pe.transpose(bank(4 + b % 2)[:, i * P:(i + 1) * P], keys[:, 4 * b + i, :], ident)
                mm.then_inc(keys_turned, 1)

            pe.wait_ge(xn_done, 4 * NT)
            pe.wait_ge(keys_out, 4)
            turn_features("peer", xn)
            pe.wait_ge(turned_lo, TURN_LO["peer"] + KD)
            def half_query(n):
                s = S_WQ + n // 4
                if n % 4 == 0:
                    pe.wait_ge(w_hi, s + 1)
                    pe.wait_ge(w_lo, s + 1)
                wh, wl = high(s % 2, KD), low(s % 2, KD)
                at = slice((n % 4) * P, (n % 4 + 1) * P)
                pe.wait_ge(mm_out, MM["wq"] + n - 1)
                three_pass(bank(2 + n % 2), lambda k: wh[:, k, at], lambda k: wl[:, k, at],
                           lambda k: xT_hi[:, k, :], lambda k: xT_lo[:, k, :], KD).then_inc(mm_done, 1)

            def scores_of(n):
                pe.wait_ge(mm_out, MM["wq"] + n + 1)
                if n == 0:
                    pe.wait_ge(keys_out, 4)
                if n >= 2:
                    pe.wait_ge(key_tops, n - 1)
                for t in range(NT):
                    mm = pe.matmul(bank(4 + n % 2)[:, t * P:(t + 1) * P], half_q[:, n % 2, t * P:(t + 1) * P], keysT[:, n, :],
                                   start=True, stop=True)
                mm.then_inc(key_scores, 1)

            for n in range(17):
                if n < 16:
                    half_query(n)
                if n >= 1:
                    scores_of(n - 1)
                if n % 4 == 3:
                    pe.wait_ge(mm_done, MM["wq"] + n + 1)
                    pe.sem_inc(w_used, 1)

            def u_turn(g, j, slot):
                u = ring[:, slot, j * D:(j + 1) * D].rearrange("p (c k) -> p c k", k=KD)
                for b in range(2):
                    if not isinstance(g, int) or 4 * g + j >= 2:
                        pe.wait_ge(u_lo, 8 * g + (2 * (j - 2) + b + 1))
                    for k in range(4):
                        mm = pe.transpose(bank((0, 6)[j % 2] + b)[:, k * P:(k + 1) * P], u[:, :, 4 * b + k], ident)
                    mm.then_inc(u_turned, 1)

            def expert_up(g, slot, uT=(uT_hi, uT_lo), next_slot=None):
                for j in range(4):
                    if j < 3:
                        u_turn(g, j + 1, slot)
                    elif next_slot is not None:
                        u_turn(g + 1, 0, next_slot)
                    pe.wait_ge(u_lo, 8 * g + (2 * j + 2))
                    if not isinstance(g, int) or 4 * g + j >= 2:
                        pe.wait_ge(ex_gelu, 4 * g + (j - 1))
                    three_pass(bank(2 + j % 2), lambda k: uT[0][:, j % 2, k, :], lambda k: uT[1][:, j % 2, k, :],
                               lambda k: xT_hi[:, k, :], lambda k: xT_lo[:, k, :], KD).then_inc(ex_a, 1)

            pe.wait_ge(ring_in[0], arrived(0, 9))
            u_turn(0, 0, 0)
            for g in range(SORTING):
                slot, rounds = early_place(g + 1)
                if g + 1 < SORTING:
                    pe.wait_ge(ring_in[slot], arrived(slot, rounds))
                expert_up(g, g % RING, uT_pre, slot if g + 1 < SORTING else None)

            pe.wait_ge(u_lo, 8 * SORTING)
            for i, src in enumerate((pick_1, pick_2, pick_g)):
                pe.wait_ge(picks_ready, i + 1)
                for t in range(NT):
                    mm = pe.transpose(bank((7, 4, 6)[i])[:, t * P:(t + 1) * P], src[:, t, :], ident)
                mm.then_inc(picks_turned, 1)

            pe.sem_inc(gate_mm, 4)
            with pe.Fori(0, NT) as i:
                for k in range(P // HB):
                    pe.wait_ge(hot_hi_done, i * 16 + (k + 1))
                    pe.wait_ge(hot_lo_done, i * 16 + (k + 1))
                    pe.wait_ge(gate_out, i * 16 + (k + 1))
                    for t in range(HB):
                        dst = gate_banks(k)[:, t, :]
                        pe.matmul(dst, hot_1[:, k % 4, :, t], hot_hi[:, k % 4, :, t], start=True, stop=False)
                        mm = pe.matmul(dst, hot_1[:, k % 4, :, t], hot_lo[:, k % 4, :, t], start=False, stop=True)
                    mm.then_inc(gate_mm, 1)

            def expert_down(g, par, s2):
                pe.wait_ge(w_hi, g + (S_EX + 1))
                pe.wait_ge(w_lo, g + (S_EX + 1))
                pe.wait_ge(ex_lo_done, 4 * g + 4)
                wh, wl = high(s2, 4), low(s2, 4)
                for b in range(8):
                    t, c = divmod(b, 2)
                    rows_, cols = slice(t * P, (t + 1) * P), slice(c * 512, (c + 1) * 512)
                    pe.wait_ge(ex_add, 8 * g + (b + 1))
                    three_pass(bank(4 + b % 2), lambda j: ex_hi[:, par, j, rows_], lambda j: ex_lo[:, par, j, rows_],
                               lambda j: wh[:, j, cols], lambda j: wl[:, j, cols], 4).then_inc(ex_b, 1)

            pe.sem_inc(ex_b, 1)
            pe.wait_ge(gate_out, 16 * NT + 2)
            slot, rounds = early_place(SORTING)
            pe.wait_ge(ring_in[slot], arrived(slot, rounds))
            u_turn(SORTING, 0, slot)
            expert_up(SORTING, slot)
            for g in range(4):
                expert_down(g, g % 2, (g + 1) % 2)
            pe.wait_ge(ring_in[3], arrived(3, 11))
            u_turn(6, 0, 3)
            expert_down(4, 0, 1)
            with pe.Fori(0, 12) as i:
                expert_up(2 * i + 6, 3)
                pe.wait_ge(ring_in[1], i * 16 + arrived(1, 12))
                u_turn(2 * i + 7, 0, 1)
                expert_down(2 * i + 5, 1, 0)
                expert_up(2 * i + 7, 1)
                pe.wait_ge(ring_in[3], i * 16 + arrived(3, 12))
                u_turn(2 * i + 8, 0, 3)
                expert_down(2 * i + 6, 0, 1)
            expert_up(30, 3)
            pe.wait_ge(ring_in[1], arrived(1, 24))
            u_turn(31, 0, 1)
            expert_down(29, 1, 0)
            expert_up(31, 1)
            expert_down(30, 0, 1)
            expert_down(31, 1, 0)

        @block.vector
        def _(dve):
            own = Steps(dve, own_v)
            dve.wait_ge(rstd_done, 1)
            for t in range(NT):
                dve.tensor_scalar(xn1[:, t, :], x_sb[:, t, :], rstd[:, t:t + 1], None, ALU.mult).then_inc(xn_done, 1)

            for n in range(8):
                dve.wait_ge(mm_done, n + 1)
                dve.tensor_copy(z_place(n), bank(2 + n % 2)[:, 0:z_width(Z_ORDER[n // 4])]).then_inc(mm_out, 1)
                if n == 3:
                    dve.wait_ge(conv_turned, 1)
                    own.did(dve.tensor_copy(conv_w[:, :, 0:6], bank(4)[:, 0:32].rearrange("p (f t) -> p f t", f=4)[:, :, 0:6]))
                    own.wait()
                    dve.wait_ge(mm_out, 4)
                if 3 <= n < 7:
                    f = n - 3
                    own.did(dve.tensor_scalar(qkT[:, f, :], conv_in[:, f, 0:T], conv_w[:, f, 0:1], conv_w[:, f, 5:6], ALU.mult, ALU.add))
                    for i in range(1, TAPS):
                        own.wait()
                        step = dve.scalar_tensor_tensor(qkT[:, f, :], conv_in[:, f, i:i + T], conv_w[:, f, i:i + 1], qkT[:, f, :], ALU.mult, ALU.add)
                        if i < TAPS - 1:
                            own.did(step)
                        else:
                            step.then_inc(conv_done, 1)

            dve.wait_ge(mm_out, 8)
            for d in range(2):
                for kind in range(2):
                    at = (2 * d + kind) * H
                    dve.tensor_tensor(gate_pad[:, :, kind, 32 * d:32 * d + H], tail[:, :, at:at + H],
                                      gate_bias[:, at:at + H].unsqueeze(1).to_broadcast([P, NT, H]), ALU.add).then_inc(gates_padded, 1)
            R = slice(0, ROWS)
            DIR = (slice(0, H), slice(32, 32 + H))
            dve.wait_ge(gates_turned, 2)
            own.did(dve.tensor_copy(lf_row[R, :], bank(6)[R, :]))
            own.wait()
            dve.scalar_tensor_tensor(u_row[R, :], lf_row[R, :], -1.0, lf_row[R, :], ALU.mult, ALU.min).then_inc(f_neg, 1)
            dve.wait_ge(f_log, 1)
            own.did(dve.scalar_tensor_tensor(lf_row[R, :], lf_row[R, :], 0.0, t_row[R, :], ALU.min, ALU.subtract))
            own.wait()
            own.did(dve.memset(b_row[R, :], 0.0))
            own.wait()
            for d in range(2):
                for c in range(NC):
                    s = slice(c * P, (c + 1) * P)
                    rev = (lambda a: a) if d == 0 else (lambda a: a[:, ::-1])
                    own.did(dve.tensor_tensor_scan(rev(b_row[DIR[d], s]), ones[DIR[d], :], rev(lf_row[DIR[d], s]), 0.0, ALU.mult, ALU.add))
            own.wait()
            own.did(dve.tensor_tensor(c_row[R, :], bank(5)[R, :], b_row[R, :], ALU.subtract))
            own.did(dve.memset(m_row[R, :], 0.0))
            own.wait()
            for i in range(NC):
                for d in range(2):
                    c = i if d == 0 else NC - 1 - i
                    s = slice(c * P, (c + 1) * P)
                    rev = (lambda a: a) if d == 0 else (lambda a: a[:, ::-1])
                    own.did(dve.tensor_tensor_scan(rev(m_row[DIR[d], s]), rev(c_row[DIR[d], s]), rev(c_row[DIR[d], s]),
                                                   prev_max[DIR[d], c:c + 1], ALU.max, ALU.max))
                own.wait()
                if i < NC - 1:
                    for d in range(2):
                        c = i if d == 0 else NC - 1 - i
                        last = c * P + (P - 1 if d == 0 else 0)
                        nxt = c + 1 if d == 0 else c - 1
                        own.did(dve.tensor_tensor(prev_max[DIR[d], nxt:nxt + 1], b_row[DIR[d], last:last + 1], m_row[DIR[d], last:last + 1], ALU.add))
                    own.wait()
            dve.tensor_scalar(negm_row[R, :], m_row[R, :], -1.0, None, ALU.mult).then_inc(rows_ready, 1)
            for c in range(NC):
                s = slice(c * P, (c + 1) * P)
                step = dve.tensor_scalar(inter_row[R, s], m_row[R, s], -1.0, prev_max[R, c:c + 1], ALU.mult, ALU.add)
                if c < NC - 1:
                    own.did(step)
                else:
                    step.then_inc(rows_ready, 1)
            dve.wait_ge(rows_ready, 1)
            dve.tensor_tensor(em_row[R, :], negm_row[R, :], b_row[R, :], ALU.subtract).then_inc(rows_ready, 1)
            own.did(dve.memset(w_row[R, :], 0.0))
            own.wait()
            for d in range(2):
                for c in range(NC):
                    s = slice(c * P, (c + 1) * P)
                    last = c * P + (P - 1 if d == 0 else 0)
                    step = dve.tensor_scalar(w_row[DIR[d], s], c_row[DIR[d], s], m_row[DIR[d], last:last + 1], None, ALU.subtract)
                    if (d, c) != (1, NC - 1):
                        own.did(step)
                    else:
                        step.then_inc(rows_ready, 1)
            dve.wait_ge(rows_exp, 1)
            own.did(dve.tensor_copy(dec_rows[DIR[0], :], inter_row[DIR[0], P - 1:T:P]))
            dve.tensor_copy(dec_rows[DIR[1], :], inter_row[DIR[1], 0:T:P]).then_inc(rows_ready, 1)
            dve.wait_ge(rstd_done, 2)
            for t in range(NT):
                dve.tensor_scalar(tail[:, t, C_CQ:C_CKV], tail[:, t, C_CQ:C_CKV], rstd[:, 16 + t:17 + t], None, ALU.mult).then_inc(latent_done, 1)
                dve.tensor_scalar(tail[:, t, C_CKV:C_KPE], tail[:, t, C_CKV:C_KPE], rstd[:, 20 + t:21 + t], None, ALU.mult).then_inc(latent_done, 1)
            dve.wait_ge(cols_turned, 5)
            w = NC * ROWS
            dve.tensor_copy(gate_cols[:, 0, :, :], bank(4)[:, 0:w].rearrange("p (c r) -> p c r", c=NC)).then_inc(cols_done, 1)
            dve.tensor_scalar(gate_cols[:, 1, :, :], bank(4)[:, w:2 * w].rearrange("p (c r) -> p c r", c=NC), DQK ** -0.5, None, ALU.mult).then_inc(cols_done, 1)
            dve.tensor_copy(gate_cols[:, 2:4, :, :], bank(5)[:, 0:2 * w].rearrange("p (a c r) -> p a c r", a=2, c=NC)).then_inc(cols_done, 1)
            dve.tensor_copy(dec_cols, bank(6)[:, 0:32].rearrange("p (a b) -> p a b", a=8)).then_inc(cols_done, 1)
            dve.wait_ge(cols_done, 4)
            dve.wait_ge(ktok_done, 2)

            for h in range(H):
                at = (h % 2) * DQK
                dirs = (h, 32 + h)
                if h >= 1:
                    dve.wait_ge(kv_done, h)
                for d in range(2):
                    for i in range(3):
                        step = dve.tensor_scalar(k_dec[:, d, i, :], k_tok[:, i + d, h * DQK:(h + 1) * DQK],
                                                 gate_cols[:, 3, i + d, dirs[d]:dirs[d] + 1], None, ALU.mult)
                step.then_inc(kdec_done, 1)
                dve.wait_ge(scores_done, h + 1)
                for d in range(2):
                    for c in range(NC):
                        step = dve.scalar_tensor_tensor(decay[:, h % 2, d, c * P:(c + 1) * P], bank(2 + d)[:, c * P:(c + 1) * P],
                                                        gate_cols[:, 0, c, dirs[d]:dirs[d] + 1], mask[d], ALU.add, ALU.add)
                step.then_inc(decay_in, 1)
                dve.wait_ge(kv_done, h + 1)
                if h >= 1:
                    dve.wait_ge(inter_done, h)
                for i in range(3):
                    for d in range(2):
                        j = i if d == 0 else 2 - i
                        src = bank(6 + d)[at:at + DQK, j * 129:(j + 1) * 129]
                        dst = state[at:at + DQK, d, j, 0:129]
                        if i == 0:
                            step = dve.tensor_copy(dst, src)
                        else:
                            before = j - 1 if d == 0 else j + 1
                            chunk = j if d == 0 else j + 1
                            step = dve.scalar_tensor_tensor(dst, state[at:at + DQK, d, before, 0:129],
                                                            dec_cols[at:at + DQK, d * H + h, chunk:chunk + 1], src, ALU.mult, ALU.add)
                        if (i, d) == (2, 1):
                            step.then_inc(state_done, 1)
                        else:
                            own.did(step)
                    if i < 2:
                        own.wait()
                dve.wait_ge(decay_exp, h + 1)
                for d in range(2):
                    dve.scalar_tensor_tensor(probs[:, h % 2, d, :, :].rearrange("p c t -> p (c t)"), bank(0), DQK ** -0.5, decay[:, h % 2, d, :],
                                             ALU.mult, ALU.mult).then_inc(probs_done, 1)
                dve.wait_ge(num_out, 2 * h + 2)
                dve.wait_ge(num_done, h + 1)
                own.did(dve.tensor_copy(den, bank(1)[:, 0:8].rearrange("p (a b) -> p a b", a=2)))
                dve.wait_ge(inter_done, h + 1)
                for d in range(2):
                    first = 1 - d
                    inter = bank(2 + d)[:, 0:387].rearrange("p (i v) -> p i v", i=3)
                    col = gate_cols[:, 1, :, dirs[d]]
                    own.did(dve.tensor_tensor(den_t[:, d, first:first + 3], inter[:, :, P], col[:, first:first + 3], ALU.mult))
                    for i in range(3):
                        c = i + first
                        step = dve.scalar_tensor_tensor(num[:, d, c, :], inter[:, i, 0:P], gate_cols[:, 1, c, dirs[d]:dirs[d] + 1],
                                                        num[:, d, c, :], ALU.mult, ALU.add)
                        if (d, i) == (1, 2):
                            step.then_inc(head_read, 1)
                        else:
                            own.did(step)
                own.wait()
                dve.wait_ge(head_read, h + 1)
                for d in range(2):
                    first = 1 - d
                    own.did(dve.tensor_tensor(den[:, d, first:first + 3], den[:, d, first:first + 3], den_t[:, d, first:first + 3], ALU.add))
                own.wait()
                own.did(dve.scalar_tensor_tensor(den_t, den, -1.0, den, ALU.mult, ALU.max))
                own.wait()
                for d in range(2):
                    own.did(dve.tensor_tensor(den_t[:, d, :], den_t[:, d, :], gate_cols[:, 2, :, dirs[d]], ALU.max))
                own.wait()
                own.did(dve.reciprocal(den_r, den_t))
                own.wait()
                for c in range(NC):
                    own.did(dve.tensor_scalar(y1[:, c, h * DV:(h + 1) * DV], num[:, 0, c, :], den_r[:, 0, c:c + 1], None, ALU.mult))
                own.wait()
                for c in range(NC):
                    step = dve.scalar_tensor_tensor(y1[:, c, h * DV:(h + 1) * DV], num[:, 1, c, :], den_r[:, 1, c:c + 1],
                                                    y1[:, c, h * DV:(h + 1) * DV], ALU.mult, ALU.add)
                step.then_inc(head_out, 1)
            dve.wait_ge(small_in, 16 * SMALLS)
            dve.tensor_copy(pos_f[0:NT, :], pos_rows[0:NT, :].bitcast(I32)).then_inc(pos_turned, 1)
            dve.wait_ge(pos_turned, 2)
            own.did(dve.tensor_copy(pos, bank(6)[:, 0:NT]))
            own.wait()
            for t in range(NT):
                own.did(dve.tensor_scalar(angle[:, t, :], const("inv_freq"), pos[:, t:t + 1], None, ALU.mult))
            own.wait()
            own.did(dve.tensor_scalar(turns, angle, float(1.0 / (2.0 * np.pi)), ROUND, ALU.mult, ALU.add))
            own.wait()
            own.did(dve.tensor_scalar(turns, turns, ROUND, None, ALU.subtract))
            for c in (TWO_PI_A, TWO_PI_B, TWO_PI_C):
                own.wait()
                own.did(dve.scalar_tensor_tensor(angle, turns, -c, angle, ALU.mult, ALU.add))
            own.wait()
            own.did(dve.tensor_scalar(angle_c, angle, float(np.pi / 2), None, ALU.add))
            own.wait()
            own.did(dve.tensor_scalar(turns, angle_c, float(np.pi), None, ALU.is_gt))
            own.wait()
            own.did(dve.scalar_tensor_tensor(angle_c, turns, float(-2.0 * np.pi), angle_c, ALU.mult, ALU.add))
            own.wait()
            PI_IN = 3.1415925
            dve.tensor_scalar(angle, angle, PI_IN, -PI_IN, ALU.min, ALU.max).then_inc(angles, 1)
            dve.tensor_scalar(angle_c, angle_c, PI_IN, -PI_IN, ALU.min, ALU.max).then_inc(angles, 1)

            dve.wait_ge(rstd_done, 3)
            dve.wait_ge(o_sig, 1)
            for t in range(NT):
                for h in range(H):
                    v = slice(h * DV, (h + 1) * DV)
                    dve.scalar_tensor_tensor(y1[:, t, v], y1[:, t, v], rstd[:, t * H + h:t * H + h + 1], o1[:, t, v],
                                             ALU.mult, ALU.mult).then_inc(y_ready, 1)

            for t in range(NT):
                qk = qk_tok[:, t % 2, :, :]
                q_flat = qk[:, 0:H, :].rearrange("p h n -> p (h n)")
                dve.wait_ge(proj_done, t + 1)
                if t >= 2:
                    dve.wait_ge(qk_turned, t - 1)
                own.did(dve.tensor_copy(q_flat[:, 0:512], bank(2)))
                own.did(dve.tensor_copy(q_flat[:, 512:768], bank(3)[:, 0:256]))
                own.did(dve.tensor_copy(qk[:, H:H + 2, 0:A_NOPE], bank(4).rearrange("p (h n) -> p h n", h=2)[:, :, 0:A_NOPE]))
                dve.tensor_copy(qk[:, H + 2:2 * H, 0:A_NOPE], bank(5).rearrange("p (h n) -> p h n", h=2)[:, :, 0:A_NOPE]).then_inc(qk_put, 1)
                dve.wait_ge(qk_squared, t + 1)
                dve.tensor_reduce(qk_sumsq[:, t, :], qk_sq, AX.X, ALU.add).then_inc(qk_summed, 1)
                dve.wait_ge(qk_rstd_done, t + 1)
                own.did(dve.tensor_tensor(qk, qk, qk_rstd[:, t, :].unsqueeze(2).to_broadcast([P, 2 * H, A_DH]), ALU.mult))
                own.wait()
                r4 = qk.rearrange("p (a h) n -> p a h n", a=2)[:, :, :, A_NOPE:]
                own.did(dve.tensor_tensor(r4, r4, rope_gain.unsqueeze(2).to_broadcast([P, 2, H, A_ROPE]), ALU.mult))
                own.wait()
                if t == 0:
                    dve.wait_ge(rotary, 2)
                if t >= 1:
                    dve.wait_ge(qk_turned, t)
                half = A_ROPE // 2
                cs = cos_t[:, t, :].unsqueeze(1).to_broadcast([P, 2 * H, half])
                sn = sin_t[:, t, :].unsqueeze(1).to_broadcast([P, 2 * H, half])
                x1, x2 = qk[:, :, A_NOPE:A_NOPE + half], qk[:, :, A_NOPE + half:]
                own.did(dve.tensor_tensor(rot[:, :, 0:half], x1, cs, ALU.mult))
                own.did(dve.tensor_tensor(rot_t, x2, sn, ALU.mult))
                own.did(dve.tensor_tensor(rot[:, :, half:], x2, cs, ALU.mult))
                own.wait()
                own.did(dve.tensor_tensor(rot[:, :, 0:half], rot[:, :, 0:half], rot_t, ALU.subtract))
                own.wait()
                own.did(dve.tensor_tensor(rot_t, x1, sn, ALU.mult))
                own.wait()
                dve.tensor_tensor(rot[:, :, half:], rot[:, :, half:], rot_t, ALU.add).then_inc(qk_rotated, 1)
                dve.wait_ge(qk_turned, t + 1)
                for b in range(2):
                    dve.tensor_copy(ropeT[0:A_ROPE, b * H:(b + 1) * H, t * P:(t + 1) * P],
                                    bank(6 + b)[0:A_ROPE, :].rearrange("p (h n) -> p h n", h=H)).then_inc(rope_out, 1)

            for i in range(H * NT + 2):
                if i < H * NT:
                    dve.wait_ge(att_scores, i + 1)
                    own.did(dve.tensor_reduce(row_max[:, i:i + 1], bank(2 + i % 2), AX.X, ALU.max))
                    own.wait()
                    dve.tensor_scalar(row_nmax[:, i:i + 1], row_max[:, i:i + 1], -(A_DH ** -0.5), None, ALU.mult).then_inc(att_max, 1)
                if 1 <= i <= H * NT:
                    n = i - 1
                    dve.wait_ge(att_turned, n + 1)
                    if n >= 2:
                        dve.wait_ge(att_pv, n - 1)
                    dve.tensor_copy(attT[:, n % 2, :], bank(4 + n % 2)).then_inc(att_out, 1)
                if i >= 2:
                    n = i - 2
                    h, q = divmod(n, NT)
                    own.did(dve.reciprocal(row_inv[:, n:n + 1], row_sum[:, n:n + 1]))
                    dve.wait_ge(att_pv, n + 1)
                    own.wait()
                    dve.tensor_scalar(y1[:, q, 512 + h * DV:512 + (h + 1) * DV], bank(6 + n % 2)[:, 0:DV],
                                      row_inv[:, n:n + 1], None, ALU.mult).then_inc(att_norm, 1)

            def turned_low(stage, gain, hi=xT_hi, lo=xT_lo):
                for k in range(KD):
                    dve.wait_ge(turned_hi, TURN[stage] + k + 1)
                    dve.scalar_tensor_tensor(lo[:, k, :], bank(TURN_BANKS[k % 4]), gains[:, gain + k:gain + k + 1], hi[:, k, :],
                                             ALU.mult, ALU.subtract).then_inc(turned_lo, 1)

            def add_linear(done_before):
                for n in range(8):
                    c, t = divmod(n, NT)
                    dve.wait_ge(mm_done, done_before + n + 1)
                    dst = x_sb[:, t, c * CW:(c + 1) * CW]
                    dve.tensor_tensor(dst, bank(2 + (done_before + n) % 2), dst, ALU.add).then_inc(mm_out, 1)

            def norm_rows(rstd_count):
                dve.wait_ge(rstd_done, rstd_count)
                for t in range(NT):
                    dve.tensor_scalar(xn[:, t, :], x_sb[:, t, :], rstd[:, t:t + 1], None, ALU.mult).then_inc(xn_done, 1)

            turned_low("out", G_Y1)
            add_linear(MM["out"])
            norm_rows(4)
            turned_low("ffn", G_FFN)

            def ff_square(g, par):
                for j in range(4):
                    dve.wait_ge(ff_a, 4 * g + j + 1)
                    dve.tensor_scalar(relu[:, j % 2, :], bank(2 + j % 2), 0.0, None, ALU.max).then_inc(ff_relu, 1)
                    dve.wait_ge(ff_relu, 4 * g + j + 1)
                    dve.tensor_tensor(hid[:, j % 2, :], relu[:, j % 2, :], relu[:, j % 2, :], ALU.mult).then_inc(ff_sq, 1)
                    dve.wait_ge(ff_sq, 4 * g + j + 1)
                    dve.wait_ge(ff_hi, 4 * g + j + 1)
                    dve.tensor_tensor(hid_lo[:, par, j, :], hid[:, j % 2, :], hid_hi[:, par, j, :], ALU.subtract).then_inc(ff_lo, 1)

            def ff_accumulate(g):
                for b in range(8):
                    t, c = divmod(b, 2)
                    dve.wait_ge(ff_b, 8 * g + b + 1)
                    dst = x_sb[:, t, c * 512:(c + 1) * 512]
                    dve.tensor_tensor(dst, bank(4 + b % 2), dst, ALU.add).then_inc(ff_add, 1)

            dve.sem_inc(ff_add, 2)
            ff_square(0, 0)
            with dve.Fori(0, 3) as i:
                ff_square(2 * i + 1, 1)
                ff_accumulate(2 * i)
                ff_square(2 * i + 2, 0)
                ff_accumulate(2 * i + 1)
            ff_square(7, 1)
            ff_accumulate(6)
            ff_accumulate(7)

            own.did(dve.tensor_scalar(gains[64:P, G_Y2:G_Y2 + KD], gains[64:P, G_Y2:G_Y2 + KD], 1.0 - LAMBDA_INIT, None, ALU.mult))
            own.wait()
            norm_rows(5)
            turned_low("mix2", G_MIX2)
            for n in range(28):
                c, r = divmod(n, 4)
                dve.wait_ge(mm_done, MM["in2"] + n + 1)
                src = bank(2 + n % 2)
                dst = (rqT[:, r, :], rkT[:, r, :], rv[:, r, :], rg[:, r, :], dqT[:, r, :], dkT[:, r, :],
                       dv2[:, r, :, :].rearrange("p h v -> p (h v)"))[c]
                if c == 4:
                    step = dve.tensor_scalar(dst, src, DIFF_D ** -0.5, None, ALU.mult)
                else:
                    step = dve.tensor_copy(dst, src)
                step.then_inc(mm_out, 1)

            intra = const("intra", h=H, i=P)
            for i in range(H + 1):
                if i < H:
                    dve.wait_ge(ret_scores, i + 1)
                    if i >= 2:
                        dve.wait_ge(ret_o, i - 1)
                    dve.tensor_tensor(ret_in[:, i % 2, :, :], bank(0).rearrange("p (c i) -> p c i", c=NC),
                                      intra[:, i, :].unsqueeze(1).to_broadcast([P, NC, P]), ALU.mult).then_inc(ret_a, 1)
                if i >= 1:
                    dve.wait_ge(ret_o, i)
                    dve.tensor_copy(y2[:, :, (i - 1) * DV:i * DV], bank(5).rearrange("p (t v) -> p t v", t=NT)).then_inc(ret_y, 1)
                if i < H:
                    dve.wait_ge(ret_kv, i + 1)
                    own.did(dve.tensor_copy(ret_s[:, 0, :], bank(4)[:, 0:P]))
                    own.wait()
                    own.did(dve.scalar_tensor_tensor(ret_s[:, 1, :], ret_s[:, 0, :], CDEC[i], bank(4)[:, P:2 * P], ALU.mult, ALU.add))
                    own.wait()
                    dve.scalar_tensor_tensor(ret_s[:, 2, :], ret_s[:, 1, :], CDEC[i], bank(4)[:, 2 * P:3 * P], ALU.mult, ALU.add).then_inc(ret_state, 1)

            own.did(dve.tensor_tensor(lam_t, lam_in[:, 0:4:2, :], lam_in[:, 1:4:2, :], ALU.mult))
            own.wait()
            dve.tensor_reduce(lam[:, 0:2], lam_t, AX.X, ALU.add).then_inc(lam_sums, 1)
            dve.wait_ge(lam_exp, 1)
            own.did(dve.tensor_tensor(lam[:, 4:5], lam[:, 3:4], lam[:, 2:3], ALU.subtract))
            own.wait()
            own.did(dve.tensor_scalar(lam[:, 5:6], lam[:, 4:5], -LAMBDA_INIT, None, ALU.add))

            negdist = const("negdist")
            for i in range(H * NT + 3):
                if i < H * NT:
                    h, q = divmod(i, NT)
                    n_keys = (q + 1) * P
                    if i >= 2:
                        dve.wait_ge(dif_turned, i - 1)
                    for m in range(2):
                        dve.wait_ge(dif_scores, 2 * i + m + 1)
                        own.did(dve.scalar_tensor_tensor(dif[:, i % 2, m, 0:n_keys], negdist[:, T - n_keys:T], SLOPES[h],
                                                         bank(2 * (i % 2) + m)[:, 0:n_keys], ALU.mult, ALU.add))
                    own.wait()
                    for m in range(2):
                        own.did(dve.tensor_reduce(row_max[:, 2 * i + m:2 * i + m + 1], dif[:, i % 2, m, 0:n_keys], AX.X, ALU.max))
                    own.wait()
                    for m in range(2):
                        dve.tensor_scalar(row_nmax[:, 2 * i + m:2 * i + m + 1], row_max[:, 2 * i + m:2 * i + m + 1], -1.0, None, ALU.mult).then_inc(dif_max, 1)
                if 1 <= i <= H * NT:
                    n = i - 1
                    n_keys = (n % NT + 1) * P
                    dve.wait_ge(dif_exp, 2 * n + 2)
                    own.did(dve.reciprocal(row_inv[:, 2 * n:2 * n + 2], row_sum[:, 2 * n:2 * n + 2]))
                    own.wait()
                    own.did(dve.tensor_tensor(row_inv[:, 2 * n + 1:2 * n + 2], row_inv[:, 2 * n + 1:2 * n + 2], lam[:, 5:6], ALU.mult))
                    own.did(dve.tensor_scalar(dif[:, n % 2, 0, 0:n_keys], dif[:, n % 2, 0, 0:n_keys], row_inv[:, 2 * n:2 * n + 1], None, ALU.mult))
                    own.wait()
                    dve.scalar_tensor_tensor(dif[:, n % 2, 0, 0:n_keys], dif[:, n % 2, 1, 0:n_keys], row_inv[:, 2 * n + 1:2 * n + 2],
                                             dif[:, n % 2, 0, 0:n_keys], ALU.mult, ALU.add).then_inc(dif_probs, 1)
                if 2 <= i <= H * NT + 1:
                    n = i - 2
                    n_keys = (n % NT + 1) * P
                    dve.wait_ge(dif_turned, n + 1)
                    if n >= 2:
                        dve.wait_ge(dif_pv, n - 1)
                    dve.tensor_copy(difT[:, n % 2, 0:n_keys], bank(4 + n % 2)[:, 0:n_keys]).then_inc(dif_out, 1)
                if i >= 3:
                    n = i - 3
                    h, q = divmod(n, NT)
                    dve.wait_ge(dif_pv, n + 1)
                    dve.tensor_copy(y2[:, q, 512 + h * DV:512 + (h + 1) * DV], bank(6 + n % 2)[:, 0:DV]).then_inc(dif_y, 1)
                if i == 2:
                    dve.wait_ge(rstd_done, 6)
                    dve.wait_ge(rg_silu, 1)
                    for t in range(NT):
                        for h in range(H):
                            v = slice(h * DV, (h + 1) * DV)
                            dve.scalar_tensor_tensor(y2[:, t, v], y2[:, t, v], rstd[:, t * H + h:t * H + h + 1], rg[:, t, v],
                                                     ALU.mult, ALU.mult).then_inc(y2_ready, 1)
            dve.wait_ge(rstd_done, 7)
            for t in range(NT):
                for h in range(H):
                    v = slice(512 + h * DV, 512 + (h + 1) * DV)
                    dve.tensor_scalar(y2[:, t, v], y2[:, t, v], rstd[:, 16 + t * H + h:17 + t * H + h], None, ALU.mult).then_inc(y2_ready, 1)
            turned_low("out2", G_Y2, y2T_hi, y2T_lo)
            add_linear(MM["out2"])

            norm_rows(8)
            turned_low("peer", G_FFN2)

            def top16(values, best, index, rest, groups, wait_for, signal):
                dve.wait_ge(*wait_for)
                for g in range(groups):
                    own.did(dve.max(best(g)[:, 0:8], values(g)))
                own.wait()
                for g in range(groups):
                    own.did(dve.max_index(index(g)[:, 0:8], best(g)[:, 0:8], values(g)))
                    own.did(dve.match_replace(rest(g), best(g)[:, 0:8], values(g), -3e38))
                own.wait()
                for g in range(groups):
                    own.did(dve.max(best(g)[:, 8:16], rest(g)))
                own.wait()
                for g in range(groups):
                    step = dve.max_index(index(g)[:, 8:16], best(g)[:, 8:16], rest(g))
                step.then_inc(signal, 1)

            for n in range(2 * P_HEADS):
                if n >= 1:
                    dve.wait_ge(key_tops, n)
                top16(lambda t: bank(4 + n % 2)[:, t * P:(t + 1) * P], lambda t: top_v[:, t, n, :], lambda t: top_i[:, t, n, :],
                      lambda t: masked[:, t, 0:P], NT, (key_scores, n + 1), key_tops)
            dve.wait_ge(key_tops, 2 * P_HEADS)
            own.did(dve.tensor_copy(top_f, top_i))
            for t in range(NT):
                for half in range(2):
                    g0 = 4 * half
                    if t or half:
                        dve.wait_ge(picks_top, 2 * t + half)
                    top16(lambda g: cand[:, t % 2, g0 + g, :, :].rearrange("p a b -> p (a b)"), lambda g: pick_v[:, t, g0 + g, :],
                          lambda g: pick_i[:, t, g0 + g, :], lambda g: masked[:, g, :], 4, (cands, t + 1), picks_top)
            dve.wait_ge(picks_top, 2 * NT)
            own.did(dve.tensor_scalar(half_i, pick_i, 4, None, ALU.logical_shift_right))
            own.wait()
            own.did(dve.tensor_copy(half_f[:, 0, :, :, :], half_i))
            own.wait()
            own.did(dve.tensor_scalar(half_i, pick_i, 15, None, ALU.bitwise_and))
            own.wait()
            dve.tensor_copy(half_f[:, 1, :, :, :], half_i).then_inc(places, 1)
            dve.tensor_tensor(pick_g.rearrange("p t (h k) -> p t h k", h=P_HEADS), pick_v,
                              pick_v[:, :, :, 0:1].to_broadcast([P, NT, P_HEADS, TOPK]), ALU.subtract).then_inc(gate_in, 1)
            dve.wait_ge(places, 1)

            def first_keys(t):
                four = [P, P_HEADS, TOPK, TOPK]
                iota16 = iota[:, 0:TOPK].unsqueeze(1).unsqueeze(1).to_broadcast(four)
                if t >= 1:
                    dve.wait_ge(match_used, t)
                dve.tensor_tensor(match1, half_f[:, 1, t, :, :].unsqueeze(3).to_broadcast(four), iota16, ALU.is_equal).then_inc(match_eq, 1)
                own.did(dve.tensor_tensor(match0, half_f[:, 0, t, :, :].unsqueeze(3).to_broadcast(four), iota16, ALU.is_equal))
                own.wait()
                own.did(dve.tensor_tensor(match0, match0, top_f[:, t, 0::2, :].unsqueeze(2).to_broadcast(four), ALU.mult))
                own.wait()
                return dve.tensor_reduce(pick_1[:, t, :].rearrange("p (h k) -> p h k", h=P_HEADS), match0, AX.X, ALU.add)

            def second_keys(t):
                dve.wait_ge(match_p, t + 1)
                return dve.tensor_reduce(pick_2[:, t, :].rearrange("p (h k) -> p h k", h=P_HEADS), match1, AX.X, ALU.add)

            for t in range(NT):
                step = first_keys(t)
                if t < NT - 1:
                    own.did(step)
                    own.wait()
                    second_keys(t).then_inc(match_used, 1)
                else:
                    step.then_inc(picks_ready, 1)
            second_keys(NT - 1).then_inc(picks_ready, 1)
            dve.wait_ge(gate_exp, 1)
            gate_rows = pick_g.rearrange("p t (h k) -> p (t h) k", h=P_HEADS)
            own.did(dve.tensor_reduce(gate_sum, gate_rows, AX.X, ALU.add))
            own.wait()
            own.did(dve.reciprocal(gate_inv, gate_sum))
            own.wait()
            dve.tensor_tensor(gate_rows, gate_rows, gate_inv.unsqueeze(2).to_broadcast([P, NT * P_HEADS, TOPK]), ALU.mult).then_inc(picks_ready, 1)
            own.did(dve.tensor_copy(iota8, iota.unsqueeze(2).to_broadcast([P, P, HB])))
            for i in range(2):
                dve.wait_ge(picks_turned, i + 1)
                dve.tensor_copy(keyT[:, i, :], bank((7, 4)[i])).then_inc(picks_out, 1)
            dve.wait_ge(picks_turned, 3)
            own.did(dve.tensor_copy(gateT[:, 0, :], bank(6)))
            own.wait()
            dve.tensor_tensor(gateT[:, 1, :], bank(6), gateT[:, 0, :], ALU.subtract).then_inc(picks_out, 1)

            dve.wait_ge(picks_out, 3)
            with dve.Fori(0, NT) as i:
                for k in range(P // HB):
                    tokens = bass.ds(i * P + HB * k, HB)
                    dve.wait_ge(gate_mm, i * 16 + (k + 1))
                    dve.tensor_tensor(hot_2[:, k % 4, :, :], iota8, keyT[:, 1, tokens].unsqueeze(1).to_broadcast([P, P, HB]),
                                      ALU.is_equal).then_inc(hot_keys, 1)
                    dve.tensor_tensor(hot_1[:, k % 4, :, :], iota8, keyT[:, 0, tokens].unsqueeze(1).to_broadcast([P, P, HB]),
                                      ALU.is_equal).then_inc(hot_keys, 1)
                    dve.wait_ge(hot_keys, i * 48 + (3 * k + 1))
                    dve.tensor_tensor(hot_lo[:, k % 4, LOW_KEYS:P, :], hot_2[:, k % 4, LOW_KEYS:P, :],
                                      gateT[:, 1, tokens].unsqueeze(1).to_broadcast([P, P - LOW_KEYS, HB]), ALU.mult).then_inc(hot_keys, 1)
                    dve.tensor_tensor(hot_hi[:, k % 4, :, :], hot_2[:, k % 4, :, :],
                                      gateT[:, 0, tokens].unsqueeze(1).to_broadcast([P, P, HB]), ALU.mult).then_inc(hot_hi_done, 1)

            def u_low(g, j):
                for b in range(2):
                    dve.wait_ge(u_hi, 8 * g + (2 * j + b + 1))
                    dve.tensor_tensor(uT_lo[:, j % 2, 4 * b:4 * b + 4, :], bank((0, 6)[j % 2] + b).rearrange("p (k n) -> p k n", k=4),
                                      uT_hi[:, j % 2, 4 * b:4 * b + 4, :], ALU.subtract).then_inc(u_lo, 1)

            def gate_times(activations, par, j):
                dve.tensor_tensor(act_g[:, j % 2, :].rearrange("p (b t) -> p b t", t=TB), activations.rearrange("p (b t) -> p b t", t=TB),
                                  gates[:, par, :, j, :], ALU.mult).then_inc(ex_mul, 1)

            def expert_hidden(g, par, gate_loads):
                dve.wait_ge(gates_in[par], gate_loads)
                group_summed(dve, g)
                for j in range(4):
                    if j < 3:
                        u_low(g, j + 1)
                    dve.wait_ge(ex_gelu, 4 * g + (j + 1))
                    gate_times(gelu[:, j % 2, :], par, j)
                    dve.wait_ge(ex_mul, 4 * g + (j + 1))
                    dve.wait_ge(ex_hi_done, 4 * g + (j + 1))
                    dve.tensor_tensor(ex_lo[:, par, j, :], act_g[:, j % 2, :], ex_hi[:, par, j, :], ALU.subtract).then_inc(ex_lo_done, 1)

            def expert_add(g, banks=range(8)):
                for b in banks:
                    t, c = divmod(b, 2)
                    dve.wait_ge(ex_b, 8 * g + (b + 2))
                    dst = x_sb[:, t, c * 512:(c + 1) * 512]
                    dve.tensor_tensor(dst, bank(4 + b % 2), dst, ALU.add).then_inc(ex_add, 1)

            dve.sem_inc(ex_add, 2)
            def early_hidden(g):
                dve.wait_ge(gates_in[g % 2], 16 * (g // 2 + 1))
                dve.wait_ge(gelu_in[g % 2], 16 * (g // 2 + 1))
                group_summed(dve, g)
                for j in range(4):
                    if 4 * g + j >= 2:
                        dve.wait_ge(ex_hi_done, 4 * g + j - 1)
                    gate_times(gelu_back[:, g % 2, j, :], g % 2, j)
                    dve.wait_ge(ex_mul, 4 * g + (j + 1))
                    dve.wait_ge(ex_hi_done, 4 * g + (j + 1))
                    dve.tensor_tensor(ex_lo[:, g % 2, j, :], act_g[:, j % 2, :], ex_hi[:, g % 2, j, :], ALU.subtract).then_inc(ex_lo_done, 1)
                    if g >= 1 and j in (1, 3):
                        expert_add(g - 1, [j // 2])

            for j in range(4):
                u_low(5, j)
            early_hidden(0)
            for g in range(1, EARLY):
                if g == EARLY - 1:
                    u_low(6, 0)
                early_hidden(g)
                expert_add(g - 1, range(2, 8))
            with dve.Fori(0, 12) as i:
                expert_hidden(2 * i + 6, 0, i * 16 + 64)
                u_low(2 * i + 7, 0)
                expert_add(2 * i + 5)
                expert_hidden(2 * i + 7, 1, i * 16 + 64)
                u_low(2 * i + 8, 0)
                expert_add(2 * i + 6)
            expert_hidden(30, 0, 16 * 16)
            u_low(31, 0)
            expert_add(29)
            expert_hidden(31, 1, 16 * 16)
            expert_add(30)
            expert_add(31)

            dve.wait_ge(rstd_done, 9)
            dve.wait_ge(out_gain_in, 16)
            for t in range(NT):
                dve.scalar_tensor_tensor(out_rows[:, t, :], x_sb[:, t, :], rstd[:, t:t + 1], out_gain, ALU.mult, ALU.mult).then_inc(out_ready, 1)


_INS = ["x", "positions", "g_mix_norm", "w_in", "conv_w", "conv_b", "b_gates", "g_mlstm_out", "g_cq", "g_ckv",
        "w_uq", "w_ukv", "g_q", "g_k", "w_out", "g_ffn_norm", "w_ff1", "w_ff2", "norm_mix_g_2", "w_in_2",
        "diff_lambda_2", "diff_subln_g_2", "w_out_2", "norm_ffn_g_2", "peer_wq_2", "peer_subkeys_2", "peer_u_2",
        "peer_v_2", "final_norm_g_2"]


def kernel(**inputs):
    import concourse.bacc as bacc
    from concourse.bass_utils import run_bass_kernel_spmd

    nc = bacc.Bacc("TRN2", target_bir_lowering=False, num_devices=1)
    arrays = {f"in_{name}": np.ascontiguousarray(inputs[name]) for name in _INS}
    arrays["in_table"] = TABLE
    ins = {name[3:]: nc.dram_tensor(name, a.shape, mybir.dt.from_np(a.dtype), kind="ExternalInput").ap()
           for name, a in arrays.items()}
    out = nc.dram_tensor("out", (1, T, D), F32, kind="ExternalOutput").ap()
    build(nc, ins, out)
    r = run_bass_kernel_spmd(nc, [arrays], core_ids=[0])
    return r.results[0]["out"]
```
